# Optimizing a Trainium2 kernel written in Bass

```python
import jax, jax.numpy as jnp
from jax import lax
import numpy as np
import math

D_MODEL = 1024
BATCH = 1
SEQ = 256
DEPTH = 2

HEAD_DIM = 64
DIL_PAIRS = ((128, 1), (512, 4), (2048, 16))
N_DIL_GROUPS = len(DIL_PAIRS)
DIL_HEADS_PER_GROUP = 4
DIL_HEADS = N_DIL_GROUPS * DIL_HEADS_PER_GROUP
SB_HEADS = 4
DIL_WIDTH = DIL_HEADS * HEAD_DIM
SB_WIDTH = SB_HEADS * HEAD_DIM
DIL_OUT_WIDTH = DIL_HEADS_PER_GROUP * HEAD_DIM
N_BRANCHES = 2
IN_COLS = 3 * DIL_WIDTH + 3 * SB_WIDTH + N_BRANCHES * D_MODEL
D_FF = 2816
CONV_WIDTH = 3
ROPE_THETA = 500000.0
ROPE_DIM = HEAD_DIM // 4
Q_BLOCK = 128
NORM_EPS = 1e-5
MAX_POS_OFFSET = 4096
MASK_VALUE = -1e30


def rms_norm(x, gain):
    xf = x.astype(jnp.float32)
    xf = xf * lax.rsqrt(jnp.mean(xf * xf, axis=-1, keepdims=True) + NORM_EPS)
    return (xf * gain.astype(jnp.float32)).astype(x.dtype)

def rope_tables(positions, dtype):
    inv_freq = ROPE_THETA ** (-jnp.arange(0, ROPE_DIM, 2, dtype=jnp.float32) / ROPE_DIM)
    ang = positions.astype(jnp.float32)[..., None] * inv_freq
    return (jnp.cos(ang)[:, :, None, None, :].astype(dtype),
            jnp.sin(ang)[:, :, None, None, :].astype(dtype))

def apply_partial_rope(x, cos, sin):
    half = ROPE_DIM // 2
    x1, x2, rest = x[..., :half], x[..., half:ROPE_DIM], x[..., ROPE_DIM:]
    return jnp.concatenate([x1 * cos - x2 * sin, x2 * cos + x1 * sin, rest], axis=-1)

def dilated_attention(q, k, v):
    b, s = q.shape[0], q.shape[1]
    n_blocks = s // Q_BLOCK
    scale = HEAD_DIM ** -0.5
    qs = [q[:, :, g] for g in range(N_DIL_GROUPS)]
    ks = [k[:, :, g] for g in range(N_DIL_GROUPS)]
    vs = [v[:, :, g] for g in range(N_DIL_GROUPS)]

    def block(t0):
        t = t0 + jnp.arange(Q_BLOCK)
        outs, lses = [], []
        for g, (window, dil) in enumerate(DIL_PAIRS):
            n_keys = window // dil + 1
            idx = t[:, None] - dil * jnp.arange(n_keys)[None, :]
            valid = idx >= 0
            idx = jnp.maximum(idx, 0)
            qg = lax.dynamic_slice_in_dim(qs[g], t0, Q_BLOCK, axis=1)
            kg = ks[g][:, idx]
            vg = vs[g][:, idx]
            sc = jnp.einsum('bqhd,bqkhd->bhqk', qg, kg).astype(jnp.float32) * scale
            sc = jnp.where(valid[None, None], sc, MASK_VALUE)
            m = jnp.max(sc, axis=-1, keepdims=True)
            p = jnp.exp(sc - m)
            den = jnp.sum(p, axis=-1)
            o = jnp.einsum('bhqk,bqkhd->bqhd', p, vg.astype(jnp.float32))
            o = o / jnp.transpose(den, (0, 2, 1))[..., None]
            outs.append(o)
            lses.append(m[..., 0] + jnp.log(den))
        o_all = jnp.stack(outs, axis=0)
        w = jax.nn.softmax(jnp.stack(lses, axis=0), axis=0)
        w = jnp.transpose(w, (0, 1, 3, 2))[..., None]
        return jnp.sum(w * o_all, axis=0).astype(q.dtype)

    out = lax.map(block, jnp.arange(n_blocks) * Q_BLOCK)
    return jnp.moveaxis(out, 0, 1).reshape(b, s, DIL_OUT_WIDTH)

def stick_breaking_attention(q, k, v):
    b, s = q.shape[0], q.shape[1]
    n_blocks = s // Q_BLOCK
    scale = HEAD_DIM ** -0.5
    key_pos = jnp.arange(s)

    def block(t0):
        qb = lax.dynamic_slice_in_dim(q, t0, Q_BLOCK, axis=1)
        z = jnp.einsum('bqhd,bkhd->bhqk', qb, k).astype(jnp.float32) * scale
        t = t0 + jnp.arange(Q_BLOCK)
        causal = key_pos[None, :] < t[:, None]
        log_keep = jnp.where(causal, jax.nn.log_sigmoid(-z), 0.0)
        suffix = lax.cumsum(log_keep, axis=3, reverse=True) - log_keep
        attn = jnp.where(causal, jnp.exp(jax.nn.log_sigmoid(z) + suffix), 0.0)
        return jnp.einsum('bhqk,bkhd->bqhd', attn, v.astype(jnp.float32)).astype(q.dtype)

    out = lax.map(block, jnp.arange(n_blocks) * Q_BLOCK)
    return jnp.moveaxis(out, 0, 1).reshape(b, s, SB_WIDTH)

def conv_ffn(h, w_up, conv_w, conv_b, w_down):
    up = h @ w_up
    a, bval = up[..., :D_FF], up[..., D_FF:]
    a = lax.conv_general_dilated(a, conv_w[:, None, :].astype(a.dtype), window_strides=(1,),
                                 padding=((CONV_WIDTH - 1, 0),),
                                 dimension_numbers=('NWC', 'WIO', 'NWC'),
                                 feature_group_count=D_FF) + conv_b
    return (jax.nn.silu(a) * bval) @ w_down

def first_inputs(seed: int = 0) -> dict:
    key = jax.random.key(seed)
    ks = jax.random.split(key, 16)
    f32 = jnp.float32
    nrm = lambda k, shape, s: jax.random.normal(k, shape, f32) * s
    x = jax.random.normal(ks[0], (BATCH, SEQ, D_MODEL), f32)
    offset = jax.random.randint(ks[1], (BATCH, 1), 0, MAX_POS_OFFSET, dtype=jnp.int32)
    positions = offset + jnp.arange(SEQ, dtype=jnp.int32)[None, :]
    return {
        "x": x,
        "positions": positions,
        "norm_mix": 1.0 + nrm(ks[2], (DEPTH, D_MODEL), 0.05),
        "w_in": nrm(ks[3], (DEPTH, D_MODEL, IN_COLS), D_MODEL ** -0.5),
        "b_gate": nrm(ks[4], (DEPTH, N_BRANCHES * D_MODEL), 0.1),
        "w_proj_a": nrm(ks[5], (DEPTH, DIL_OUT_WIDTH, D_MODEL), DIL_OUT_WIDTH ** -0.5),
        "w_proj_b": nrm(ks[6], (DEPTH, SB_WIDTH, D_MODEL), SB_WIDTH ** -0.5),
        "w_out": nrm(ks[7], (DEPTH, D_MODEL, D_MODEL), D_MODEL ** -0.5),
        "norm_ffn": 1.0 + nrm(ks[8], (DEPTH, D_MODEL), 0.05),
        "w_up": nrm(ks[9], (DEPTH, D_MODEL, 2 * D_FF), D_MODEL ** -0.5),
        "conv_w": nrm(ks[10], (DEPTH, CONV_WIDTH, D_FF), CONV_WIDTH ** -0.5),
        "conv_b": nrm(ks[11], (DEPTH, D_FF), 0.02),
        "w_down": nrm(ks[12], (DEPTH, D_FF, D_MODEL), D_FF ** -0.5),
        "norm_final": 1.0 + nrm(ks[13], (D_MODEL,), 0.05),
    }

def first_block(x, positions, norm_mix, w_in, b_gate, w_proj_a, w_proj_b, w_out,
              norm_ffn, w_up, conv_w, conv_b, w_down, norm_final):
    b, s, _ = x.shape
    cos, sin = rope_tables(positions, x.dtype)
    splits = np.cumsum([DIL_WIDTH, DIL_WIDTH, DIL_WIDTH, SB_WIDTH, SB_WIDTH, SB_WIDTH]).tolist()
    for l in range(DEPTH):
        h = rms_norm(x, norm_mix[l])
        proj = h @ w_in[l]
        dq, dk, dv, sq, sk, sv, gate_logits = jnp.split(proj, splits, axis=-1)
        dshape = (b, s, N_DIL_GROUPS, DIL_HEADS_PER_GROUP, HEAD_DIM)
        dq = apply_partial_rope(dq.reshape(dshape), cos, sin)
        dk = apply_partial_rope(dk.reshape(dshape), cos, sin)
        dv = dv.reshape(dshape)
        sshape = (b, s, SB_HEADS, HEAD_DIM)
        y_a = dilated_attention(dq, dk, dv) @ w_proj_a[l]
        y_b = stick_breaking_attention(sq.reshape(sshape), sk.reshape(sshape), sv.reshape(sshape)) @ w_proj_b[l]
        gates = jax.nn.sigmoid(gate_logits + b_gate[l])
        mixed = gates[..., :D_MODEL] * y_a + gates[..., D_MODEL:] * y_b
        x = x + mixed @ w_out[l]
        h = rms_norm(x, norm_ffn[l])
        x = x + conv_ffn(h, w_up[l], conv_w[l], conv_b[l], w_down[l])
    return rms_norm(x, norm_final)


DEPTH_2 = 1

D_MIX = D_MODEL
GDN_WIDTH = D_MIX // 2
GDN_HEAD_DIM = 128
GDN_HEADS = GDN_WIDTH // GDN_HEAD_DIM
GDN_CHUNK = 64
LRU_WIDTH = D_MIX - GDN_WIDTH
LRU_BLOCKS = 8
LRU_BLOCK_DIM = LRU_WIDTH // LRU_BLOCKS
LRU_C = 8.0
CONV_WIDTH_2 = 4
D_FF_2 = 4 * D_MODEL
EPS = 1e-6
SPLIT_SIZES = (3 * GDN_WIDTH, GDN_WIDTH, GDN_HEADS, GDN_HEADS, LRU_WIDTH, LRU_WIDTH)
IN_COLS_2 = sum(SPLIT_SIZES)
SPLIT_IDX = tuple(int(i) for i in np.cumsum(SPLIT_SIZES)[:-1])


def rmsnorm(x, w):
    xf = x.astype(jnp.float32)
    y = xf * lax.rsqrt(jnp.mean(xf * xf, axis=-1, keepdims=True) + EPS)
    return (y * w.astype(jnp.float32)).astype(x.dtype)

def l2norm(x):
    xf = x.astype(jnp.float32)
    return xf * lax.rsqrt(jnp.sum(xf * xf, axis=-1, keepdims=True) + EPS)

def causal_depthwise_conv(x, w):
    c = x.shape[-1]
    return lax.conv_general_dilated(
        x, w[:, None, :].astype(x.dtype), window_strides=(1,),
        padding=[(CONV_WIDTH_2 - 1, 0)], dimension_numbers=("NWC", "WIO", "NWC"),
        feature_group_count=c)

def gated_delta_rule_chunked(q, k, v, g, beta):
    f32 = jnp.float32
    b, s, h, dk = q.shape
    dv = v.shape[-1]
    c = GDN_CHUNK
    n = s // c

    def to_chunks(t):
        t = jnp.moveaxis(t.astype(f32), 2, 1)
        return t.reshape(b, h, n, c, *t.shape[3:])

    q = to_chunks(q) * (dk ** -0.5)
    k = to_chunks(k)
    v = to_chunks(v)
    g_cum = jnp.cumsum(to_chunks(g), axis=-1)
    beta = to_chunks(beta)

    causal = jnp.tril(jnp.ones((c, c), dtype=bool))
    strict = jnp.tril(jnp.ones((c, c), dtype=bool), -1)
    diff = g_cum[..., :, None] - g_cum[..., None, :]
    decay = jnp.where(causal, jnp.exp(jnp.where(causal, diff, 0.0)), 0.0)

    k_beta = k * beta[..., None]
    v_beta = v * beta[..., None]
    a_low = jnp.where(strict, jnp.einsum("bhnid,bhnjd->bhnij", k_beta, k) * decay, 0.0)
    i_plus_a = a_low + jnp.eye(c, dtype=f32)
    rhs = jnp.concatenate([v_beta, k_beta * jnp.exp(g_cum)[..., None]], axis=-1)
    sol = lax.linalg.triangular_solve(i_plus_a, rhs, left_side=True, lower=True)
    u = sol[..., :dv]
    w = sol[..., dv:]
    qk_intra = jnp.where(causal, jnp.einsum("bhnid,bhnjd->bhnij", q, k) * decay, 0.0)

    def step(state, inp):
        q_c, k_c, u_c, w_c, attn_c, g_c = inp
        v_new = u_c - jnp.einsum("bhck,bhkv->bhcv", w_c, state)
        o_c = (jnp.einsum("bhck,bhkv->bhcv", q_c * jnp.exp(g_c)[..., None], state)
               + jnp.einsum("bhij,bhjv->bhiv", attn_c, v_new))
        g_last = g_c[..., -1]
        k_dec = k_c * jnp.exp(g_last[..., None] - g_c)[..., None]
        state = state * jnp.exp(g_last)[..., None, None] + jnp.einsum("bhck,bhcv->bhkv", k_dec, v_new)
        return state, o_c

    xs = tuple(jnp.moveaxis(t, 2, 0) for t in (q, k, u, w, qk_intra, g_cum))
    state0 = jnp.zeros((b, h, dk, dv), f32)
    _, o = lax.scan(step, state0, xs)
    o = jnp.moveaxis(o, 0, 2).reshape(b, h, s, dv)
    return jnp.moveaxis(o, 1, 2)

def rg_lru(x, wa, ba, wx, bx, a_param):
    f32 = jnp.float32
    b, s, d = x.shape
    xf = x.astype(f32)
    xb = xf.reshape(b, s, LRU_BLOCKS, LRU_BLOCK_DIM)
    r = jax.nn.sigmoid(jnp.einsum("bsgi,gij->bsgj", xb, wa.astype(f32)) + ba.astype(f32)).reshape(b, s, d)
    i = jax.nn.sigmoid(jnp.einsum("bsgi,gij->bsgj", xb, wx.astype(f32)) + bx.astype(f32)).reshape(b, s, d)
    log_a = -LRU_C * r * jax.nn.softplus(-a_param.astype(f32))
    a = jnp.exp(log_a)
    gated_x = jnp.sqrt(-jnp.expm1(2.0 * log_a)) * (i * xf)

    def combine(c1, c2):
        a1, b1 = c1
        a2, b2 = c2
        return a1 * a2, a2 * b1 + b2

    _, h = lax.associative_scan(combine, (a, gated_x), axis=1)
    return h

def hybrid_layer(x, norm_mix_w, w_in, gdn_conv_w, gdn_A_log, gdn_dt_bias, gdn_norm_w,
                 lru_conv_w, lru_conv_b, lru_gate_a_w, lru_gate_a_b, lru_gate_x_w, lru_gate_x_b,
                 lru_a_param, w_out, norm_mlp_w, w_ff1, w_ff2):
    b, s, _ = x.shape
    dt = x.dtype
    h = rmsnorm(x, norm_mix_w)
    proj = jnp.einsum("bsd,de->bse", h, w_in.astype(dt))
    qkv, z, b_logit, a_logit, lru_x, lru_gate = jnp.split(proj, SPLIT_IDX, axis=-1)

    qkv = jax.nn.silu(causal_depthwise_conv(qkv, gdn_conv_w))
    q, k, v = jnp.split(qkv, 3, axis=-1)
    q = l2norm(q.reshape(b, s, GDN_HEADS, GDN_HEAD_DIM))
    k = l2norm(k.reshape(b, s, GDN_HEADS, GDN_HEAD_DIM))
    v = v.reshape(b, s, GDN_HEADS, GDN_HEAD_DIM)
    beta = jax.nn.sigmoid(b_logit.astype(jnp.float32))
    g = -jnp.exp(gdn_A_log.astype(jnp.float32)) * jax.nn.softplus(
        a_logit.astype(jnp.float32) + gdn_dt_bias.astype(jnp.float32))
    o = gated_delta_rule_chunked(q, k, v, g, beta)
    z = z.reshape(b, s, GDN_HEADS, GDN_HEAD_DIM).astype(jnp.float32)
    o = rmsnorm(o, gdn_norm_w) * jax.nn.silu(z)
    gdn_out = o.reshape(b, s, GDN_WIDTH).astype(dt)

    xr = causal_depthwise_conv(lru_x, lru_conv_w) + lru_conv_b.astype(dt)
    hr = rg_lru(xr, lru_gate_a_w, lru_gate_a_b, lru_gate_x_w, lru_gate_x_b, lru_a_param)
    lru_out = (hr * jax.nn.gelu(lru_gate.astype(jnp.float32))).astype(dt)

    mix = jnp.concatenate([gdn_out, lru_out], axis=-1)
    x = x + jnp.einsum("bse,ed->bsd", mix, w_out.astype(dt))

    m = rmsnorm(x, norm_mlp_w)
    u = jax.nn.relu(jnp.einsum("bsd,df->bsf", m, w_ff1.astype(dt)))
    x = x + jnp.einsum("bsf,fd->bsd", u * u, w_ff2.astype(dt))
    return x

def second_inputs(seed: int = 0) -> dict:
    key = jax.random.key(seed)
    ks = jax.random.split(key, 24)
    f32 = jnp.float32
    nrm = lambda k, shape, scale: (jax.random.normal(k, shape, f32) * scale)
    x = jax.random.normal(ks[0], (BATCH, SEQ, D_MODEL), f32)
    norm_mix_w = 1.0 + nrm(ks[1], (DEPTH_2, D_MODEL), 0.02)
    w_in = nrm(ks[2], (DEPTH_2, D_MODEL, IN_COLS_2), D_MODEL ** -0.5)
    gdn_conv_w = nrm(ks[3], (DEPTH_2, CONV_WIDTH_2, 3 * GDN_WIDTH), CONV_WIDTH_2 ** -0.5)
    gdn_A_log = jnp.log(jax.random.uniform(ks[4], (DEPTH_2, GDN_HEADS), f32, 1.0, 16.0))
    dt0 = jnp.exp(jax.random.uniform(ks[5], (DEPTH_2, GDN_HEADS), f32, math.log(1e-3), math.log(1e-1)))
    gdn_dt_bias = dt0 + jnp.log(-jnp.expm1(-dt0))
    gdn_norm_w = 1.0 + nrm(ks[6], (DEPTH_2, GDN_HEAD_DIM), 0.02)
    lru_conv_w = nrm(ks[7], (DEPTH_2, CONV_WIDTH_2, LRU_WIDTH), CONV_WIDTH_2 ** -0.5)
    lru_conv_b = nrm(ks[8], (DEPTH_2, LRU_WIDTH), 0.01)
    lru_gate_a_w = nrm(ks[9], (DEPTH_2, LRU_BLOCKS, LRU_BLOCK_DIM, LRU_BLOCK_DIM), LRU_BLOCK_DIM ** -0.5)
    lru_gate_a_b = nrm(ks[10], (DEPTH_2, LRU_BLOCKS, LRU_BLOCK_DIM), 0.01)
    lru_gate_x_w = nrm(ks[11], (DEPTH_2, LRU_BLOCKS, LRU_BLOCK_DIM, LRU_BLOCK_DIM), LRU_BLOCK_DIM ** -0.5)
    lru_gate_x_b = nrm(ks[12], (DEPTH_2, LRU_BLOCKS, LRU_BLOCK_DIM), 0.01)
    a_c = jax.random.uniform(ks[13], (DEPTH_2, LRU_WIDTH), f32, 0.9, 0.999)
    sig_l = a_c ** (1.0 / LRU_C)
    lru_a_param = jnp.log(sig_l) - jnp.log1p(-sig_l)
    w_out = nrm(ks[14], (DEPTH_2, D_MIX, D_MODEL), D_MIX ** -0.5)
    norm_mlp_w = 1.0 + nrm(ks[15], (DEPTH_2, D_MODEL), 0.02)
    w_ff1 = nrm(ks[16], (DEPTH_2, D_MODEL, D_FF_2), D_MODEL ** -0.5)
    w_ff2 = nrm(ks[17], (DEPTH_2, D_FF_2, D_MODEL), D_FF_2 ** -0.5)
    final_norm_w = 1.0 + nrm(ks[18], (D_MODEL,), 0.02)
    return {"x": x, "norm_mix_w": norm_mix_w, "w_in": w_in, "gdn_conv_w": gdn_conv_w,
            "gdn_A_log": gdn_A_log, "gdn_dt_bias": gdn_dt_bias, "gdn_norm_w": gdn_norm_w,
            "lru_conv_w": lru_conv_w, "lru_conv_b": lru_conv_b,
            "lru_gate_a_w": lru_gate_a_w, "lru_gate_a_b": lru_gate_a_b,
            "lru_gate_x_w": lru_gate_x_w, "lru_gate_x_b": lru_gate_x_b,
            "lru_a_param": lru_a_param, "w_out": w_out, "norm_mlp_w": norm_mlp_w,
            "w_ff1": w_ff1, "w_ff2": w_ff2, "final_norm_w": final_norm_w}

def second_block(x, norm_mix_w, w_in, gdn_conv_w, gdn_A_log, gdn_dt_bias, gdn_norm_w,
              lru_conv_w, lru_conv_b, lru_gate_a_w, lru_gate_a_b, lru_gate_x_w, lru_gate_x_b,
              lru_a_param, w_out, norm_mlp_w, w_ff1, w_ff2, final_norm_w):
    for layer in range(DEPTH_2):
        x = hybrid_layer(x, norm_mix_w[layer], w_in[layer], gdn_conv_w[layer], gdn_A_log[layer],
                         gdn_dt_bias[layer], gdn_norm_w[layer], lru_conv_w[layer], lru_conv_b[layer],
                         lru_gate_a_w[layer], lru_gate_a_b[layer], lru_gate_x_w[layer],
                         lru_gate_x_b[layer], lru_a_param[layer], w_out[layer], norm_mlp_w[layer],
                         w_ff1[layer], w_ff2[layer])
    return rmsnorm(x, final_norm_w)


def setup_inputs(seed=0):
    out = dict(first_inputs(seed))
    for name, value in second_inputs(seed + 1).items():
        if name != "x":
            out[name + "_2"] = value
    return out


def reference(
    x, positions, norm_mix, w_in, b_gate, w_proj_a, w_proj_b, w_out, norm_ffn, w_up, conv_w,
    conv_b, w_down, norm_final, norm_mix_w_2, w_in_2, gdn_conv_w_2, gdn_A_log_2, gdn_dt_bias_2,
    gdn_norm_w_2, lru_conv_w_2, lru_conv_b_2, lru_gate_a_w_2, lru_gate_a_b_2, lru_gate_x_w_2,
    lru_gate_x_b_2, lru_a_param_2, w_out_2, norm_mlp_w_2, w_ff1_2, w_ff2_2, final_norm_w_2,
):
    x = first_block(
        x, positions, norm_mix, w_in, b_gate, w_proj_a, w_proj_b, w_out, norm_ffn, w_up, conv_w,
        conv_b, w_down, norm_final,
    )
    return second_block(
        x, norm_mix_w_2, w_in_2, gdn_conv_w_2, gdn_A_log_2, gdn_dt_bias_2, gdn_norm_w_2,
        lru_conv_w_2, lru_conv_b_2, lru_gate_a_w_2, lru_gate_a_b_2, lru_gate_x_w_2,
        lru_gate_x_b_2, lru_a_param_2, w_out_2, norm_mlp_w_2, w_ff1_2, w_ff2_2, final_norm_w_2,
    )


_drawn_inputs = setup_inputs


def setup_inputs(seed=0):
    import zlib

    import numpy as np

    out = dict(_drawn_inputs(seed))
    spreads = {}
    factors = {'conv_b': 3.338,
     'norm_mix_w_2': 3.584,
     'gdn_norm_w_2': 18.183,
     'lru_conv_b_2': 10.263,
     'lru_gate_a_b_2': 200.0,
     'lru_gate_x_b_2': 64.0,
     'norm_mlp_w_2': 11.406,
     'final_norm_w_2': 21.888}
    for name, (base, spread) in spreads.items():
        noise = np.random.default_rng([zlib.crc32(name.encode()), seed]).standard_normal(out[name].shape)
        drawn = base * np.exp(spread * noise) if base else spread * noise
        out[name] = __import__('jax').numpy.asarray(drawn.astype(out[name].dtype))
    for name, factor in factors.items():
        out[name] = (out[name] * factor).astype(out[name].dtype)
    return out
```

```python
from contextlib import ExitStack

import numpy as np

import concourse.bass as bass
from concourse import mybir

F32 = mybir.dt.float32
F32R = mybir.dt.float32r
I32 = mybir.dt.int32
ACT = mybir.ActivationFunctionType
ALU = mybir.AluOpType

P = 128
T = 256
NB = T // P
D = 1024
KD = D // P
DEPTH = 2
HEAD = 64
HEADS = 4
GROUPS = 3
DILATIONS = (1, 4, 16)
WINDOWS = (128, 512, 2048)
DIL_W = GROUPS * HEADS * HEAD
SB_W = HEADS * HEAD
ROPE_THETA = 500000.0
ROPE = HEAD // 4
FF = 2816
FF_TILES = FF // P
PARTS1 = ((0, 12), (12, 10))
PARTS2 = ((0, 12), (12, 10), (22, 10))
EPS1 = 1e-5
EPS2 = 1e-6
GH = 4
LT = 4
LRU_C = 8.0
GELU_C = float(np.sqrt(2.0 / np.pi))
LEVELS = 7
FF2_TILES = 4 * D // P
HID = 12
TICK0 = 8
SCRATCH = 14976
X_TOTAL = KD * (1 + 3 * DEPTH + 1 + len(PARTS2))
PER_LAYER = 4 + KD + FF_TILES
MIX_BASE = [PER_LAYER * l + 4 for l in range(DEPTH)]
LO_BEFORE_MLP = PER_LAYER * DEPTH + KD
ROUND = 1.5 * 2 ** 23


def short(x, bits):
    m, e = np.frexp(x)
    return float(np.ldexp(np.round(m * 2 ** bits), int(e) - bits))


_A = short(2 * np.pi, 10)
_B = short(2 * np.pi - _A, 10)
TWO_PI = (_A, _B, float(2 * np.pi - _A - _B))
PI_BELOW = float(np.nextafter(np.float32(np.pi), np.float32(0)))
SLOTS = 3
SLAB = 2048
RING = 3
BANK_SC, BANK_T, BANK_O = 3, 5, 7
FAR = -1e30

CONST_COLS = {}


def constants():
    p = np.arange(P)[:, None]
    c = np.arange(P)[None, :]
    parts = {}
    parts["ident"] = (p == c)
    parts["ones"] = np.ones((P, P))
    parts["neg_ge"] = -1.0 * (p >= c)
    parts["neg_ones"] = -np.ones((P, P))
    parts["le"] = (p <= c)
    parts["lt"] = (p < c)
    rot = np.zeros((P, P))
    inv = np.zeros((P, 1))
    freq = ROPE_THETA ** (-np.arange(0, ROPE, 2) / ROPE)
    for base in (0, HEAD):
        for i in range(ROPE // 2):
            rot[base + ROPE // 2 + i, base + i] = -1.0
            rot[base + i, base + ROPE // 2 + i] = 1.0
            inv[base + i] = inv[base + ROPE // 2 + i] = freq[i]
    parts["rot"] = rot
    parts["inv_freq"] = inv
    for qb in range(NB):
        keys = (qb + 1) * P
        q = qb * P + p
        k = np.arange(keys)[None, :]
        cols = [np.where((q >= k) & (q - k <= w) & ((q - k) % d == 0), 0.0, FAR) for w, d in zip(WINDOWS, DILATIONS)]
        parts[f"dil_mask{qb}"] = np.concatenate(cols, axis=1)
    strict = np.where(p < c, 0.0, FAR)
    parts["sb_mask"] = np.concatenate([strict, np.zeros((P, P)), strict], axis=1)
    for lv in range(LEVELS):
        b = 1 << lv
        below = (p // (2 * b) == c // (2 * b)) & (p // b % 2 == 1) & (c // b % 2 == 0)
        parts[f"neg_level{lv}"] = -1.0 * (below.T if lv == 0 else below)
    pick = np.zeros((P, 15))
    pick[:, 7] = 1.0
    parts["pick"] = pick
    at = 0
    for name, a in parts.items():
        CONST_COLS[name] = (at, a.shape[1])
        at += a.shape[1]
    return np.concatenate([a.astype(np.float32) for a in parts.values()], axis=1)


CONSTS = constants()

PARAM_COLS = {}


def params(a):
    cols = []
    at = 0

    def put(name, rows):
        nonlocal at
        cols.append(rows)
        PARAM_COLS[name] = at
        at += rows.shape[1]

    def tiles(v):
        return np.reshape(v, (-1, P)).T

    for l in range(DEPTH):
        put(f"norm_mix{l}", tiles(a["norm_mix"][l]))
        put(f"b_gate{l}", tiles(a["b_gate"][l]))
        put(f"norm_ffn{l}", tiles(a["norm_ffn"][l]))
        put(f"conv_w{l}", tiles(a["conv_w"][l]))
        put(f"conv_b{l}", tiles(a["conv_b"][l]))
    put("norm_final", tiles(a["norm_final"]))
    put("norm_mix2", tiles(a["norm_mix_w_2"][0]))
    put("gdn_conv", tiles(a["gdn_conv_w_2"][0]))
    put("gdn_norm", tiles(a["gdn_norm_w_2"][0]))
    put("lru_conv", tiles(a["lru_conv_w_2"][0]))
    put("lru_conv_b", tiles(a["lru_conv_b_2"][0]))
    put("gate_a_b", tiles(a["lru_gate_a_b_2"][0]))
    put("gate_x_b", tiles(a["lru_gate_x_b_2"][0]))
    put("a_param", tiles(a["lru_a_param_2"][0]))
    put("norm_mlp", tiles(a["norm_mlp_w_2"][0]))
    put("A_log", np.broadcast_to(np.reshape(a["gdn_A_log_2"][0], (1, GH)), (P, GH)))
    put("dt_bias", np.broadcast_to(np.reshape(a["gdn_dt_bias_2"][0], (1, GH)), (P, GH)))
    PARAM_COLS["cols"] = at
    return np.concatenate(cols, axis=1)


def lru_blocks(a):
    out = np.zeros((P, 2, LT, P), np.float32)
    for n, name in enumerate(("lru_gate_a_w_2", "lru_gate_x_w_2")):
        for t in range(LT):
            out[:HEAD, n, t, :HEAD] = a[name][0, 2 * t]
            out[HEAD:, n, t, HEAD:] = a[name][0, 2 * t + 1]
    return np.reshape(out, (P, -1))


class Slab:
    def __init__(self, n, stage, src, chunks, cols, index):
        self.n, self.stage, self.src, self.chunks, self.cols, self.index = n, stage, src, chunks, cols, index
        self.tiles = []
        self.freed = None


class Plan:

    def __init__(self, w):
        self.slabs = []
        self.stages = {}
        self.readers = []
        self.counts = {}
        self.firsts = 0
        for l in range(DEPTH):
            win = w["w_in"][l]
            order = [("s", 3 * DIL_W), ("s", 3 * DIL_W + SB_W), ("v", 3 * DIL_W + 2 * SB_W)]
            order += [("rope", 256 * i) for i in range(6)]
            order += [("v", 2 * DIL_W + 256 * i) for i in range(3)]
            order += [("gate", 3 * DIL_W + 3 * SB_W + 256 * i) for i in range(8)]
            for kind, c in order:
                self.add((l, "in"), win[:, c:c + 256], kind)
            self.add((l, "proj"), w["w_proj_a"][l], None)
            self.add((l, "proj"), w["w_proj_b"][l], None)
            for m in range(KD):
                self.tile(self.slabs[-2], "pa")
                self.tile(self.slabs[-1], "pb")
            for c in range(4):
                self.add((l, "out"), w["w_out"][l][:, 256 * c:256 * c + 256], "x")
            for half, (f0, n) in enumerate(PARTS1):
                for j in range(n // 2):
                    c = (f0 + 2 * j) * P
                    self.add((l, "up", half), w["w_up"][l][:, c:c + 256], "fa")
                    self.add((l, "up", half), w["w_up"][l][:, FF + c:FF + c + 256], "fb")
                self.down((l, "down", half), w["w_down"][l], f0, n)
        win = w["w_in_2"][0]
        gw = 512
        order = [("conv", 256 * i) for i in range(6)] + [("ba", 4 * gw)]
        order += [("conv", 4 * gw + 8 + 256 * i) for i in range(2)]
        order += [("lg", 5 * gw + 8 + 256 * i) for i in range(2)]
        order += [("z", 3 * gw + 256 * i) for i in range(2)]
        for kind, c in order:
            self.add((2, "in"), win[:, c:c + (8 if kind == "ba" else 256)], kind)
        for c in range(4):
            self.add((2, "out"), w["w_out_2"][0][:, 256 * c:256 * c + 256], "x")
        for half, (f0, n) in enumerate(PARTS2):
            for j in range(n // 2):
                c = (f0 + 2 * j) * P
                self.add((2, "up", half), w["w_ff1_2"][0][:, c:c + 256], "f2")
            self.down((2, "down", half), w["w_ff2_2"][0], f0, n)
        for s in self.slabs:
            if s.tiles:
                s.freed = ("main_tile", s.tiles[-1] + 1)

    def add(self, stage, src, kind):
        rows, cols = src.shape
        index = len(self.stages.setdefault(stage, []))
        s = Slab(len(self.slabs), stage, src, rows // P, cols, index)
        s.kind = kind
        self.slabs.append(s)
        self.stages[stage].append(s)
        if kind:
            for _ in range(2):
                self.tile(s, kind)

    def down(self, stage, src, f0, n):
        for c in range(4):
            for piece in range(2):
                r = (f0 + piece * n // 2) * P
                self.add(stage, src[r:r + n // 2 * P, 256 * c:256 * c + 256], None)
                if piece == 0:
                    self.firsts += 1
                    self.slabs[-1].freed = ("first_piece", self.firsts)
            for _ in range(2):
                self.tile(self.slabs[-1], "x")

    READERS = {"s": ["s_tile"], "rope": ["q_raw", "q_cos"], "v": ["v_tile"], "gate": ["gate_raw"], "pa": ["ya_gated"],
               "pb": ["yb_gated"], "x": ["x_tile"], "fa": ["a_tile"], "fb": ["h_tile"], "conv": ["c_tile"],
               "ba": ["ba_tile"], "lg": ["lg_tile"], "z": ["z_tile"], "f2": ["r_tile"]}

    def tile(self, slab, kind):
        slab.tiles.append(len(self.readers))
        pairs = []
        for name in self.READERS[kind]:
            self.counts[name] = self.counts.get(name, KD if name == "x_tile" else 0) + 1
            pairs.append((name, self.counts[name]))
        self.readers.append(pairs)


class Count:

    def __init__(self):
        self.covered, self.taken, self.sent = {}, {}, {}

    def due(self, name, value):
        fresh = value > self.covered.get(name, 0)
        if fresh:
            self.covered[name] = value
        return fresh

    def next(self, name, k=1):
        self.taken[name] = self.taken.get(name, 0) + k
        return self.taken[name]

    def one(self, name):
        self.sent[name] = self.sent.get(name, 0) + 1
        return 1


SEMS = [
    "load_consts", "load_params", "load_x", "load_pos", "load_rows", "load_lru", "stored",
    "slab_in0", "slab_in1", "slab_in2",
    "split_hi", "split_lo", "main_tile", "first_piece",
    "x_turned", "x_tile", "square", "xg_hi", "xg_lo", "stat_sum", "var", "rs_guess", "rstd", "rtok_sum", "rtok",
    "angle", "sine", "rope_factor", "q_raw", "q_cos", "q_turned", "q_sin", "q_tile",
    "s_tile", "v_tile", "sb_z", "sb_log", "sb_loss", "sb_exponent", "sb_min", "sb_attn", "sb_out",
    "dil_scores", "dil_masked", "dil_exp", "dil_probs", "dil_turned", "dil_pT", "dil_out",
    "hid_hi", "hid_lo",
    "gate_raw", "gate", "ya_gated", "yb_gated", "mixed",
    "a_tile", "a_tap", "a_conv", "a_silu", "a_scaled", "h_tile", "r_tile", "r_square",
    "c_tile", "c_tap", "c_conv", "c_silu", "ba_tile", "lg_tile", "z_tile", "z_silu",
    "d_cum", "d_rows", "d_sum", "d_spread", "d_turned", "d_kk", "d_x0", "d_ax", "d_x", "d_new", "d_state", "d_pred",
    "d_out", "e_beta", "e_rate", "e_shift", "e_log", "e_decay", "e_cum", "e_last", "e_edec", "e_ecum", "e_erow",
    "e_diff", "e_exp", "e_masks", "e_square", "e_var", "e_guess", "e_rs", "e_qk", "e_vtok", "e_kdec", "e_r", "e_qdec",
    "e_at", "e_xt0", "e_x", "e_mm", "e_xt", "e_new", "e_state", "e_osq", "e_og", "e_h",
    "l_log", "l_rate", "l_logits", "l_gates", "l_decay", "l_tanh", "l_minus", "l_root", "l_cubic", "l_gelu", "l_h",
    "y_turned", "y_tile",
    "dve_step", "act_step", "pool_step",
]


def build(nc, w, consts_d, params_d, lru_d, out):
    plan = Plan(w)
    with ExitStack() as ctx:
        S = {n: ctx.enter_context(nc.semaphore(n)) for n in SEMS}

        def sb(name, cols, dt=F32):
            return ctx.enter_context(nc.sbuf_tensor("sb_" + name, [P, cols], dt))[:, :]

        raw = sb("raw", SLOTS * SLAB)
        w_hi = sb("w_hi", SLOTS * SLAB, F32R)
        w_lo = sb("w_lo", SLOTS * SLAB, F32R)
        xt = sb("xt", KD * T)
        xg_hi = sb("xg_hi", KD * T, F32R)
        xg_lo = sb("xg_lo", KD * T, F32R)
        hid_hi = sb("hid_hi", HID * T, F32R)
        hid_lo = sb("hid_lo", HID * T, F32R)
        cst = sb("consts", CONSTS.shape[1])
        par = sb("params", PARAM_COLS["cols"])
        sq = sb("sq", 4 * T)
        rs = sb("rs", 6 * T)
        cs = sb("cs", 4 * T)
        rtok = sb("rtok", NB)
        gfg2 = sb("gfg2", KD)
        small = sb("small", 128)
        scratch = sb("scratch", SCRATCH)
        psum = ctx.enter_context(nc.psum_tensor("psum", [P, 8, 512], F32))

        def C(name, a=0, b=None):
            at, n = CONST_COLS[name]
            return cst[:, at + a:at + (n if b is None else b)]

        def col(name, i=0):
            c = PARAM_COLS[name] + i
            return par[:, c:c + 1]

        class Carve:

            def __init__(self, at=0):
                self.at = at

            def __call__(self, cols):
                a = self.at
                self.at += cols
                assert self.at <= SCRATCH, self.at
                return scratch[:, a:a + cols]

        def tl(buf, i, n=T):
            return buf[:, i * n:(i + 1) * n]

        cut = Carve()
        x_in = scratch[:, 0:NB * D]
        qk = cut(12 * T)
        s_t = cut(4 * T)
        v_tok = cut(NB * 1024)
        gates = cut(16 * T)
        prob = cut(2 * 768)
        pT = cut(2 * 768)
        sb_log = cut(384)
        rope_raw, rope_tmp = gates[:, 0:2 * T], gates[:, 2 * T:4 * T]
        mixA, mixB, mix32 = prob[:, 0:2 * T], prob[:, 2 * T:4 * T], prob[:, 4 * T:6 * T]
        cut = Carve()
        AB = cut(4 * (T + 2))
        y_conv, s_silu, s_scaled, h32 = cut(4 * T), cut(4 * T), cut(4 * T), cut(4 * T)
        cut = Carve()
        qkv = cut(12 * T)
        z_t, lru_x, lru_g = cut(4 * T), cut(4 * T), cut(4 * T)
        mats = cut(4096)
        attn = cut(1024)
        v_tk = cut(1024)
        norm_rows = cut(1024)
        state = cut(512)
        cbuf, c_conv = mats[:, 0:4 * (T + 3)], mats[:, 2048:2048 + 4 * T]
        AT, XX, XT, MM = (tl(mats, i, 1024) for i in range(4))
        k_dec, vn0 = norm_rows[:, 0:512], norm_rows[:, 512:1024]
        r_tok, q_dec = qkv[:, 8 * T:10 * T], qkv[:, 10 * T:12 * T]
        vn1 = v_tk[:, 0:512]
        l_r, l_i, l_a, l_t = (tl(mats, i, 1024) for i in range(4))
        l_scan = attn
        l_hid = v_tk
        l_w = cs
        gain_rows, y_out = scratch[:, 0:D], scratch[:, D:3 * D]

        def flat(bank, a, b):
            return psum_flat[:, bank * 512 + a:bank * 512 + b]

        psum_flat = psum[:, :, :].rearrange("p a b -> p (a b)")

        def part(buf, s):
            i = s.n % SLOTS
            return buf[:, i * SLAB:i * SLAB + s.chunks * s.cols]

        def by_chunk(buf, s):
            return part(buf, s).rearrange("p (k c) -> p k c", k=s.chunks)

        def heads(buf, n=P):
            return buf.rearrange("p (h c) -> p h c", c=n)

        def over_heads(m):
            return m.unsqueeze(1).to_broadcast([P, GH, P])

        VAR, GUESS, TMP, TMP2, RSTD, RSTD2 = (tl(rs, i) for i in range(6))
        COS, SIN, COSR, SINR = (tl(cs, i) for i in range(4))
        N_VAR, N_GUESS, N_TMP, N_RS = (tl(norm_rows, i)[0:8, :] for i in range(4))

        def sm(a, n):
            return small[:, a:a + n]

        dil_bias, dil_den, dil_rden = sm(0, 8), sm(8, 8), sm(16, 8)
        ba, beta, shift, decay, logs = sm(24, 16), sm(40, 8), sm(48, 8), sm(56, 8), sm(64, 8)
        cum, rate, edec, ecum, l_rate, l_log = sm(72, 8), sm(80, 4), sm(84, 4), sm(88, 4), sm(92, 4), sm(96, 4)
        zero_col = sm(100, 1)

        def prob_of(u):
            return tl(prob, u % 2, 768)

        def pT_of(u):
            return tl(pT, u % 2, 768)

        def loss_of(h):
            return tl(pT, h % 2, 768)[:, 0:384]

        def attn_of(h):
            return tl(prob, h % 2, 768)[:, 0:384]

        def v_head(b, i):
            return tl(v_tok, b, 1024)[:, i * HEAD:(i + 1) * HEAD]

        def mat(buf, b, h):
            return buf[:, b * 512 + h * P:b * 512 + h * P + P]

        block = ctx.enter_context(nc.Block())

        @block.sync
        def _(eng):
            q = Count()
            eng.dma_start(x_in.rearrange("p (b d) -> p b d", b=NB),
                          w["x"][0].rearrange("(b p) d -> p b d", p=P)).then_inc(S["load_x"], 16)
            eng.dma_start(cst, consts_d).then_inc(S["load_consts"], 16)
            eng.dma_start(par, params_d).then_inc(S["load_params"], 16)
            eng.dma_start(TMP.bitcast(I32), w["positions"].to_broadcast([P, T])).then_inc(S["load_pos"], 16)
            for s in plan.slabs:
                if q.due("split_lo", s.n - SLOTS + 1):
                    eng.wait_ge(S["split_lo"], s.n - SLOTS + 1)
                eng.dma_start(by_chunk(raw, s), s.src.rearrange("(k p) c -> p k c", p=P))\
                    .then_inc(S[f"slab_in{s.n % SLOTS}"], 16)
                if s.stage == (2, "in") and s.index == 6:
                    if q.due("q_tile", 12 * DEPTH):
                        eng.wait_ge(S["q_tile"], 12 * DEPTH)
                    eng.dma_start(l_w, lru_d).then_inc(S["load_lru"], 16)
                if s.stage == (2, "up", 0) and s.index == 3:
                    if q.due("x_tile", KD + 24 * DEPTH + KD):
                        eng.wait_ge(S["x_tile"], KD + 24 * DEPTH + KD)
                    if q.due("hid_lo", LO_BEFORE_MLP):
                        eng.wait_ge(S["hid_lo"], LO_BEFORE_MLP)
                    eng.dma_start(gain_rows, w["final_norm_w_2"].unsqueeze(0).to_broadcast([P, D]))\
                        .then_inc(S["load_rows"], 16)
            n = 0
            for b in range(NB):
                for half in range(2):
                    n += 1
                    if q.due("y_tile", n):
                        eng.wait_ge(S["y_tile"], n)
                    eng.dma_start(out[0, b * P:(b + 1) * P, half * 512:(half + 1) * 512],
                                  tl(y_out, n - 1, 512)).then_inc(S["stored"], 16)
            eng.wait_ge(S["stored"], 16 * n)

        @block.tensor
        def _(pe):
            q = Count()

            def mul(ps, lhsT, rhs, start=True, stop=True):
                return nc.tensor.matmul(ps, lhsT, rhs, start=start, stop=stop, skip_group_check=True)

            def main_tile(s, t, j, act, base, k0=0, first=True, last=True):
                if first and t >= RING:
                    for name, value in plan.readers[t - RING]:
                        if q.due(name, value):
                            pe.wait_ge(S[name], value)
                if q.due("split_lo", s.n + 1):
                    pe.wait_ge(S["split_lo"], s.n + 1)
                hi, lo = by_chunk(w_hi, s), by_chunk(w_lo, s)
                c = slice(j * P, j * P + P)
                for k in range(s.chunks):
                    if q.due(act[2], base + k0 + k + 1):
                        pe.wait_ge(S[act[2]], base + k0 + k + 1)
                    ah, al = tl(act[0], k0 + k), tl(act[1], k0 + k)
                    if s.kind in ("v", "ba"):
                        ps = psum[:, t % RING, 0:s.cols]
                        trio = [(ah[:, c], hi[:, k, :]), (al[:, c], hi[:, k, :]), (ah[:, c], lo[:, k, :])]
                    else:
                        ps = psum[:, t % RING, 0:T]
                        trio = [(hi[:, k, c], ah), (hi[:, k, c], al), (lo[:, k, c], ah)]
                    for i, (a, b) in enumerate(trio):
                        mm = mul(ps, a, b, first and k == 0 and i == 0, last and k == s.chunks - 1 and i == 2)
                if last:
                    mm.then_inc(S["main_tile"], 1)
                return mm

            def slab_two(s, act, base, between):
                for j, t in enumerate(s.tiles):
                    main_tile(s, t, j, act, base)
                    between(2 * s.index + j)

            def down(stage, base, n, stats, two):
                for s in plan.stages[stage]:
                    last = s.index % 2 == 1
                    tiles = s.tiles if last else plan.slabs[s.n + 1].tiles
                    for j, t in enumerate(tiles):
                        mm = main_tile(s, t, j, hid, base, 0 if not last else n // 2, not last, last)
                        m = s.index // 2 * 2 + j
                        if last and stats and m:
                            stat(m - 1, two)
                    if not last:
                        mm.then_inc(S["first_piece"], 1)

            def stat(m, two=False):
                for n in range(2 if two else 1):
                    pe.wait_ge(S["square"], q.next("square"))
                    mm = mul(psum[:, BANK_T + n, 0:T], C("ones"), tl(sq, 2 * n + m % 2), m == 0, m == KD - 1)
                    mm.then_inc(S["stat_sum"], 1)

            def token_factor(n):
                if q.due("rstd", n):
                    pe.wait_ge(S["rstd"], n)
                for b in range(NB):
                    mm = mul(psum[:, BANK_T + 1, 384 + b:385 + b], RSTD[0:1, b * P:b * P + P], C("ones", 0, 1)[0:1, :])
                mm.then_inc(S["rtok_sum"], 1)

            xg = (xg_hi, xg_lo, "xg_lo")
            hid = (hid_hi, hid_lo, "hid_lo")
            xg_base = hid_base = 0

            if q.due("load_consts", 16):
                pe.wait_ge(S["load_consts"], 16)
            if q.due("load_x", 16):
                pe.wait_ge(S["load_x"], 16)
            xv = x_in.rearrange("p (b d) -> p b d", b=NB)
            for m in range(KD):
                if q.due("x_tile", m - 1):
                    pe.wait_ge(S["x_tile"], m - 1)
                for b in range(NB):
                    mm = nc.tensor.transpose(psum[:, BANK_SC + m % 2, b * P:b * P + P], xv[:, b, m * P:m * P + P], C("ident"))
                mm.then_inc(S["x_turned"], 1)
                if m:
                    stat(m - 1)

            for l in range(DEPTH):
                def turn_q(r):
                    if q.due("rtok", l + 1):
                        pe.wait_ge(S["rtok"], l + 1)
                    if q.due("q_raw", 12 * l + r + 1):
                        pe.wait_ge(S["q_raw"], 12 * l + r + 1)
                    if q.due("q_sin", 12 * l + r - 1):
                        pe.wait_ge(S["q_sin"], 12 * l + r - 1)
                    mul(psum[:, BANK_T + r % 2, 0:T], C("rot"), tl(rope_raw, r % 2)).then_inc(S["q_turned"], 1)

                def sb_a(h):
                    if q.due("s_tile", 4 * (l + 1)):
                        pe.wait_ge(S["s_tile"], 4 * (l + 1))
                    if q.due("sb_min", 4 * l + h - 1):
                        pe.wait_ge(S["sb_min"], 4 * l + h - 1)
                    rows = slice(HEAD * (h % 2), HEAD * (h % 2) + HEAD)
                    ps = psum[:, BANK_SC + h % 2, :]
                    qh, kh = tl(s_t, h // 2)[rows, :], tl(s_t, 2 + h // 2)[rows, :]
                    mul(ps[:, 0:T], kh[:, 0:P], qh, True, False)
                    mul(ps[:, T:T + P], kh[:, P:T], qh[:, P:T], False, False).then_inc(S["sb_z"], 1)

                def sb_b(h):
                    if q.due("sb_loss", 4 * l + h + 1):
                        pe.wait_ge(S["sb_loss"], 4 * l + h + 1)
                    ps = psum[:, BANK_SC + h % 2, :]
                    loss = loss_of(h)
                    mul(ps[:, 0:T], C("neg_ge"), loss[:, 0:T], False, False)
                    mul(ps[:, P:T], C("neg_ones"), loss[:, T:T + P], False, False)
                    mul(ps[:, T:T + P], C("neg_ge"), loss[:, T:T + P], False, True).then_inc(S["sb_exponent"], 1)

                def sb_c(h):
                    if q.due("sb_attn", 4 * l + h + 1):
                        pe.wait_ge(S["sb_attn"], 4 * l + h + 1)
                    if q.due("v_tile", 8 * l + 2):
                        pe.wait_ge(S["v_tile"], 8 * l + 2)
                    o = psum[HEAD * (h % 2):HEAD * (h % 2) + HEAD, BANK_O, :]
                    at = attn_of(h)
                    c = T * (h // 2)
                    mul(o[:, c:c + T], v_head(0, GROUPS * HEADS + h), at[:, 0:T], True, False)
                    mul(o[:, c + P:c + T], v_head(1, GROUPS * HEADS + h), at[:, T:T + P], False, True)\
                        .then_inc(S["sb_out"], 1)

                def dil_a(u):
                    h, qb = u // 2, u % 2
                    keys = (qb + 1) * P
                    if q.due("q_tile", 12 * (l + 1)):
                        pe.wait_ge(S["q_tile"], 12 * (l + 1))
                    if q.due("sb_min", 4 * (l + 1)):
                        pe.wait_ge(S["sb_min"], 4 * (l + 1))
                    if q.due("dil_masked", 8 * l + u):
                        pe.wait_ge(S["dil_masked"], 8 * l + u)
                    rows = slice(HEAD * (h % 2), HEAD * (h % 2) + HEAD)
                    for g in range(GROUPS):
                        tile = (g * HEADS + h) // 2
                        mm = mul(flat(BANK_SC, g * keys, g * keys + keys),
                                 tl(qk, tile)[rows, qb * P:qb * P + P], tl(qk, 6 + tile)[rows, 0:keys])
                    mm.then_inc(S["dil_scores"], 1)

                def dil_b(u):
                    if q.due("dil_probs", 8 * l + u + 1):
                        pe.wait_ge(S["dil_probs"], 8 * l + u + 1)
                    if q.due("dil_pT", 8 * l + u):
                        pe.wait_ge(S["dil_pT"], 8 * l + u)
                    if q.due("q_sin", 12 * (l + 1)):
                        pe.wait_ge(S["q_sin"], 12 * (l + 1))
                    for i in range(GROUPS * (u % 2 + 1)):
                        mm = nc.tensor.transpose(flat(BANK_T, i * P, i * P + P), prob_of(u)[:, i * P:i * P + P], C("ident"))
                    mm.then_inc(S["dil_turned"], 1)

                def dil_c(u):
                    h, qb = u // 2, u % 2
                    if q.due("dil_pT", 8 * l + u + 1):
                        pe.wait_ge(S["dil_pT"], 8 * l + u + 1)
                    if q.due("v_tile", 8 * (l + 1)):
                        pe.wait_ge(S["v_tile"], 8 * (l + 1))
                    if q.due("hid_lo", hid_base + 2):
                        pe.wait_ge(S["hid_lo"], hid_base + 2)
                    n = GROUPS * (qb + 1)
                    c = T * (h // 2) + qb * P
                    o = psum[HEAD * (h % 2):HEAD * (h % 2) + HEAD, BANK_O, c:c + P]
                    for i in range(n):
                        g, kb = i // (qb + 1), i % (qb + 1)
                        mm = mul(o, v_head(kb, g * HEADS + h), pT_of(u)[:, i * P:i * P + P], i == 0, i == n - 1)
                    mm.then_inc(S["dil_out"], 1)

                for s in plan.stages[(l, "in")]:
                    tick = s.index - TICK0
                    if tick >= 2:
                        sb_c(tick - 2) if tick < 6 else dil_c(tick - 6)
                    if tick >= 1:
                        sb_b(tick - 1) if tick < 5 else dil_b(tick - 5)
                    if tick >= 0:
                        sb_a(tick) if tick < 4 else dil_a(tick - 4)

                    def between(i):
                        if i == 0:
                            stat(KD - 1)
                        if i == 3:
                            token_factor(2 * l + 1)
                        if 0 <= i - 7 < 12:
                            turn_q(i - 7)

                    slab_two(s, xg, xg_base, between)
                dil_c(6)
                dil_b(7)
                dil_c(7)
                xg_base += KD
                sa, sbr = plan.stages[(l, "proj")]
                for m in range(KD):
                    main_tile(sa, sa.tiles[m], m, (hid_hi[:, 10 * T:], hid_lo[:, 10 * T:], "hid_lo"), hid_base + 2)
                    main_tile(sbr, sbr.tiles[m], m, (hid_hi[:, 8 * T:], hid_lo[:, 8 * T:], "hid_lo"), hid_base)
                hid_base += 4
                for s in plan.stages[(l, "out")]:
                    slab_two(s, hid, hid_base, lambda i: stat(i - 1) if i else None)
                hid_base += KD
                for half, (f0, n) in enumerate(PARTS1):
                    for s in plan.stages[(l, "up", half)]:
                        slab_two(s, xg, xg_base, lambda i: stat(KD - 1) if i == half == 0 else None)
                    down((l, "down", half), hid_base, n, half == len(PARTS1) - 1, l == DEPTH - 1)
                    hid_base += n
                xg_base += KD

            for s in plan.stages[(2, "in")]:
                def between(i):
                    if i == 0:
                        stat(KD - 1, True)
                    if i == 2:
                        token_factor(5)

                slab_two(s, xg, xg_base, between)
            xg_base += KD

            def wide(buf, i):
                return buf[:, i:i + 1].to_broadcast([buf.shape[0], P])

            if q.due("e_decay", 1):
                pe.wait_ge(S["e_decay"], 1)
            for b in range(NB):
                mm = mul(psum[:, BANK_O, 4 * b:4 * b + 4], C("le"), decay[:, 4 * b:4 * b + 4])
            mm.then_inc(S["d_cum"], 1)
            if q.due("e_beta", 1):
                pe.wait_ge(S["e_beta"], 1)
            for b in range(NB):
                for h in range(GH):
                    mul(psum[:, BANK_SC + b, h * P:h * P + P], wide(decay, 4 * b + h), C("le"))
            for b in range(NB):
                for h in range(GH):
                    mm = mul(psum[:, BANK_T + b, h * P:h * P + P], wide(beta, 4 * b + h), C("ident"))
            mm.then_inc(S["d_rows"], 1)
            if q.due("e_cum", 1):
                pe.wait_ge(S["e_cum"], 1)
            for c in range(8):
                if q.due("e_square", c + 1):
                    pe.wait_ge(S["e_square"], c + 1)
                mm = mul(psum[0:8, BANK_O, 0:T], C("pick", 7 - c, 15 - c), tl(sq, c % 4), c == 0, c == 7)
                mm.then_inc(S["d_sum"], 1)
            if q.due("e_rs", 1):
                pe.wait_ge(S["e_rs"], 1)
            if q.due("e_masks", 2):
                pe.wait_ge(S["e_masks"], 2)
            if q.due("e_edec", 1):
                pe.wait_ge(S["e_edec"], 1)
            if q.due("e_erow", 1):
                pe.wait_ge(S["e_erow"], 1)
            for c in range(8):
                mm = mul(psum[:, BANK_SC + c // 2, (c % 2) * T:(c % 2) * T + T], wide(C("ident")[0:8, :], c), N_RS)
            mm.then_inc(S["d_spread"], 1)
            if q.due("e_qk", 4):
                pe.wait_ge(S["e_qk"], 4)
            for b in range(NB):
                for h in range(GH):
                    nc.tensor.transpose(psum[:, BANK_SC + b, h * P:h * P + P], tl(qkv, 8 + h)[:, b * P:b * P + P], C("ident"))
            for h in range(GH):
                mm = nc.tensor.transpose(psum[:, BANK_O, h * P:h * P + P], tl(qkv, 4 + h)[:, 0:P], C("ident"))
            mm.then_inc(S["d_turned"], 1)
            for b in range(NB):
                if q.due("e_at", b):
                    pe.wait_ge(S["e_at"], b)
                for n, rhs in enumerate((4, 0)):
                    for h in range(GH):
                        mm = mul(psum[:, BANK_T + n, h * P:h * P + P], tl(qkv, 4 + h)[:, b * P:b * P + P],
                                 tl(qkv, rhs + h)[:, b * P:b * P + P])
                mm.then_inc(S["d_kk"], 1)
            if q.due("e_vtok", 2):
                pe.wait_ge(S["e_vtok"], 2)
            for b in range(NB):
                if q.due("e_xt0", b + 1):
                    pe.wait_ge(S["e_xt0"], b + 1)
                for h in range(GH):
                    mm = nc.tensor.transpose(psum[:, BANK_SC + b, h * P:h * P + P], mat(XT, b, h), C("ident"))
                mm.then_inc(S["d_x0"], 1)
            for lv in range(1, LEVELS):
                done = 2 * (lv - 1)
                for b in range(NB):
                    if q.due("e_x", done + b + 1):
                        pe.wait_ge(S["e_x"], done + b + 1)
                    for h in range(GH):
                        mm = mul(psum[:, BANK_SC + b, h * P:h * P + P], mat(AT, b, h), mat(XX, b, h))
                    mm.then_inc(S["d_ax"], 1)
                for b in range(NB):
                    if q.due("e_mm", done + b + 1):
                        pe.wait_ge(S["e_mm"], done + b + 1)
                    if q.due("e_xt", done + b):
                        pe.wait_ge(S["e_xt"], done + b)
                    if lv < LEVELS - 1:
                        if q.due("e_x", 2 + done + b):
                            pe.wait_ge(S["e_x"], 2 + done + b)
                    for h in range(GH):
                        ps = psum[:, BANK_T, h * P:h * P + P]
                        mul(ps, C("ident"), mat(XT, b, h), True, False)
                        mm = mul(ps, mat(MM, b, h), mat(XT, b, h), False, True)
                    if lv < LEVELS - 1:
                        for h in range(GH):
                            ps = psum[:, BANK_T + 1, h * P:h * P + P]
                            mul(ps, C("ident"), mat(XX, b, h), True, False)
                            mm = mul(ps, mat(XT, b, h), mat(MM, b, h), False, True)
                    mm.then_inc(S["d_x"], 1)
            last = 2 * (LEVELS - 1)
            if q.due("e_xt", last - 1):
                pe.wait_ge(S["e_xt"], last - 1)
            if q.due("e_r", 1):
                pe.wait_ge(S["e_r"], 1)
            for h in range(GH):
                mm = mul(psum[:, BANK_SC, h * P:h * P + P], mat(XT, 0, h), tl(r_tok, h, P))
            mm.then_inc(S["d_new"], 1)
            if q.due("e_new", 1):
                pe.wait_ge(S["e_new"], 1)
            if q.due("e_kdec", 1):
                pe.wait_ge(S["e_kdec"], 1)
            for h in range(GH):
                mm = mul(psum[:, BANK_SC + 1, h * P:h * P + P], tl(k_dec, h, P), tl(vn0, h, P))
            mm.then_inc(S["d_state"], 1)
            if q.due("e_state", 1):
                pe.wait_ge(S["e_state"], 1)
            if q.due("e_xt", last):
                pe.wait_ge(S["e_xt"], last)
            for h in range(GH):
                mm = mul(psum[:, BANK_T, h * P:h * P + P], tl(qkv, 4 + h)[:, P:T], tl(state, h, P))
            mm.then_inc(S["d_pred"], 1)
            if q.due("e_r", 2):
                pe.wait_ge(S["e_r"], 2)
            for h in range(GH):
                mm = mul(psum[:, BANK_SC, h * P:h * P + P], mat(XT, 1, h), tl(r_tok, h, P))
            mm.then_inc(S["d_new"], 1)
            if q.due("e_new", 2):
                pe.wait_ge(S["e_new"], 2)
            if q.due("e_qdec", 1):
                pe.wait_ge(S["e_qdec"], 1)
            for h in range(GH):
                o = psum[:, BANK_T + h // 2, (h % 2) * T:(h % 2) * T + T]
                mul(o[:, 0:P], tl(vn0, h, P), mat(attn, 0, h))
                mul(o[:, P:T], tl(vn1, h, P), mat(attn, 1, h), True, False)
                mm = mul(o[:, P:T], tl(state, h, P), tl(q_dec, h, P), False, True)
            mm.then_inc(S["d_out"], 1)
            for h in range(GH):
                if q.due("e_osq", h + 1):
                    pe.wait_ge(S["e_osq"], h + 1)
                mm = mul(psum[0:8, BANK_O, 0:T], C("pick", 7 - h, 15 - h), tl(sq, h), h == 0, h == GH - 1)
                mm.then_inc(S["d_sum"], 1)
            if q.due("e_rs", 2):
                pe.wait_ge(S["e_rs"], 2)
            for h in range(GH):
                mm = mul(psum[:, BANK_SC + h // 2, (h % 2) * T:(h % 2) * T + T], wide(C("ident")[0:8, :], h), N_RS)
            mm.then_inc(S["d_spread"], 1)
            if q.due("load_lru", 16):
                pe.wait_ge(S["load_lru"], 16)
            if q.due("e_h", GH):
                pe.wait_ge(S["e_h"], GH)
            if q.due("c_conv", 16):
                pe.wait_ge(S["c_conv"], 16)
            for n in range(2):
                for t in range(LT):
                    mm = mul(psum[:, BANK_SC + 2 * n + t // 2, (t % 2) * T:(t % 2) * T + T],
                             tl(l_w, n * LT + t, P), tl(lru_x, t))
            mm.then_inc(S["l_logits"], 1)

            for s in plan.stages[(2, "out")]:
                slab_two(s, hid, hid_base, lambda i: stat(i - 1) if i else None)
            hid_base += KD
            for half, (f0, n) in enumerate(PARTS2):
                for s in plan.stages[(2, "up", half)]:
                    slab_two(s, xg, xg_base, lambda i: stat(KD - 1) if i == half == 0 else None)
                down((2, "down", half), hid_base, n, half == len(PARTS2) - 1, False)
                hid_base += n
            for n in range(2 * NB):
                b, half = n // 2, n % 2
                if q.due("y_tile", n - 1):
                    pe.wait_ge(S["y_tile"], n - 1)
                if q.due("x_tile", X_TOTAL):
                    pe.wait_ge(S["x_tile"], X_TOTAL)
                for i in range(4):
                    mm = nc.tensor.transpose(psum[:, BANK_SC + n % 2, i * P:i * P + P],
                                             tl(xt, 4 * half + i)[:, b * P:b * P + P], C("ident"))
                mm.then_inc(S["y_turned"], 1)
                if n == 1:
                    stat(KD - 1)
                    token_factor(7)

        @block.scalar
        def _(act):
            q = Count()
            LOGEXP = "natural_log_exp_and_others"

            def f(out_, in_, func, **kw):
                return nc.scalar.activation(out_, in_, func, **kw)

            def split(n):
                if n >= len(plan.slabs):
                    return
                s = plan.slabs[n]
                if q.due(f"slab_in{n % SLOTS}", 16 * (n // SLOTS + 1)):
                    act.wait_ge(S[f"slab_in{n % SLOTS}"], 16 * (n // SLOTS + 1))
                if n >= SLOTS:
                    name, value = plan.slabs[n - SLOTS].freed
                    if q.due(name, value):
                        act.wait_ge(S[name], value)
                f(part(w_hi, s), part(raw, s), ACT.Copy).then_inc(S["split_hi"], 1)

            def prep(m, gain, square_gain=None):
                act.wait_ge(S["x_tile"], q.next("x_tile"))
                for n in range(2 if square_gain else 1):
                    if m >= 2:
                        if q.due("stat_sum", stats_before + (m - 2) * (2 if square_gain else 1) + n + 1):
                            act.wait_ge(S["stat_sum"], stats_before + (m - 2) * (2 if square_gain else 1) + n + 1)
                    kw = {} if n == 0 else {"scale": square_gain(m)}
                    f(tl(sq, 2 * n + m % 2), tl(xt, m), ACT.Square, **kw).then_inc(S["square"], 1)
                f(tl(xg_hi, m), tl(xt, m), ACT.Copy, scale=gain(m)).then_inc(S["xg_hi"], 1)

            def guess():
                act.preload_act_table_set(LOGEXP)
                act.wait_ge(S["var"], q.next("var"))
                f(GUESS, VAR, ACT.Ln).then_inc(S["act_step"], q.one("act_step"))
                act.wait_ge(S["act_step"], q.sent["act_step"])
                f(GUESS, GUESS, ACT.Exp, scale=-0.5).then_inc(S["rs_guess"], 1)

            def hid_high(i, src):
                f(tl(hid_hi, i), src, ACT.Copy).then_inc(S["hid_hi"], 1)

            stats_before = 0
            if q.due("angle", 1):
                act.wait_ge(S["angle"], 1)
            f(SIN, SINR, ACT.Sin).then_inc(S["sine"], 1)
            f(COS, SINR, ACT.Sin, scale=0.5).then_inc(S["sine"], 1)
            for n in range(SLOTS):
                split(n)
            if q.due("load_params", 16):
                act.wait_ge(S["load_params"], 16)
            for m in range(KD):
                prep(m, lambda m: col("norm_mix0", m))
            stats_before += KD

            for l in range(DEPTH):
                guess()
                for s in plan.stages[(l, "in")]:
                    tick = s.index - TICK0

                    def sb_tick(h):
                        if h:
                            sb_weights(h - 1)
                        if q.due("sb_z", 4 * l + h + 1):
                            act.wait_ge(S["sb_z"], 4 * l + h + 1)
                        if q.due("sb_loss", 4 * l + h):
                            act.wait_ge(S["sb_loss"], 4 * l + h)
                        z = psum[:, BANK_SC + h % 2, 0:384]
                        f(sb_log, z, ACT.Abs).then_inc(S["act_step"], q.one("act_step"))
                        act.wait_ge(S["act_step"], q.sent["act_step"])
                        f(sb_log, sb_log, ACT.Exp, scale=-1.0).then_inc(S["act_step"], q.one("act_step"))
                        act.wait_ge(S["act_step"], q.sent["act_step"])
                        f(sb_log, sb_log, ACT.Ln, bias=1.0).then_inc(S["sb_log"], 1)

                    def sb_weights(h):
                        if q.due("sb_min", 4 * l + h + 1):
                            act.wait_ge(S["sb_min"], 4 * l + h + 1)
                        f(attn_of(h), attn_of(h), ACT.Exp).then_inc(S["sb_attn"], 1)

                    def dil_turned(u):
                        if q.due("dil_turned", 8 * l + u + 1):
                            act.wait_ge(S["dil_turned"], 8 * l + u + 1)
                        n = GROUPS * (u % 2 + 1) * P
                        f(pT_of(u)[:, 0:n], flat(BANK_T, 0, n), ACT.Copy).then_inc(S["dil_pT"], 1)

                    def dil_exp(u):
                        if q.due("dil_masked", 8 * l + u + 1):
                            act.wait_ge(S["dil_masked"], 8 * l + u + 1)
                        n = GROUPS * (u % 2 + 1) * P
                        f(prob_of(u)[:, 0:n], prob_of(u)[:, 0:n], ACT.Exp, scale=-1.0,
                                 bias=dil_bias[:, u:u + 1], accum_out=dil_den[:, u:u + 1]).then_inc(S["dil_exp"], 1)

                    if s.kind == "v":
                        for j, t in enumerate(s.tiles):
                            if q.due("main_tile", t + 1):
                                act.wait_ge(S["main_tile"], t + 1)
                            if q.due("rtok", l + 1):
                                act.wait_ge(S["rtok"], l + 1)
                            v0 = (3 if s.index == 2 else s.index - 9) * T
                            f(tl(v_tok, j, 1024)[:, v0:v0 + T], psum[:, t % RING, 0:T], ACT.Copy,
                                     scale=rtok[:, j:j + 1]).then_inc(S["v_tile"], 1)
                    if s.kind == "rope":
                        for j, t in enumerate(s.tiles):
                            r = 2 * (s.index - 3) + j
                            if q.due("main_tile", t + 1):
                                act.wait_ge(S["main_tile"], t + 1)
                            if q.due("q_turned", 12 * l + r - 1):
                                act.wait_ge(S["q_turned"], 12 * l + r - 1)
                            f(tl(rope_raw, r % 2), psum[:, t % RING, 0:T], ACT.Copy).then_inc(S["q_raw"], 1)
                    if 0 <= tick < 4:
                        sb_tick(tick)
                    elif tick == 4:
                        sb_weights(3)
                    elif tick > 4:
                        dil_turned(tick - 5)
                    if tick >= 4:
                        dil_exp(tick - 4)
                    if tick == 5:
                        if q.due("sb_out", 4 * (l + 1)):
                            act.wait_ge(S["sb_out"], 4 * (l + 1))
                        for i in range(2):
                            hid_high(8 + i, tl(psum[:, BANK_O, :], i))
                    split(s.n + SLOTS)
                dil_turned(7)
                if q.due("dil_out", 8 * (l + 1)):
                    act.wait_ge(S["dil_out"], 8 * (l + 1))
                for i in range(2):
                    hid_high(10 + i, tl(psum[:, BANK_O, :], i))
                for m in range(KD):
                    for i in (m, KD + m):
                        if q.due("gate_raw", 16 * (l + 1)):
                            act.wait_ge(S["gate_raw"], 16 * (l + 1))
                        f(tl(gates, i), tl(gates, i), ACT.Sigmoid, bias=col(f"b_gate{l}", i)).then_inc(S["gate"], 1)
                    if m:
                        act.wait_ge(S["mixed"], q.next("mixed"))
                        hid_high(m - 1, tl(mix32, (m - 1) % 2))
                act.wait_ge(S["mixed"], q.next("mixed"))
                hid_high(KD - 1, tl(mix32, (KD - 1) % 2))
                sa, sbr = plan.stages[(l, "proj")]
                split(sa.n + SLOTS)
                split(sbr.n + SLOTS)
                for s in plan.stages[(l, "out")]:
                    for j in range(2):
                        prep(2 * s.index + j, lambda m: col(f"norm_ffn{l}", m))
                    split(s.n + SLOTS)
                stats_before += KD
                guess()
                for half, (f0, n) in enumerate(PARTS1):
                    for s in plan.stages[(l, "up", half)]:
                        for j in range(2):
                            i = f0 + s.index // 2 * 2 + j
                            r = i % 4
                            if s.kind == "fa":
                                act.wait_ge(S["a_tile"], q.next("a_tile"))
                                if q.due("a_silu", q.sent.get("a_silu", 0)):
                                    act.wait_ge(S["a_silu"], q.sent.get("a_silu", 0))
                                f(tl(y_conv, r), tl(AB, r, T + 2)[:, 2:], ACT.Identity,
                                         scale=col(f"conv_w{l}", 2 * FF_TILES + i), bias=col(f"conv_b{l}", i))\
                                             .then_inc(S["a_tap"], 1)
                            else:
                                act.wait_ge(S["h_tile"], q.next("h_tile"))
                                hid_high(i - f0, tl(h32, r))
                        if s.kind == "fa":
                            split(s.n + SLOTS)
                            for j in range(2):
                                r = (f0 + s.index // 2 * 2 + j) % 4
                                act.wait_ge(S["a_conv"], q.next("a_conv"))
                                if q.due("a_scaled", q.sent.get("a_silu", 0) - 3):
                                    act.wait_ge(S["a_scaled"], q.sent.get("a_silu", 0) - 3)
                                f(tl(s_silu, r), tl(y_conv, r), ACT.Silu).then_inc(S["a_silu"], q.one("a_silu"))
                        else:
                            split(s.n + SLOTS)
                    for s in plan.stages[(l, "down", half)]:
                        if s.index % 2 == 1:
                            for j in range(2):
                                m = s.index // 2 * 2 + j
                                if half < len(PARTS1) - 1:
                                    act.wait_ge(S["x_tile"], q.next("x_tile"))
                                elif l < DEPTH - 1:
                                    prep(m, lambda m: col(f"norm_mix{l + 1}", m))
                                else:
                                    prep(m, lambda m: gfg2[:, m:m + 1], lambda m: col("norm_final", m))
                        split(s.n + SLOTS)
                stats_before += KD * (2 if l == DEPTH - 1 else 1)

            guess()
            guess()
            conv = 0
            for s in plan.stages[(2, "in")]:
                if s.kind == "conv":
                    lru = conv >= 12
                    for j in range(2):
                        c = conv + j
                        act.wait_ge(S["c_tile"], q.next("c_tile"))
                        if c >= 4:
                            if q.due("c_silu", min(c - 3, 12)):
                                act.wait_ge(S["c_silu"], min(c - 3, 12))
                        f(tl(lru_x, c - 12) if lru else tl(c_conv, c % 4), tl(cbuf, c % 4, T + 3)[:, 3:],
                                 ACT.Identity, scale=col("lru_conv", 3 * LT + c - 12) if lru else col("gdn_conv", 36 + c),
                                 bias=col("lru_conv_b", c - 12) if lru else zero_col).then_inc(S["c_tap"], 1)
                    split(s.n + SLOTS)
                    for j in range(2):
                        if not lru:
                            act.wait_ge(S["c_conv"], q.next("c_conv"))
                            f(tl(qkv, conv + j), tl(c_conv, (conv + j) % 4), ACT.Silu).then_inc(S["c_silu"], 1)
                    conv += 2
                elif s.kind == "z":
                    for j in range(2):
                        act.wait_ge(S["z_tile"], q.next("z_tile"))
                        i = 2 * (s.index - 11) + j
                        f(tl(z_t, i), tl(z_t, i), ACT.Silu).then_inc(S["z_silu"], 1)
                    split(s.n + SLOTS)
                else:
                    split(s.n + SLOTS)
            ba_v = ba.rearrange("p (b c) -> p b c", b=NB)
            if q.due("ba_tile", 2):
                act.wait_ge(S["ba_tile"], 2)
            f(beta.rearrange("p (b c) -> p b c", b=NB), ba_v[:, :, 0:4], ACT.Sigmoid).then_inc(S["e_beta"], 1)
            act.preload_act_table_set(LOGEXP)
            f(rate, par[:, PARAM_COLS["A_log"]:PARAM_COLS["A_log"] + GH], ACT.Exp).then_inc(S["e_rate"], 1)
            for src, dst, name, scale in ((shift, logs, "e_log", 1.0),
                                          (par[:, PARAM_COLS["a_param"]:PARAM_COLS["a_param"] + LT], l_log, "l_log", 1.0)):
                if name == "e_log":
                    if q.due("e_shift", 1):
                        act.wait_ge(S["e_shift"], 1)
                f(dst, src, ACT.Abs).then_inc(S["act_step"], q.one("act_step"))
                act.wait_ge(S["act_step"], q.sent["act_step"])
                f(dst, dst, ACT.Exp, scale=-1.0).then_inc(S["act_step"], q.one("act_step"))
                act.wait_ge(S["act_step"], q.sent["act_step"])
                f(dst, dst, ACT.Ln, bias=1.0).then_inc(S[name], q.one(name))
            for c in range(8):
                if q.due("c_silu", 8):
                    act.wait_ge(S["c_silu"], 8)
                if q.due("d_sum", c - 3):
                    act.wait_ge(S["d_sum"], c - 3)
                f(tl(sq, c % 4), tl(qkv, c), ACT.Square).then_inc(S["e_square"], 1)
            if q.due("e_last", 1):
                act.wait_ge(S["e_last"], 1)
            f(edec, edec, ACT.Exp).then_inc(S["e_edec"], 1)
            if q.due("e_cum", 1):
                act.wait_ge(S["e_cum"], 1)
            f(ecum, cum[:, 4:8], ACT.Exp).then_inc(S["e_ecum"], 1)
            if q.due("d_rows", 1):
                act.wait_ge(S["d_rows"], 1)
            f(state, psum[:, BANK_SC + 1, :], ACT.Exp).then_inc(S["e_erow"], 1)
            for b in range(NB):
                if q.due("e_diff", b + 1):
                    act.wait_ge(S["e_diff"], b + 1)
                f(tl(MM, b, 512), tl(MM, b, 512), ACT.Exp).then_inc(S["e_exp"], 1)

            def row_guess():
                act.wait_ge(S["e_var"], q.next("e_var"))
                f(N_GUESS, N_VAR, ACT.Ln).then_inc(S["act_step"], q.one("act_step"))
                act.wait_ge(S["act_step"], q.sent["act_step"])
                f(N_GUESS, N_GUESS, ACT.Exp, scale=-0.5).then_inc(S["e_guess"], 1)

            row_guess()
            if q.due("d_turned", 1):
                act.wait_ge(S["d_turned"], 1)
            for b in range(NB):
                f(tl(v_tk, b, 512), psum[:, BANK_SC + b, :], ACT.Copy).then_inc(S["e_vtok"], 1)
            for b in range(NB):
                if q.due("d_x0", b + 1):
                    act.wait_ge(S["d_x0"], b + 1)
                f(tl(XX, b, 512), psum[:, BANK_SC + b, :], ACT.Copy).then_inc(S["e_x"], 1)
            for lv in range(1, LEVELS):
                for b in range(NB):
                    act.wait_ge(S["d_x"], q.next("d_x"))
                    f(tl(XT, b, 512), psum[:, BANK_T, :], ACT.Copy).then_inc(S["e_xt"], 1)
                    if lv < LEVELS - 1:
                        f(tl(XX, b, 512), psum[:, BANK_T + 1, :], ACT.Copy).then_inc(S["e_x"], 1)
            if q.due("d_new", 1):
                act.wait_ge(S["d_new"], 1)
            if q.due("e_kdec", 1):
                act.wait_ge(S["e_kdec"], 1)
            f(vn0, psum[:, BANK_SC, :], ACT.Copy).then_inc(S["e_new"], 1)
            if q.due("d_state", 1):
                act.wait_ge(S["d_state"], 1)
            if q.due("e_qdec", 1):
                act.wait_ge(S["e_qdec"], 1)
            f(state, psum[:, BANK_SC + 1, :], ACT.Copy).then_inc(S["e_state"], 1)
            if q.due("d_new", 2):
                act.wait_ge(S["d_new"], 2)
            if q.due("e_r", 2):
                act.wait_ge(S["e_r"], 2)
            f(vn1, psum[:, BANK_SC, :], ACT.Copy).then_inc(S["e_new"], 1)
            if q.due("d_out", 1):
                act.wait_ge(S["d_out"], 1)
            for h in range(GH):
                f(tl(sq, h), psum[:, BANK_T + h // 2, (h % 2) * T:(h % 2) * T + T], ACT.Square)\
                    .then_inc(S["e_osq"], 1)
            row_guess()
            for h in range(GH):
                if q.due("e_h", h + 1):
                    act.wait_ge(S["e_h"], h + 1)
                hid_high(h, tl(z_t, h))
            if q.due("l_logits", 1):
                act.wait_ge(S["l_logits"], 1)
            for n, (dst, name) in enumerate(((l_r, "gate_a_b"), (l_i, "gate_x_b"))):
                for t in range(LT):
                    f(tl(dst, t), psum[:, BANK_SC + 2 * n + t // 2, (t % 2) * T:(t % 2) * T + T], ACT.Sigmoid,
                             bias=col(name, t)).then_inc(S["l_gates"], q.one("l_gates"))
            if q.due("l_rate", 1):
                act.wait_ge(S["l_rate"], 1)
            act.wait_ge(S["l_gates"], q.sent["l_gates"])
            for t in range(LT):
                f(tl(l_a, t), tl(l_r, t), ACT.Exp, scale=l_rate[:, t:t + 1]).then_inc(S["l_decay"], 1)
                f(tl(l_t, t), tl(l_r, t), ACT.Tanh, scale=l_rate[:, t:t + 1]).then_inc(S["l_tanh"], 1)
            if q.due("l_cubic", 1):
                act.wait_ge(S["l_cubic"], 1)
            f(l_scan, l_scan, ACT.Tanh, scale=GELU_C).then_inc(S["l_gelu"], 1)
            if q.due("l_minus", 1):
                act.wait_ge(S["l_minus"], 1)
            f(l_t, l_t, ACT.Sqrt, scale=-1.0).then_inc(S["l_root"], 1)
            for t in range(LT):
                if q.due("l_h", t + 1):
                    act.wait_ge(S["l_h"], t + 1)
                hid_high(GH + t, tl(l_hid, t))
            for s in plan.stages[(2, "out")]:
                for j in range(2):
                    prep(2 * s.index + j, lambda m: col("norm_mlp", m))
                split(s.n + SLOTS)
            stats_before += KD
            guess()
            for half, (f0, n) in enumerate(PARTS2):
                for s in plan.stages[(2, "up", half)]:
                    for j in range(2):
                        act.wait_ge(S["r_square"], q.next("r_square"))
                        hid_high(2 * s.index + j, tl(h32, (f0 + 2 * s.index + j) % 4))
                    split(s.n + SLOTS)
                for s in plan.stages[(2, "down", half)]:
                    if s.index % 2 == 1:
                        for j in range(2):
                            m = s.index // 2 * 2 + j
                            act.wait_ge(S["x_tile"], q.next("x_tile"))
                            if half == len(PARTS2) - 1:
                                if q.due("stat_sum", stats_before + m - 1):
                                    act.wait_ge(S["stat_sum"], stats_before + m - 1)
                                f(tl(sq, m % 2), tl(xt, m), ACT.Square).then_inc(S["square"], 1)
                    split(s.n + SLOTS)
            guess()

        @block.vector
        def _(dve):
            q = Count()
            v = nc.vector

            def stt(out_, a, scalar, b, op0, op1):
                return v.scalar_tensor_tensor(out=out_, in0=a, scalar=scalar, in1=b, op0=op0, op1=op1)

            def split(n):
                if n >= len(plan.slabs):
                    return
                s = plan.slabs[n]
                if q.due("split_hi", n + 1):
                    dve.wait_ge(S["split_hi"], n + 1)
                v.tensor_tensor(part(w_lo, s), part(raw, s), part(w_hi, s).bitcast(F32), ALU.subtract)\
                    .then_inc(S["split_lo"], 1)

            def x_low(m, gain):
                dve.wait_ge(S["xg_hi"], q.next("xg_hi"))
                stt(tl(xg_lo, m), tl(xt, m), gain(m), tl(xg_hi, m).bitcast(F32), ALU.mult, ALU.subtract)\
                    .then_inc(S["xg_lo"], 1)

            def x_add(m, t):
                if q.due("main_tile", t + 1):
                    dve.wait_ge(S["main_tile"], t + 1)
                v.tensor_tensor(tl(xt, m), tl(xt, m), psum[:, t % RING, 0:T], ALU.add).then_inc(S["x_tile"], 1)

            def x_stage(slabs, gain):
                for s in slabs:
                    for j, t in enumerate(s.tiles):
                        m = t - first_tile(slabs)
                        x_add(m, t)
                        if gain and m:
                            x_low(m - 1, gain)
                    if s is slabs[-1] and gain:
                        x_low(KD - 1, gain)
                    split(s.n + SLOTS)

            def first_tile(slabs):
                return next(s.tiles[0] for s in slabs if s.tiles)

            def newton(var, guess_, tmp, dst, signal):
                v.tensor_tensor(tmp, guess_, guess_, ALU.mult).then_inc(S["dve_step"], q.one("dve_step"))
                dve.wait_ge(S["dve_step"], q.sent["dve_step"])
                stt(tmp, tmp, -0.5, var, ALU.mult, ALU.mult).then_inc(S["dve_step"], q.one("dve_step"))
                dve.wait_ge(S["dve_step"], q.sent["dve_step"])
                stt(dst, tmp, 1.5, guess_, ALU.add, ALU.mult).then_inc(S[signal], q.one(signal))

            def variance(n, eps):
                if q.due("stat_sum", n):
                    dve.wait_ge(S["stat_sum"], n)
                v.tensor_scalar(VAR, psum[:, BANK_T, 0:T], 1.0 / D, eps, ALU.mult, ALU.add)\
                    .then_inc(S["var"], q.one("var"))

            def norm(n, eps):
                variance(n, eps)
                dve.wait_ge(S["rs_guess"], q.next("rs_guess"))
                newton(VAR, GUESS, TMP, RSTD, "rstd")
                dve.wait_ge(S["rstd"], q.sent["rstd"])

            def take_rtok(n):
                if q.due("rtok_sum", n):
                    dve.wait_ge(S["rtok_sum"], n)
                v.tensor_copy(rtok, psum[:, BANK_T + 1, 384:384 + NB]).then_inc(S["rtok"], q.one("rtok"))
                dve.wait_ge(S["rtok"], q.sent["rtok"])

            def hid_low(i, src):
                dve.wait_ge(S["hid_hi"], q.next("hid_hi"))
                v.tensor_tensor(tl(hid_lo, i), src, tl(hid_hi, i).bitcast(F32), ALU.subtract).then_inc(S["hid_lo"], 1)

            if q.due("load_pos", 16):
                dve.wait_ge(S["load_pos"], 16)
            if q.due("load_consts", 16):
                dve.wait_ge(S["load_consts"], 16)
            v.tensor_copy(VAR, TMP.bitcast(I32)).then_inc(S["dve_step"], q.one("dve_step"))
            dve.wait_ge(S["dve_step"], q.sent["dve_step"])
            v.tensor_scalar(VAR, VAR, C("inv_freq"), None, ALU.mult).then_inc(S["dve_step"], q.one("dve_step"))
            dve.wait_ge(S["dve_step"], q.sent["dve_step"])
            v.tensor_scalar(TMP2, VAR, 1.0 / (2 * np.pi), ROUND, ALU.mult, ALU.add)\
                .then_inc(S["dve_step"], q.one("dve_step"))
            dve.wait_ge(S["dve_step"], q.sent["dve_step"])
            v.tensor_scalar(TMP2, TMP2, ROUND, None, ALU.subtract).then_inc(S["dve_step"], q.one("dve_step"))
            dve.wait_ge(S["dve_step"], q.sent["dve_step"])
            for c in TWO_PI:
                stt(VAR, TMP2, -c, VAR, ALU.mult, ALU.add).then_inc(S["dve_step"], q.one("dve_step"))
                dve.wait_ge(S["dve_step"], q.sent["dve_step"])
            v.tensor_scalar(SINR, VAR, PI_BELOW, -PI_BELOW, ALU.min, ALU.max).then_inc(S["angle"], 1)
            for n in range(SLOTS):
                split(n)
            if q.due("load_params", 16):
                dve.wait_ge(S["load_params"], 16)
            for m in range(KD):
                if q.due("x_turned", m + 1):
                    dve.wait_ge(S["x_turned"], m + 1)
                v.tensor_copy(tl(xt, m), psum[:, BANK_SC + m % 2, 0:T]).then_inc(S["x_tile"], 1)
                if m:
                    x_low(m - 1, lambda m: col("norm_mix0", m))
            x_low(KD - 1, lambda m: col("norm_mix0", m))
            if q.due("sine", 2):
                dve.wait_ge(S["sine"], 2)
            v.tensor_tensor(COS, COS, COS, ALU.mult).then_inc(S["dve_step"], q.one("dve_step"))
            dve.wait_ge(S["dve_step"], q.sent["dve_step"])
            v.tensor_scalar(COS, COS, -2.0, 1.0, ALU.mult, ALU.add).then_inc(S["dve_step"], q.one("dve_step"))
            dve.wait_ge(S["dve_step"], q.sent["dve_step"])
            v.memset(zero_col, 0.0).then_inc(S["dve_step"], q.one("dve_step"))
            dve.wait_ge(S["dve_step"], q.sent["dve_step"])
            v.tensor_tensor(gfg2, par[:, PARAM_COLS["norm_final"]:PARAM_COLS["norm_final"] + KD],
                                 par[:, PARAM_COLS["norm_mix2"]:PARAM_COLS["norm_mix2"] + KD], ALU.mult)\
                                     .then_inc(S["dve_step"], q.one("dve_step"))
            dve.wait_ge(S["dve_step"], q.sent["dve_step"])
            stats = KD

            for l in range(DEPTH):
                def q_sin(r):
                    if q.due("q_turned", 12 * l + r + 1):
                        dve.wait_ge(S["q_turned"], 12 * l + r + 1)
                    if q.due("q_tile", 12 * l + r - 1):
                        dve.wait_ge(S["q_tile"], 12 * l + r - 1)
                    v.tensor_tensor(tl(rope_tmp, r % 2), psum[:, BANK_T + r % 2, 0:T], SINR, ALU.mult)\
                        .then_inc(S["q_sin"], 1)

                def sb_loss(h):
                    if q.due("sb_log", 4 * l + h + 1):
                        dve.wait_ge(S["sb_log"], 4 * l + h + 1)
                    loss = loss_of(h)
                    stt(loss, psum[:, BANK_SC + h % 2, 0:384], 0.0, sb_log, ALU.max, ALU.add)\
                        .then_inc(S["dve_step"], q.one("dve_step"))
                    dve.wait_ge(S["dve_step"], q.sent["dve_step"])
                    ends = loss.rearrange("p (n c) -> p n c", c=P)[:, 0:3:2, :]
                    v.tensor_tensor(ends, ends, C("lt").unsqueeze(1).to_broadcast([P, 2, P]), ALU.mult)\
                        .then_inc(S["sb_loss"], 1)

                def sb_min(h):
                    if q.due("sb_exponent", 4 * l + h + 1):
                        dve.wait_ge(S["sb_exponent"], 4 * l + h + 1)
                    stt(attn_of(h), psum[:, BANK_SC + h % 2, 0:384], 0.0, C("sb_mask"), ALU.min, ALU.add)\
                        .then_inc(S["sb_min"], 1)

                def dil_mask(u):
                    if q.due("dil_scores", 8 * l + u + 1):
                        dve.wait_ge(S["dil_scores"], 8 * l + u + 1)
                    n = GROUPS * (u % 2 + 1) * P
                    v.tensor_tensor_reduce(prob_of(u)[:, 0:n], flat(BANK_SC, 0, n), C(f"dil_mask{u % 2}"),
                                                  -HEAD ** -0.5, 3e38, ALU.add, ALU.min, dil_bias[:, u:u + 1])\
                                                      .then_inc(S["dil_masked"], 1)

                def dil_scale(u):
                    if q.due("dil_exp", 8 * l + u + 1):
                        dve.wait_ge(S["dil_exp"], 8 * l + u + 1)
                    n = GROUPS * (u % 2 + 1) * P
                    v.reciprocal(dil_rden[:, u:u + 1], dil_den[:, u:u + 1]).then_inc(S["dve_step"], q.one("dve_step"))
                    dve.wait_ge(S["dve_step"], q.sent["dve_step"])
                    v.tensor_scalar(prob_of(u)[:, 0:n], prob_of(u)[:, 0:n], dil_rden[:, u:u + 1], None, ALU.mult)\
                        .then_inc(S["dil_probs"], 1)

                norm(stats, EPS1)
                v.tensor_tensor(COSR, COS, RSTD, ALU.mult).then_inc(S["dve_step"], q.one("dve_step"))
                dve.wait_ge(S["dve_step"], q.sent["dve_step"])
                v.tensor_tensor(SINR, SIN, RSTD, ALU.mult).then_inc(S["dve_step"], q.one("dve_step"))
                dve.wait_ge(S["dve_step"], q.sent["dve_step"])
                for s in plan.stages[(l, "in")]:
                    tick = s.index - TICK0
                    for j, t in enumerate(s.tiles):
                        i = 2 * s.index + j
                        ps = psum[:, t % RING, 0:T]
                        if s.kind == "s":
                            if q.due("main_tile", t + 1):
                                dve.wait_ge(S["main_tile"], t + 1)
                            stt(tl(s_t, i), ps, HEAD ** -0.5 if i < 2 else 1.0, RSTD, ALU.mult, ALU.mult)\
                                .then_inc(S["s_tile"], 1)
                        if s.kind == "rope":
                            if q.due("q_raw", 12 * l + i - 5):
                                dve.wait_ge(S["q_raw"], 12 * l + i - 5)
                            v.tensor_tensor(tl(qk, i - 6), ps, COSR, ALU.mult).then_inc(S["q_cos"], 1)
                        if i == 4:
                            take_rtok(l + 1)
                        if 0 <= i - 8 < 12:
                            q_sin(i - 8)
                    if 1 <= tick < 5:
                        sb_min(tick - 1)
                    if 0 <= tick < 4:
                        sb_loss(tick)
                    elif tick >= 4:
                        dil_mask(tick - 4)
                    if tick == 5:
                        if q.due("hid_hi", q.taken.get("hid_hi", 0) + 2):
                            dve.wait_ge(S["hid_hi"], q.taken.get("hid_hi", 0) + 2)
                        for i in range(2):
                            hid_low(8 + i, tl(psum[:, BANK_O, :], i))
                    if s.kind == "gate":
                        for j, t in enumerate(s.tiles):
                            if q.due("main_tile", t + 1):
                                dve.wait_ge(S["main_tile"], t + 1)
                            v.tensor_tensor(tl(gates, 2 * (s.index - 12) + j), psum[:, t % RING, 0:T], RSTD, ALU.mult)\
                                .then_inc(S["gate_raw"], 1)
                    split(s.n + SLOTS)
                    if tick >= 4:
                        dil_scale(tick - 4)
                if q.due("hid_hi", q.taken["hid_hi"] + 2):
                    dve.wait_ge(S["hid_hi"], q.taken["hid_hi"] + 2)
                for i in range(2):
                    hid_low(10 + i, tl(psum[:, BANK_O, :], i))
                sa, sbr = plan.stages[(l, "proj")]
                for m in range(KD):
                    if q.due("mixed", KD * l + m - 1):
                        dve.wait_ge(S["mixed"], KD * l + m - 1)
                    for s, buf, i, name in ((sa, mixA, m, "ya_gated"), (sbr, mixB, KD + m, "yb_gated")):
                        t = s.tiles[m]
                        if q.due("main_tile", t + 1):
                            dve.wait_ge(S["main_tile"], t + 1)
                        if q.due("gate", 16 * l + 2 * m + (1 if s is sa else 2)):
                            dve.wait_ge(S["gate"], 16 * l + 2 * m + (1 if s is sa else 2))
                        v.tensor_tensor(tl(buf, m % 2), psum[:, t % RING, 0:T], tl(gates, i), ALU.mult)\
                            .then_inc(S[name], q.one(name))
                    if m:
                        hid_low(m - 1, tl(mix32, (m - 1) % 2))
                hid_low(KD - 1, tl(mix32, (KD - 1) % 2))
                split(sa.n + SLOTS)
                split(sbr.n + SLOTS)
                x_stage(plan.stages[(l, "out")], lambda m: col(f"norm_ffn{l}", m))
                stats += KD
                norm(stats, EPS1)
                for r in range(4):
                    v.memset(tl(AB, r, T + 2)[:, 0:2], 0.0).then_inc(S["dve_step"], q.one("dve_step"))
                for half, (f0, n) in enumerate(PARTS1):
                    for s in plan.stages[(l, "up", half)]:
                        for j, t in enumerate(s.tiles):
                            r = (f0 + s.index // 2 * 2 + j) % 4
                            if q.due("main_tile", t + 1):
                                dve.wait_ge(S["main_tile"], t + 1)
                            ps = psum[:, t % RING, 0:T]
                            if s.kind == "fa":
                                v.tensor_tensor(tl(AB, r, T + 2)[:, 2:], ps, RSTD, ALU.mult).then_inc(S["a_tile"], 1)
                            else:
                                dve.wait_ge(S["a_scaled"], q.next("a_scaled"))
                                v.tensor_tensor(tl(h32, r), ps, tl(s_scaled, r), ALU.mult).then_inc(S["h_tile"], 1)
                        for j in range(2):
                            i = f0 + s.index // 2 * 2 + j
                            r = i % 4
                            if s.kind == "fa":
                                dve.wait_ge(S["a_tap"], q.next("a_tap"))
                                dve.wait_ge(S["dve_step"], q.sent["dve_step"])
                                for tap in (1, 0):
                                    ins = stt(tl(y_conv, r), tl(AB, r, T + 2)[:, tap:tap + T],
                                              col(f"conv_w{l}", tap * FF_TILES + i), tl(y_conv, r), ALU.mult, ALU.add)
                                    if tap:
                                        ins.then_inc(S["dve_step"], q.one("dve_step"))
                                        dve.wait_ge(S["dve_step"], q.sent["dve_step"])
                                    else:
                                        ins.then_inc(S["a_conv"], 1)
                            else:
                                hid_low(i - f0, tl(h32, r))
                        split(s.n + SLOTS)
                    last = half == len(PARTS1) - 1
                    gain = None
                    if last:
                        gain = (lambda m: col(f"norm_mix{l + 1}", m)) if l < DEPTH - 1 else (lambda m: gfg2[:, m:m + 1])
                    x_stage(plan.stages[(l, "down", half)], gain)
                stats += KD * (2 if l == DEPTH - 1 else 1)

            variance(stats, EPS1)
            dve.wait_ge(S["rs_guess"], q.next("rs_guess"))
            newton(VAR, GUESS, TMP, RSTD, "dve_step")
            dve.wait_ge(S["dve_step"], q.sent["dve_step"])
            v.tensor_tensor(TMP, RSTD, RSTD, ALU.mult).then_inc(S["dve_step"], q.one("dve_step"))
            dve.wait_ge(S["dve_step"], q.sent["dve_step"])
            stt(TMP, psum[:, BANK_T + 1, 0:T], 1.0 / D, TMP, ALU.mult, ALU.mult)\
                .then_inc(S["dve_step"], q.one("dve_step"))
            dve.wait_ge(S["dve_step"], q.sent["dve_step"])
            v.tensor_scalar(VAR, TMP, EPS2, None, ALU.add).then_inc(S["var"], q.one("var"))
            for m in range(KD):
                stt(tl(xt, m), tl(xt, m), col("norm_final", m), RSTD, ALU.mult, ALU.mult)\
                    .then_inc(S["dve_step"], q.one("dve_step"))
            dve.wait_ge(S["var"], q.sent["var"])
            dve.wait_ge(S["rs_guess"], q.next("rs_guess"))
            newton(VAR, GUESS, TMP, RSTD2, "dve_step")
            dve.wait_ge(S["dve_step"], q.sent["dve_step"])
            v.tensor_tensor(RSTD, RSTD, RSTD2, ALU.mult).then_inc(S["rstd"], q.one("rstd"))
            dve.wait_ge(S["rstd"], q.sent["rstd"])
            for r in range(4):
                v.memset(tl(cbuf, r, T + 3)[:, 0:3], 0.0).then_inc(S["dve_step"], q.one("dve_step"))
            conv = 0
            for s in plan.stages[(2, "in")]:
                for j, t in enumerate(s.tiles):
                    if q.due("main_tile", t + 1):
                        dve.wait_ge(S["main_tile"], t + 1)
                    ps = psum[:, t % RING, 0:T]
                    if s.kind == "conv":
                        v.tensor_tensor(tl(cbuf, (conv + j) % 4, T + 3)[:, 3:], ps, RSTD, ALU.mult)\
                            .then_inc(S["c_tile"], 1)
                    if s.kind == "ba":
                        v.tensor_scalar(tl(ba, j, 8), ps[:, 0:8], rtok[:, j:j + 1], None, ALU.mult)\
                            .then_inc(S["ba_tile"], q.one("ba_tile"))
                    if s.kind == "z":
                        v.tensor_tensor(tl(z_t, 2 * (s.index - 11) + j), ps, RSTD, ALU.mult).then_inc(S["z_tile"], 1)
                    if s.kind == "lg":
                        v.tensor_tensor(tl(lru_g, 2 * (s.index - 9) + j), ps, RSTD, ALU.mult)\
                            .then_inc(S["lg_tile"], q.one("lg_tile"))
                if s.index == 1:
                    take_rtok(DEPTH + 1)
                if s.kind == "conv":
                    for j in range(2):
                        c = conv + j
                        lru = c >= 12
                        dst = tl(lru_x, c - 12) if lru else tl(c_conv, c % 4)
                        dve.wait_ge(S["c_tap"], q.next("c_tap"))
                        dve.wait_ge(S["dve_step"], q.sent["dve_step"])
                        for tap in (2, 1, 0):
                            g = col("lru_conv", tap * LT + c - 12) if lru else col("gdn_conv", tap * 12 + c)
                            ins = stt(dst, tl(cbuf, c % 4, T + 3)[:, tap:tap + T], g, dst, ALU.mult, ALU.add)
                            if tap:
                                ins.then_inc(S["dve_step"], q.one("dve_step"))
                                dve.wait_ge(S["dve_step"], q.sent["dve_step"])
                            else:
                                ins.then_inc(S["c_conv"], q.one("c_conv"))
                    conv += 2
                split(s.n + SLOTS)

            ba_v = ba.rearrange("p (b c) -> p b c", b=NB)
            dt = par[:, PARAM_COLS["dt_bias"]:PARAM_COLS["dt_bias"] + GH]
            dve.wait_ge(S["ba_tile"], q.sent["ba_tile"])
            v.tensor_tensor(shift.rearrange("p (b c) -> p b c", b=NB), ba_v[:, :, 4:8],
                                   dt.unsqueeze(1).to_broadcast([P, NB, GH]), ALU.add)\
                                       .then_inc(S["e_shift"], q.one("e_shift"))
            dve.wait_ge(S["e_shift"], q.sent["e_shift"])
            if q.due("e_log", 1):
                dve.wait_ge(S["e_log"], 1)
            stt(decay, shift, 0.0, logs, ALU.max, ALU.add).then_inc(S["dve_step"], q.one("dve_step"))
            dve.wait_ge(S["dve_step"], q.sent["dve_step"])
            if q.due("e_rate", 1):
                dve.wait_ge(S["e_rate"], 1)
            stt(decay.rearrange("p (b c) -> p b c", b=NB), decay.rearrange("p (b c) -> p b c", b=NB), -1.0,
                       rate.unsqueeze(1).to_broadcast([P, NB, GH]), ALU.mult, ALU.mult).then_inc(S["e_decay"], 1)
            if q.due("l_log", 1):
                dve.wait_ge(S["l_log"], 1)
            ap = par[:, PARAM_COLS["a_param"]:PARAM_COLS["a_param"] + LT]
            v.tensor_scalar(l_rate, ap, -1.0, 0.0, ALU.mult, ALU.max).then_inc(S["dve_step"], q.one("dve_step"))
            dve.wait_ge(S["dve_step"], q.sent["dve_step"])
            v.tensor_tensor(l_rate, l_rate, l_log, ALU.add).then_inc(S["dve_step"], q.one("dve_step"))
            dve.wait_ge(S["dve_step"], q.sent["dve_step"])
            v.tensor_scalar(l_rate, l_rate, -LRU_C, None, ALU.mult).then_inc(S["l_rate"], 1)
            if q.due("d_cum", 1):
                dve.wait_ge(S["d_cum"], 1)
            v.tensor_copy(cum, psum[:, BANK_O, 0:8]).then_inc(S["e_cum"], q.one("e_cum"))
            dve.wait_ge(S["e_cum"], q.sent["e_cum"])
            if q.due("d_rows", 1):
                dve.wait_ge(S["d_rows"], 1)
            v.tensor_tensor(edec.unsqueeze(2), heads(psum[:, BANK_SC, :])[:, :, P - 1:P], cum[:, 0:4].unsqueeze(2),
                                   ALU.subtract).then_inc(S["e_last"], 1)
            if q.due("e_erow", 1):
                dve.wait_ge(S["e_erow"], 1)
            for b in range(NB):
                for h in range(GH):
                    ins = v.tensor_scalar(mat(MM, b, h), psum[:, BANK_SC + b, h * P:h * P + P],
                                          cum[:, 4 * b + h:4 * b + h + 1], 0.0, ALU.subtract, ALU.min)
                ins.then_inc(S["e_diff"], 1)
            for b in range(NB):
                if q.due("e_exp", b + 1):
                    dve.wait_ge(S["e_exp"], b + 1)
                v.tensor_tensor(heads(tl(attn, b, 512)), heads(tl(MM, b, 512)), over_heads(C("le")), ALU.mult)\
                    .then_inc(S["dve_step"], q.one("dve_step"))
                dve.wait_ge(S["dve_step"], q.sent["dve_step"])
                v.tensor_tensor(heads(tl(AT, b, 512)), heads(tl(attn, b, 512)), over_heads(C("lt")), ALU.mult)\
                    .then_inc(S["dve_step"], q.one("dve_step"))
                dve.wait_ge(S["dve_step"], q.sent["dve_step"])
                v.tensor_tensor(tl(AT, b, 512), tl(AT, b, 512), psum[:, BANK_T + b, :], ALU.mult)\
                    .then_inc(S["e_masks"], q.one("e_masks"))

            def row_rs(mean, count):
                if q.due("d_sum", count):
                    dve.wait_ge(S["d_sum"], count)
                v.tensor_scalar(N_VAR, psum[0:8, BANK_O, 0:T], mean, EPS2, ALU.mult, ALU.add).then_inc(S["e_var"], 1)
                dve.wait_ge(S["e_guess"], q.next("e_guess"))
                newton(N_VAR, N_GUESS, N_TMP, N_RS, "dve_step")
                dve.wait_ge(S["dve_step"], q.sent["dve_step"])

            row_rs(1.0, 8)
            v.tensor_scalar(N_RS[0:GH, :], N_RS[0:GH, :], P ** -0.5, None, ALU.mult).then_inc(S["e_rs"], 1)
            if q.due("d_spread", 1):
                dve.wait_ge(S["d_spread"], 1)
            for i in range(4):
                v.tensor_tensor(tl(qkv, i, 512), tl(qkv, i, 512), psum[:, BANK_SC + i, :], ALU.mult)\
                    .then_inc(S["e_qk"], q.one("e_qk"))
            if q.due("d_turned", 1):
                dve.wait_ge(S["d_turned"], 1)
            if q.due("e_edec", 1):
                dve.wait_ge(S["e_edec"], 1)
            for h in range(GH):
                ins = v.tensor_scalar(tl(k_dec, h, P), psum[:, BANK_O, h * P:h * P + P], edec[:, h:h + 1], None, ALU.mult)
            ins.then_inc(S["e_kdec"], 1)
            if q.due("e_vtok", 1):
                dve.wait_ge(S["e_vtok"], 1)
            for h in range(GH):
                ins = v.tensor_scalar(tl(r_tok, h, P), tl(v_tk, h, P), beta[:, h:h + 1], None, ALU.mult)
            ins.then_inc(S["e_r"], 1)
            if q.due("e_erow", 1):
                dve.wait_ge(S["e_erow"], 1)
            dve.wait_ge(S["e_qk"], q.sent["e_qk"])
            v.tensor_tensor(heads(q_dec), heads(qkv[:, 0:4 * T], T)[:, :, P:T], heads(state), ALU.mult)\
                .then_inc(S["e_qdec"], 1)
            for b in range(NB):
                if q.due("d_kk", b + 1):
                    dve.wait_ge(S["d_kk"], b + 1)
                dve.wait_ge(S["e_masks"], q.sent["e_masks"])
                v.tensor_tensor(tl(AT, b, 512), tl(AT, b, 512), psum[:, BANK_T, :], ALU.mult)\
                    .then_inc(S["dve_step"], q.one("dve_step"))
                v.tensor_tensor(tl(attn, b, 512), tl(attn, b, 512), psum[:, BANK_T + 1, :], ALU.mult)\
                    .then_inc(S["e_at"], q.one("e_at"))
                dve.wait_ge(S["e_at"], q.sent["e_at"])
                v.tensor_tensor(heads(tl(XT, b, 512)), heads(tl(AT, b, 512)), over_heads(C("neg_level0")), ALU.mult)\
                    .then_inc(S["dve_step"], q.one("dve_step"))
                dve.wait_ge(S["dve_step"], q.sent["dve_step"])
                v.tensor_tensor(heads(tl(XT, b, 512)), heads(tl(XT, b, 512)), over_heads(C("ident")), ALU.add)\
                    .then_inc(S["e_xt0"], 1)
            for lv in range(1, LEVELS):
                for b in range(NB):
                    dve.wait_ge(S["d_ax"], q.next("d_ax"))
                    v.tensor_tensor(heads(tl(MM, b, 512)), heads(psum[:, BANK_SC + b, :]),
                                           over_heads(C(f"neg_level{lv}")), ALU.mult).then_inc(S["e_mm"], 1)
            if q.due("e_ecum", 1):
                dve.wait_ge(S["e_ecum"], 1)
            v.tensor_scalar(ecum, ecum, -1.0, None, ALU.mult).then_inc(S["dve_step"], q.one("dve_step"))
            dve.wait_ge(S["dve_step"], q.sent["dve_step"])
            if q.due("d_pred", 1):
                dve.wait_ge(S["d_pred"], 1)
            for h in range(GH):
                ins = stt(tl(r_tok, h, P), psum[:, BANK_T, h * P:h * P + P], ecum[:, h:h + 1], tl(v_tk, GH + h, P),
                          ALU.mult, ALU.add)
            ins.then_inc(S["dve_step"], q.one("dve_step"))
            dve.wait_ge(S["dve_step"], q.sent["dve_step"])
            for h in range(GH):
                ins = v.tensor_scalar(tl(r_tok, h, P), tl(r_tok, h, P), beta[:, 4 + h:5 + h], None, ALU.mult)
            ins.then_inc(S["e_r"], 1)
            if q.due("d_out", 1):
                dve.wait_ge(S["d_out"], 1)
            if q.due("z_silu", 4):
                dve.wait_ge(S["z_silu"], 4)
            if q.due("e_osq", GH):
                dve.wait_ge(S["e_osq"], GH)
            for h in range(GH):
                stt(tl(z_t, h), psum[:, BANK_T + h // 2, (h % 2) * T:(h % 2) * T + T], col("gdn_norm"), tl(z_t, h),
                           ALU.mult, ALU.mult).then_inc(S["e_og"], q.one("e_og"))
            row_rs(1.0 / P, 8 + GH)
            v.tensor_copy(N_RS, N_RS).then_inc(S["e_rs"], 1)
            if q.due("d_spread", 2):
                dve.wait_ge(S["d_spread"], 2)
            dve.wait_ge(S["e_og"], q.sent["e_og"])
            for h in range(GH):
                v.tensor_tensor(tl(z_t, h), tl(z_t, h), psum[:, BANK_SC + h // 2, (h % 2) * T:(h % 2) * T + T],
                                       ALU.mult).then_inc(S["e_h"], q.one("e_h"))
                dve.wait_ge(S["e_h"], q.sent["e_h"])
            for h in range(GH):
                hid_low(h, tl(z_t, h))
            dve.wait_ge(S["lg_tile"], q.sent["lg_tile"])
            v.tensor_tensor(l_scan, lru_g, lru_g, ALU.mult).then_inc(S["dve_step"], q.one("dve_step"))
            dve.wait_ge(S["dve_step"], q.sent["dve_step"])
            v.tensor_scalar(l_scan, l_scan, 0.044715, 1.0, ALU.mult, ALU.add)\
                .then_inc(S["dve_step"], q.one("dve_step"))
            dve.wait_ge(S["dve_step"], q.sent["dve_step"])
            v.tensor_tensor(l_scan, l_scan, lru_g, ALU.mult).then_inc(S["l_cubic"], 1)
            if q.due("l_decay", LT):
                dve.wait_ge(S["l_decay"], LT)
            if q.due("l_tanh", LT):
                dve.wait_ge(S["l_tanh"], LT)
            v.tensor_tensor(l_r, l_a, l_a, ALU.mult).then_inc(S["dve_step"], q.one("dve_step"))
            dve.wait_ge(S["dve_step"], q.sent["dve_step"])
            stt(l_t, l_r, 1.0, l_t, ALU.add, ALU.mult).then_inc(S["l_minus"], 1)
            dve.wait_ge(S["c_conv"], q.sent["c_conv"])
            v.tensor_tensor(l_i, l_i, lru_x, ALU.mult).then_inc(S["dve_step"], q.one("dve_step"))
            dve.wait_ge(S["dve_step"], q.sent["dve_step"])
            if q.due("l_root", 1):
                dve.wait_ge(S["l_root"], 1)
            v.tensor_tensor(l_i, l_i, l_t, ALU.mult).then_inc(S["dve_step"], q.one("dve_step"))
            dve.wait_ge(S["dve_step"], q.sent["dve_step"])
            for t in range(LT):
                v.tensor_tensor_scan(tl(l_r, t), tl(l_a, t), tl(l_i, t), 0.0, ALU.mult, ALU.add)\
                    .then_inc(S["dve_step"], q.one("dve_step"))
            dve.wait_ge(S["dve_step"], q.sent["dve_step"])
            if q.due("l_gelu", 1):
                dve.wait_ge(S["l_gelu"], 1)
            stt(l_scan, l_scan, 1.0, lru_g, ALU.add, ALU.mult).then_inc(S["dve_step"], q.one("dve_step"))
            dve.wait_ge(S["dve_step"], q.sent["dve_step"])
            for t in range(LT):
                stt(tl(l_hid, t), tl(l_scan, t), 0.5, tl(l_r, t), ALU.mult, ALU.mult).then_inc(S["l_h"], q.one("l_h"))
                dve.wait_ge(S["l_h"], q.sent["l_h"])
            for t in range(LT):
                hid_low(GH + t, tl(l_hid, t))
            x_stage(plan.stages[(2, "out")], lambda m: col("norm_mlp", m))
            stats += KD
            norm(stats, EPS2)
            for half, (f0, n) in enumerate(PARTS2):
                for s in plan.stages[(2, "up", half)]:
                    for j, t in enumerate(s.tiles):
                        i = f0 + 2 * s.index + j
                        if q.due("main_tile", t + 1):
                            dve.wait_ge(S["main_tile"], t + 1)
                        if q.due("r_square", i - 3):
                            dve.wait_ge(S["r_square"], i - 3)
                        stt(tl(y_conv, i % 4), psum[:, t % RING, 0:T], 0.0, RSTD, ALU.max, ALU.mult)\
                            .then_inc(S["r_tile"], 1)
                    for j in range(2):
                        i = 2 * s.index + j
                        hid_low(i, tl(h32, (f0 + i) % 4))
                    split(s.n + SLOTS)
                x_stage(plan.stages[(2, "down", half)], None)
            stats += KD
            norm(stats, EPS2)
            take_rtok(DEPTH + 2)
            if q.due("load_rows", 16):
                dve.wait_ge(S["load_rows"], 16)
            for n in range(2 * NB):
                b, half = n // 2, n % 2
                if q.due("y_turned", n + 1):
                    dve.wait_ge(S["y_turned"], n + 1)
                stt(tl(y_out, n, 512), psum[:, BANK_SC + n % 2, :], rtok[:, b:b + 1], tl(gain_rows, half, 512),
                           ALU.mult, ALU.mult).then_inc(S["y_tile"], 1)

        @block.gpsimd
        def _(pool):
            q = Count()
            g = nc.gpsimd
            for l in range(DEPTH):
                for r in range(12):
                    pool.wait_ge(S["q_sin"], q.next("q_sin"))
                    if q.due("q_cos", 12 * l + r + 1):
                        pool.wait_ge(S["q_cos"], 12 * l + r + 1)
                    g.tensor_tensor(tl(qk, r), tl(qk, r), tl(rope_tmp, r % 2), ALU.add).then_inc(S["q_tile"], 1)
                for m in range(KD):
                    pool.wait_ge(S["yb_gated"], q.next("yb_gated"))
                    if q.due("hid_lo", MIX_BASE[l] + m - 1):
                        pool.wait_ge(S["hid_lo"], MIX_BASE[l] + m - 1)
                    g.tensor_tensor(tl(mix32, m % 2), tl(mixA, m % 2), tl(mixB, m % 2), ALU.add)\
                        .then_inc(S["mixed"], 1)
                for i in range(FF_TILES):
                    pool.wait_ge(S["a_silu"], q.next("a_silu"))
                    if q.due("h_tile", FF_TILES * l + i - 3):
                        pool.wait_ge(S["h_tile"], FF_TILES * l + i - 3)
                    if q.due("rstd", 2 * l + 2):
                        pool.wait_ge(S["rstd"], 2 * l + 2)
                    g.tensor_tensor(tl(s_scaled, i % 4), tl(s_silu, i % 4), RSTD, ALU.mult).then_inc(S["a_scaled"], 1)
            for i in range(FF2_TILES):
                pool.wait_ge(S["r_tile"], q.next("r_tile"))
                if q.due("hid_lo", LO_BEFORE_MLP + i - 3):
                    pool.wait_ge(S["hid_lo"], LO_BEFORE_MLP + i - 3)
                g.tensor_tensor(tl(h32, i % 4), tl(y_conv, i % 4), tl(y_conv, i % 4), ALU.mult)\
                    .then_inc(S["r_square"], 1)


VECTORS = ("norm_mix", "b_gate", "norm_ffn", "conv_w", "conv_b", "norm_final", "norm_mix_w_2", "gdn_conv_w_2",
           "gdn_A_log_2", "gdn_dt_bias_2", "gdn_norm_w_2", "lru_conv_w_2", "lru_conv_b_2", "lru_gate_a_b_2",
           "lru_gate_x_b_2", "lru_a_param_2", "norm_mlp_w_2")
DIRECT = ("x", "positions", "w_in", "w_proj_a", "w_proj_b", "w_out", "w_up", "w_down", "w_in_2", "w_out_2", "w_ff1_2",
          "w_ff2_2", "final_norm_w_2")


def kernel(**inputs):
    import concourse.bacc as bacc
    from concourse.bass_utils import run_bass_kernel_spmd

    nc = bacc.Bacc("TRN2", target_bir_lowering=False, num_devices=1)
    a = {n: np.ascontiguousarray(v) for n, v in inputs.items()}
    packed = {"consts": CONSTS, "params": params(a), "lru_blocks": lru_blocks(a)}
    arrays, aps = {}, {}
    for name in (*DIRECT, *packed):
        v = np.ascontiguousarray(packed[name] if name in packed else a[name])
        arrays[f"in_{name}"] = v
        aps[name] = nc.dram_tensor(f"in_{name}", v.shape, mybir.dt.from_np(v.dtype), kind="ExternalInput").ap()
    out = nc.dram_tensor("out", (1, T, D), F32, kind="ExternalOutput").ap()
    build(nc, aps, aps["consts"], aps["params"], aps["lru_blocks"], out)
    r = run_bass_kernel_spmd(nc, [arrays], core_ids=[0])
    return r.results[0]["out"]
```

```python
from contextlib import ExitStack

import numpy as np

import concourse.bass as bass
from concourse import mybir

F32 = mybir.dt.float32
F32R = mybir.dt.float32r
I32 = mybir.dt.int32
ACT = mybir.ActivationFunctionType
ALU = mybir.AluOpType

P = 128
T = 256
NB = T // P
D = 1024
KD = D // P
DEPTH = 2
HEAD = 64
HEADS = 4
GROUPS = 3
DILATIONS = (1, 4, 16)
WINDOWS = (128, 512, 2048)
DIL_W = GROUPS * HEADS * HEAD
SB_W = HEADS * HEAD
ROPE_THETA = 500000.0
ROPE = HEAD // 4
FF = 2816
FF_TILES = FF // P
PARTS1 = ((0, 12), (12, 10))
PARTS2 = ((0, 12), (12, 10), (22, 10))
EPS1 = 1e-5
EPS2 = 1e-6
GH = 4
LT = 4
LRU_C = 8.0
GELU_C = float(np.sqrt(2.0 / np.pi))
HALF = P // 2
LEVELS = 7
FF2_TILES = 4 * D // P
HID = 12
TICK0 = 8
SCRATCH = 14976
POOL_SLABS = {(2, "in"): (1, 3, *range(5, 13)), (2, "up", 0): (2,)}
for _l in range(DEPTH):
    POOL_SLABS.update({(_l, "in"): (2, *range(13, 20)), (_l, "proj"): (0, 1), (_l, "out"): (2,), (_l, "up", 0): (2,)})
X_TOTAL = KD * (1 + 3 * DEPTH + 2 + len(PARTS2))
PER_LAYER = 4 + KD + FF_TILES
MIX_BASE = [PER_LAYER * l + 4 for l in range(DEPTH)]
LO_BEFORE_MLP = PER_LAYER * DEPTH + KD
ROUND = 1.5 * 2 ** 23


def short(x, bits):
    m, e = np.frexp(x)
    return float(np.ldexp(np.round(m * 2 ** bits), int(e) - bits))


_A = short(2 * np.pi, 10)
_B = short(2 * np.pi - _A, 10)
TWO_PI = (_A, _B, float(2 * np.pi - _A - _B))
PI_BELOW = float(np.nextafter(np.float32(np.pi), np.float32(0)))
SLOTS = 3
SLAB = 2048
RING = 3
BANK_SC, BANK_T, BANK_O = 3, 5, 7
Y_ORDER = ((0, 0), (1, 0), (0, 1), (1, 1))
Y_BANKS = (BANK_SC, BANK_SC + 1, 0, 1)
FAR = -1e30

CONST_COLS = {}


def constants():
    p = np.arange(P)[:, None]
    c = np.arange(P)[None, :]
    parts = {}
    parts["ident"] = (p == c)
    parts["ones"] = np.ones((P, P))
    parts["neg_ge"] = -1.0 * (p >= c)
    parts["neg_ones"] = -np.ones((P, P))
    parts["le"] = (p <= c)
    parts["lt"] = (p < c)
    rot = np.zeros((P, P))
    inv = np.zeros((P, 1))
    freq = ROPE_THETA ** (-np.arange(0, ROPE, 2) / ROPE)
    for base in (0, HEAD):
        for i in range(ROPE // 2):
            rot[base + ROPE // 2 + i, base + i] = -1.0
            rot[base + i, base + ROPE // 2 + i] = 1.0
            inv[base + i] = inv[base + ROPE // 2 + i] = freq[i]
    parts["rot"] = rot
    parts["inv_freq"] = inv
    for qb in range(NB):
        keys = (qb + 1) * P
        q = qb * P + p
        k = np.arange(keys)[None, :]
        cols = [np.where((q >= k) & (q - k <= w) & ((q - k) % d == 0), 0.0, FAR) for w, d in zip(WINDOWS, DILATIONS)]
        parts[f"dil_mask{qb}"] = np.concatenate(cols, axis=1)
    strict = np.where(p < c, 0.0, FAR)
    parts["sb_mask"] = np.concatenate([strict, np.zeros((P, P)), strict], axis=1)
    for lv in range(LEVELS):
        b = 1 << lv
        below = (p // (2 * b) == c // (2 * b)) & (p // b % 2 == 1) & (c // b % 2 == 0)
        parts[f"neg_level{lv}"] = -1.0 * (below.T if lv == 0 else below[:, c[0] // b % 2 == 0])
    pick = np.zeros((P, 15))
    pick[:, 7] = 1.0
    parts["pick"] = pick
    at = 0
    for name, a in parts.items():
        CONST_COLS[name] = (at, a.shape[1])
        at += a.shape[1]
    return np.concatenate([a.astype(np.float32) for a in parts.values()], axis=1)


CONSTS = constants()
EARLY = 2 * P

PARAM_COLS = {}


def params(a):
    cols = []
    at = 0

    def put(name, rows):
        nonlocal at
        cols.append(rows)
        PARAM_COLS[name] = at
        at += rows.shape[1]

    def tiles(v):
        return np.reshape(v, (-1, P)).T

    for l in range(DEPTH):
        put(f"norm_mix{l}", tiles(a["norm_mix"][l]))
        put(f"b_gate{l}", tiles(a["b_gate"][l]))
        put(f"norm_ffn{l}", tiles(a["norm_ffn"][l]))
        put(f"conv_w{l}", tiles(a["conv_w"][l]))
        put(f"conv_b{l}", tiles(a["conv_b"][l]))
    put("norm_final", tiles(a["norm_final"]))
    put("norm_mix2", tiles(a["norm_mix_w_2"][0]))
    put("gdn_conv", tiles(a["gdn_conv_w_2"][0]))
    put("gdn_norm", tiles(a["gdn_norm_w_2"][0]))
    put("lru_conv", tiles(a["lru_conv_w_2"][0]))
    put("lru_conv_b", tiles(a["lru_conv_b_2"][0]))
    put("gate_a_b", tiles(a["lru_gate_a_b_2"][0]))
    put("gate_x_b", tiles(a["lru_gate_x_b_2"][0]))
    put("a_param", tiles(a["lru_a_param_2"][0]))
    put("norm_mlp", tiles(a["norm_mlp_w_2"][0]))
    put("A_log", np.broadcast_to(np.reshape(a["gdn_A_log_2"][0], (1, GH)), (P, GH)))
    put("dt_bias", np.broadcast_to(np.reshape(a["gdn_dt_bias_2"][0], (1, GH)), (P, GH)))
    PARAM_COLS["cols"] = at
    return np.concatenate(cols, axis=1)


def lru_blocks(a):
    out = np.zeros((P, 2, LT, P), np.float32)
    for n, name in enumerate(("lru_gate_a_w_2", "lru_gate_x_w_2")):
        for t in range(LT):
            out[:HEAD, n, t, :HEAD] = a[name][0, 2 * t]
            out[HEAD:, n, t, HEAD:] = a[name][0, 2 * t + 1]
    return np.reshape(out, (P, -1))


class Slab:
    def __init__(self, n, stage, src, chunks, cols, index):
        self.n, self.stage, self.src, self.chunks, self.cols, self.index = n, stage, src, chunks, cols, index
        self.tiles = []
        self.freed = None


class Plan:

    def __init__(self, w):
        self.slabs = []
        self.stages = {}
        self.readers = []
        self.counts = {}
        self.firsts = 0
        for l in range(DEPTH):
            win = w["w_in"][l]
            order = [("s", 3 * DIL_W), ("s", 3 * DIL_W + SB_W), ("v", 3 * DIL_W + 2 * SB_W)]
            order += [("rope", 256 * i) for i in range(6)]
            order += [("v", 2 * DIL_W + 256 * i) for i in range(3)]
            order += [("gate", 3 * DIL_W + 3 * SB_W + 256 * i) for i in range(8)]
            for kind, c in order:
                self.add((l, "in"), win[:, c:c + 256], kind)
            self.add((l, "proj"), w["w_proj_a"][l], None)
            self.add((l, "proj"), w["w_proj_b"][l], None)
            for m in range(KD):
                self.tile(self.slabs[-2], "pa")
                self.tile(self.slabs[-1], "pb")
            for c in range(4):
                self.add((l, "out"), w["w_out"][l][:, 256 * c:256 * c + 256], "x")
            for half, (f0, n) in enumerate(PARTS1):
                for j in range(n // 2):
                    c = (f0 + 2 * j) * P
                    self.add((l, "up", half), w["w_up"][l][:, c:c + 256], "fa")
                    self.add((l, "up", half), w["w_up"][l][:, FF + c:FF + c + 256], "fb")
                self.down((l, "down", half), w["w_down"][l], f0, n)
        win = w["w_in_2"][0]
        gw = 512
        order = [("conv", 256 * i) for i in (2, 3)] + [("ba", 4 * gw)] + [("conv", 256 * i) for i in (0, 1, 4, 5)]
        order += [("conv", 4 * gw + 8 + 256 * i) for i in range(2)]
        order += [("lg", 5 * gw + 8 + 256 * i) for i in range(2)]
        order += [("z", 3 * gw + 256 * i) for i in range(2)]
        for kind, c in order:
            self.add((2, "in"), win[:, c:c + (8 if kind == "ba" else 256)], kind)
        for s in self.stages[(2, "in")]:
            s.conv = {0: 4, 1: 6, 3: 0, 4: 2, 5: 8, 6: 10, 7: 12, 8: 14}.get(s.index)
        for half, r in (("lru", GH * P), ("gdn", 0)):
            for c in range(4):
                self.add((2, "out", half), w["w_out_2"][0][r:r + LT * P, 256 * c:256 * c + 256], "x")
        for half, (f0, n) in enumerate(PARTS2):
            for j in range(n // 2):
                c = (f0 + 2 * j) * P
                self.add((2, "up", half), w["w_ff1_2"][0][:, c:c + 256], "f2")
            self.down((2, "down", half), w["w_ff2_2"][0], f0, n)
        lows = {"split_lo": 0, "pool_lo": 0}
        for s in self.slabs:
            if s.tiles:
                s.freed = ("main_tile", s.tiles[-1] + 1)
            name = "pool_lo" if s.index in POOL_SLABS.get(s.stage, ()) else "split_lo"
            lows[name] += 1
            s.low = (name, lows[name])

    def add(self, stage, src, kind):
        rows, cols = src.shape
        index = len(self.stages.setdefault(stage, []))
        s = Slab(len(self.slabs), stage, src, rows // P, cols, index)
        s.kind = kind
        self.slabs.append(s)
        self.stages[stage].append(s)
        if kind:
            for _ in range(2):
                self.tile(s, kind)

    def down(self, stage, src, f0, n):
        for c in range(4):
            for piece in range(2):
                r = (f0 + piece * n // 2) * P
                self.add(stage, src[r:r + n // 2 * P, 256 * c:256 * c + 256], None)
                if piece == 0:
                    self.firsts += 1
                    self.slabs[-1].freed = ("first_piece", self.firsts)
            for _ in range(2):
                self.tile(self.slabs[-1], "x")

    READERS = {"s": ["s_tile"], "rope": ["q_raw", "q_cos"], "v": ["v_tile"], "gate": ["gate_raw"], "pa": ["ya_gated"],
               "pb": ["yb_gated"], "x": ["x_tile"], "fa": ["a_tile"], "fb": ["h_tile"], "conv": ["c_tile"],
               "ba": ["ba_tile"], "lg": ["lg_tile"], "z": ["z_tile"], "f2": ["r_tile"]}

    def tile(self, slab, kind):
        slab.tiles.append(len(self.readers))
        pairs = []
        for name in self.READERS[kind]:
            self.counts[name] = self.counts.get(name, KD if name == "x_tile" else 0) + 1
            pairs.append((name, self.counts[name]))
        self.readers.append(pairs)


class Count:

    def __init__(self):
        self.covered, self.taken, self.sent = {}, {}, {}

    def due(self, name, value):
        fresh = value > self.covered.get(name, 0)
        if fresh:
            self.covered[name] = value
        return fresh

    def next(self, name, k=1):
        self.taken[name] = self.taken.get(name, 0) + k
        return self.taken[name]

    def one(self, name):
        self.sent[name] = self.sent.get(name, 0) + 1
        return 1


SEMS = [
    "load_consts", "load_rest", "load_params", "load_x", "load_pos", "load_rows", "load_lru", "stored",
    "slab_in0", "slab_in1", "slab_in2",
    "split_hi", "split_lo", "pool_lo", "main_tile", "first_piece",
    "x_turned", "x_tile", "square", "sq_added", "xg_hi", "xg_lo", "stat_sum", "var", "rs_guess", "rstd", "rtok_sum", "rtok",
    "angle", "sine", "rope_factor", "q_raw", "q_cos", "q_turned", "q_sin", "q_tile",
    "s_tile", "v_tile", "sb_z", "sb_log", "sb_loss", "sb_exponent", "sb_min", "sb_attn", "sb_out",
    "dil_scores", "dil_masked", "dil_exp", "dil_probs", "dil_turned", "dil_pT", "dil_out",
    "hid_hi", "hid_lo",
    "gate_raw", "gate", "ya_gated", "yb_gated", "mixed",
    "a_tile", "a_tap", "a_conv", "a_silu", "a_scaled", "h_tile", "r_tile", "r_square",
    "c_tile", "c_tap", "c_conv", "c_silu", "ba_tile", "lg_tile", "z_tile", "z_silu",
    "d_cum", "d_rows", "d_sum", "d_spread", "d_turned", "d_kk", "d_x0", "d_ax", "d_x", "d_xt", "d_new", "d_state", "d_pred",
    "d_out", "e_beta", "e_rate", "e_shift", "e_log", "e_decay", "e_cum", "e_last", "e_edec", "e_ecum", "e_erow",
    "e_diff", "e_exp", "e_masked", "e_masks", "e_square", "e_var", "e_guess", "e_rs", "e_qk", "e_vtok", "e_kdec", "e_r", "e_qdec",
    "e_at", "e_xt0", "e_x", "e_mm", "e_xt", "e_new", "e_state", "e_og", "e_h",
    "l_log", "l_rate", "l_logits", "l_gates", "l_square", "l_gsquare", "l_gated", "l_decay", "l_tanh", "l_minus", "l_root", "l_cubic", "l_gelu", "l_h",
    "y_turned", "y_tile",
    "dve_step", "act_step", "pool_step",
]


def build(nc, w, consts_d, params_d, lru_d, out):
    plan = Plan(w)
    with ExitStack() as ctx:
        S = {n: ctx.enter_context(nc.semaphore(n)) for n in SEMS}

        def sb(name, cols, dt=F32):
            return ctx.enter_context(nc.sbuf_tensor("sb_" + name, [P, cols], dt))[:, :]

        raw = sb("raw", SLOTS * SLAB)
        w_hi = sb("w_hi", SLOTS * SLAB, F32R)
        w_lo = sb("w_lo", SLOTS * SLAB, F32R)
        xt = sb("xt", KD * T)
        xg_hi = sb("xg_hi", KD * T, F32R)
        xg_lo = sb("xg_lo", KD * T, F32R)
        hid_hi = sb("hid_hi", HID * T, F32R)
        hid_lo = sb("hid_lo", HID * T, F32R)
        cst = sb("consts", CONSTS.shape[1])
        par = sb("params", PARAM_COLS["cols"])
        sq = sb("sq", 4 * T)
        rs = sb("rs", 6 * T)
        cs = sb("cs", 4 * T)
        rtok = sb("rtok", NB)
        gfg2 = sb("gfg2", KD)
        small = sb("small", 128)
        scratch = sb("scratch", SCRATCH)
        psum = ctx.enter_context(nc.psum_tensor("psum", [P, 8, 512], F32))

        def C(name, a=0, b=None):
            at, n = CONST_COLS[name]
            return cst[:, at + a:at + (n if b is None else b)]

        def col(name, i=0):
            c = PARAM_COLS[name] + i
            return par[:, c:c + 1]

        class Carve:

            def __init__(self, at=0):
                self.at = at

            def __call__(self, cols):
                a = self.at
                self.at += cols
                assert self.at <= SCRATCH, self.at
                return scratch[:, a:a + cols]

        def tl(buf, i, n=T):
            return buf[:, i * n:(i + 1) * n]

        cut = Carve()
        x_in = scratch[:, 0:NB * D]
        qk = cut(12 * T)
        s_t = cut(4 * T)
        v_tok = cut(NB * 1024)
        gates = cut(16 * T)
        prob = cut(2 * 768)
        pT = cut(2 * 768)
        sb_log = cut(384)
        rope_raw, rope_tmp = gates[:, 0:2 * T], gates[:, 2 * T:4 * T]
        mixA, mixB, mix32 = prob[:, 0:2 * T], prob[:, 2 * T:4 * T], prob[:, 4 * T:6 * T]
        cut = Carve()
        AB = cut(4 * (T + 2))
        y_conv, s_silu, s_scaled, h32 = cut(4 * T), cut(4 * T), cut(4 * T), cut(4 * T)
        cut = Carve()
        qkv = cut(12 * T)
        z_t, lru_x, lru_g = cut(4 * T), cut(4 * T), cut(4 * T)
        mats = cut(4096)
        attn = cut(1024)
        v_tk = cut(1024)
        norm_rows = cut(1024)
        state = cut(512)
        cbuf = cut(4 * (T + 3))
        AT, XX, XT, MM = (tl(mats, i, 1024) for i in range(4))
        k_dec, vn0 = norm_rows[:, 0:512], norm_rows[:, 512:1024]
        r_tok, q_dec = qkv[:, 8 * T:10 * T], qkv[:, 10 * T:12 * T]
        vn1 = v_tk[:, 0:512]
        l_t = qkv[:, 0:LT * T]
        l_r, l_i, l_scan = cbuf[:, 0:LT * T], sq, lru_x
        l_a = [vn0[:, 0:T], vn0[:, T:2 * T], MM[:, 2 * T:3 * T], MM[:, 3 * T:4 * T]]
        l_w = cs
        gain_rows, y_out = scratch[:, 0:D], scratch[:, D:3 * D]

        def flat(bank, a, b):
            return psum_flat[:, bank * 512 + a:bank * 512 + b]

        psum_flat = psum[:, :, :].rearrange("p a b -> p (a b)")

        def part(buf, s):
            i = s.n % SLOTS
            return buf[:, i * SLAB:i * SLAB + s.chunks * s.cols]

        def by_chunk(buf, s):
            return part(buf, s).rearrange("p (k c) -> p k c", k=s.chunks)

        def heads(buf, n=P):
            return buf.rearrange("p (h c) -> p h c", c=n)

        def over_heads(m):
            return m.unsqueeze(1).to_broadcast([P, GH, P])

        VAR, GUESS, TMP, TMP2, RSTD, RSTD2 = (tl(rs, i) for i in range(6))
        SUMS = (TMP2, RSTD2)
        COS, SIN, COSR, SINR = (tl(cs, i) for i in range(4))
        N_VAR, N_GUESS, N_TMP, N_RS = (tl(rs, i)[0:8, :] for i in range(4))

        def sm(a, n):
            return small[:, a:a + n]

        dil_bias, dil_den, dil_rden = sm(0, 8), sm(8, 8), sm(16, 8)
        ba, beta, shift, decay, logs = sm(24, 16), sm(40, 8), sm(48, 8), sm(56, 8), sm(64, 8)
        cum, rate, edec, ecum, l_rate, l_log = sm(72, 8), sm(80, 4), sm(84, 4), sm(88, 4), sm(92, 4), sm(96, 4)
        zero_col = sm(100, 1)

        def prob_of(u):
            return tl(prob, u % 2, 768)

        def pT_of(u):
            return tl(pT, u % 2, 768)

        def loss_of(h):
            return tl(pT, h % 2, 768)[:, 0:384]

        def attn_of(h):
            return tl(prob, h % 2, 768)[:, 0:384]

        def v_head(b, i):
            return tl(v_tok, b, 1024)[:, i * HEAD:(i + 1) * HEAD]

        def mat(buf, b, h):
            return buf[:, b * 512 + h * P:b * 512 + h * P + P]

        def even(m, lv):
            return m.rearrange("p (n two c) -> p n two c", two=2, c=1 << lv)[:, :, 0, :]

        def blocks(m, lv):
            return m.rearrange("p (n c) -> p n c", c=1 << lv)

        def kept(b, h=None):
            return tl(MM, b, T) if h is None else tl(MM, b, T)[:, h * HALF:(h + 1) * HALF]

        def pair(b):
            return BANK_SC + 2 * b, BANK_SC + 2 * b + 1

        block = ctx.enter_context(nc.Block())

        @block.sync
        def _(eng):
            q = Count()
            eng.dma_start(cst[:, 0:EARLY], consts_d[:, 0:EARLY]).then_inc(S["load_consts"], 16)
            eng.dma_start(par, params_d).then_inc(S["load_params"], 16)
            eng.dma_start(x_in.rearrange("p (b d) -> p b d", b=NB),
                          w["x"][0].rearrange("(b p) d -> p b d", p=P)).then_inc(S["load_x"], 16)
            for s in plan.slabs:
                if s.n >= SLOTS:
                    name, value = plan.slabs[s.n - SLOTS].low
                    if q.due(name, value):
                        eng.wait_ge(S[name], value)
                eng.dma_start(by_chunk(raw, s), s.src.rearrange("(k p) c -> p k c", p=P))\
                    .then_inc(S[f"slab_in{s.n % SLOTS}"], 16)
                if s.n == 1:
                    eng.dma_start(COS.bitcast(I32), w["positions"].to_broadcast([P, T])).then_inc(S["load_pos"], 16)
                    eng.dma_start(cst[:, EARLY:], consts_d[:, EARLY:]).then_inc(S["load_rest"], 16)
                if s.stage == (2, "in") and s.index == 3:
                    if q.due("q_tile", 12 * DEPTH):
                        eng.wait_ge(S["q_tile"], 12 * DEPTH)
                    eng.dma_start(l_w, lru_d).then_inc(S["load_lru"], 16)
                if s.stage == (2, "up", 0) and s.index == 3:
                    if q.due("x_tile", KD + 24 * DEPTH + 2 * KD):
                        eng.wait_ge(S["x_tile"], KD + 24 * DEPTH + 2 * KD)
                    if q.due("hid_lo", LO_BEFORE_MLP):
                        eng.wait_ge(S["hid_lo"], LO_BEFORE_MLP)
                    eng.dma_start(gain_rows, w["final_norm_w_2"].unsqueeze(0).to_broadcast([P, D]))\
                        .then_inc(S["load_rows"], 16)
            for n, (b, half) in enumerate(Y_ORDER):
                if q.due("y_tile", n + 1):
                    eng.wait_ge(S["y_tile"], n + 1)
                eng.dma_start(out[0, b * P:(b + 1) * P, half * 512:(half + 1) * 512],
                              tl(y_out, n, 512)).then_inc(S["stored"], 16)
            eng.wait_ge(S["stored"], 16 * len(Y_ORDER))

        @block.tensor
        def _(pe):
            q = Count()

            def mul(ps, lhsT, rhs, start=True, stop=True):
                return nc.tensor.matmul(ps, lhsT, rhs, start=start, stop=stop, skip_group_check=True)

            def main_tile(s, t, j, act, base, k0=0, first=True, last=True):
                if first and t >= RING:
                    for name, value in plan.readers[t - RING]:
                        if q.due(name, value):
                            pe.wait_ge(S[name], value)
                name, value = s.low
                if q.due(name, value):
                    pe.wait_ge(S[name], value)
                hi, lo = by_chunk(w_hi, s), by_chunk(w_lo, s)
                c = slice(j * P, j * P + P)
                for k in range(s.chunks):
                    if q.due(act[2], base + k0 + k + 1):
                        pe.wait_ge(S[act[2]], base + k0 + k + 1)
                    ah, al = tl(act[0], k0 + k), tl(act[1], k0 + k)
                    if s.kind in ("v", "ba"):
                        ps = psum[:, t % RING, 0:s.cols]
                        trio = [(ah[:, c], hi[:, k, :]), (al[:, c], hi[:, k, :]), (ah[:, c], lo[:, k, :])]
                    else:
                        ps = psum[:, t % RING, 0:T]
                        trio = [(hi[:, k, c], ah), (hi[:, k, c], al), (lo[:, k, c], ah)]
                    for i, (a, b) in enumerate(trio):
                        mm = mul(ps, a, b, first and k == 0 and i == 0, last and k == s.chunks - 1 and i == 2)
                if last:
                    mm.then_inc(S["main_tile"], 1)
                return mm

            def slab_two(s, act, base, between):
                for j, t in enumerate(s.tiles):
                    main_tile(s, t, j, act, base)
                    between(2 * s.index + j)

            def down(stage, base, n):
                for s in plan.stages[stage]:
                    last = s.index % 2 == 1
                    tiles = s.tiles if last else plan.slabs[s.n + 1].tiles
                    for j, t in enumerate(tiles):
                        mm = main_tile(s, t, j, hid, base, 0 if not last else n // 2, not last, last)
                    if not last:
                        mm.then_inc(S["first_piece"], 1)

            def stat(two=False):
                kinds = 2 if two else 1
                pe.wait_ge(S["sq_added"], q.next("sq_added", (KD - 2) * kinds))
                for n in range(kinds):
                    mul(psum[:, BANK_T + n, 0:T], C("ones"), SUMS[n], True, False).then_inc(S["stat_sum"], 1)
                pe.wait_ge(S["square"], q.next("square", KD * kinds))
                for n in range(kinds):
                    mul(psum[:, BANK_T + n, 0:T], C("ones"), tl(sq, 2 * n + 1), False, True).then_inc(S["stat_sum"], 1)

            def token_factor(n):
                if q.due("rstd", n):
                    pe.wait_ge(S["rstd"], n)
                for b in range(NB):
                    mm = mul(psum[:, BANK_T + 1, 384 + b:385 + b], RSTD[0:1, b * P:b * P + P], C("ones", 0, 1)[0:1, :])
                mm.then_inc(S["rtok_sum"], 1)

            xg = (xg_hi, xg_lo, "xg_lo")
            hid = (hid_hi, hid_lo, "hid_lo")
            xg_base = hid_base = 0

            if q.due("load_consts", 16):
                pe.wait_ge(S["load_consts"], 16)
            if q.due("load_x", 16):
                pe.wait_ge(S["load_x"], 16)
            xv = x_in.rearrange("p (b d) -> p b d", b=NB)
            for m in range(KD):
                if q.due("x_tile", m - 3):
                    pe.wait_ge(S["x_tile"], m - 3)
                for b in range(NB):
                    mm = nc.tensor.transpose(psum[:, BANK_SC + m % 4, b * P:b * P + P], xv[:, b, m * P:m * P + P], C("ident"))
                mm.then_inc(S["x_turned"], 1)
            if q.due("load_rest", 16):
                pe.wait_ge(S["load_rest"], 16)

            for l in range(DEPTH):
                def turn_q(r):
                    if q.due("rtok", l + 1):
                        pe.wait_ge(S["rtok"], l + 1)
                    if q.due("q_raw", 12 * l + r + 1):
                        pe.wait_ge(S["q_raw"], 12 * l + r + 1)
                    if q.due("q_sin", 12 * l + r - 1):
                        pe.wait_ge(S["q_sin"], 12 * l + r - 1)
                    mul(psum[:, BANK_T + r % 2, 0:T], C("rot"), tl(rope_raw, r % 2)).then_inc(S["q_turned"], 1)

                def sb_a(h):
                    if q.due("s_tile", 4 * (l + 1)):
                        pe.wait_ge(S["s_tile"], 4 * (l + 1))
                    if q.due("sb_min", 4 * l + h - 1):
                        pe.wait_ge(S["sb_min"], 4 * l + h - 1)
                    rows = slice(HEAD * (h % 2), HEAD * (h % 2) + HEAD)
                    ps = psum[:, BANK_SC + h % 2, :]
                    qh, kh = tl(s_t, h // 2)[rows, :], tl(s_t, 2 + h // 2)[rows, :]
                    mul(ps[:, 0:T], kh[:, 0:P], qh, True, False)
                    mul(ps[:, T:T + P], kh[:, P:T], qh[:, P:T], False, False).then_inc(S["sb_z"], 1)

                def sb_b(h):
                    if q.due("sb_loss", 4 * l + h + 1):
                        pe.wait_ge(S["sb_loss"], 4 * l + h + 1)
                    ps = psum[:, BANK_SC + h % 2, :]
                    loss = loss_of(h)
                    mul(ps[:, 0:T], C("neg_ge"), loss[:, 0:T], False, False)
                    mul(ps[:, P:T], C("neg_ones"), loss[:, T:T + P], False, False)
                    mul(ps[:, T:T + P], C("neg_ge"), loss[:, T:T + P], False, True).then_inc(S["sb_exponent"], 1)

                def sb_c(h):
                    if q.due("sb_attn", 4 * l + h + 1):
                        pe.wait_ge(S["sb_attn"], 4 * l + h + 1)
                    if q.due("v_tile", 8 * l + 2):
                        pe.wait_ge(S["v_tile"], 8 * l + 2)
                    o = psum[HEAD * (h % 2):HEAD * (h % 2) + HEAD, BANK_O, :]
                    at = attn_of(h)
                    c = T * (h // 2)
                    mul(o[:, c:c + T], v_head(0, GROUPS * HEADS + h), at[:, 0:T], True, False)
                    mul(o[:, c + P:c + T], v_head(1, GROUPS * HEADS + h), at[:, T:T + P], False, True)\
                        .then_inc(S["sb_out"], 1)

                def dil_a(u):
                    h, qb = u // 2, u % 2
                    keys = (qb + 1) * P
                    if q.due("q_tile", 12 * (l + 1)):
                        pe.wait_ge(S["q_tile"], 12 * (l + 1))
                    if q.due("sb_min", 4 * (l + 1)):
                        pe.wait_ge(S["sb_min"], 4 * (l + 1))
                    if q.due("dil_masked", 8 * l + u):
                        pe.wait_ge(S["dil_masked"], 8 * l + u)
                    rows = slice(HEAD * (h % 2), HEAD * (h % 2) + HEAD)
                    for g in range(GROUPS):
                        tile = (g * HEADS + h) // 2
                        mm = mul(flat(BANK_SC, g * keys, g * keys + keys),
                                 tl(qk, tile)[rows, qb * P:qb * P + P], tl(qk, 6 + tile)[rows, 0:keys])
                    mm.then_inc(S["dil_scores"], 1)

                def dil_b(u):
                    if q.due("dil_probs", 8 * l + u + 1):
                        pe.wait_ge(S["dil_probs"], 8 * l + u + 1)
                    if q.due("dil_pT", 8 * l + u):
                        pe.wait_ge(S["dil_pT"], 8 * l + u)
                    if q.due("q_sin", 12 * (l + 1)):
                        pe.wait_ge(S["q_sin"], 12 * (l + 1))
                    for i in range(GROUPS * (u % 2 + 1)):
                        mm = nc.tensor.transpose(flat(BANK_T, i * P, i * P + P), prob_of(u)[:, i * P:i * P + P], C("ident"))
                    mm.then_inc(S["dil_turned"], 1)

                def dil_c(u):
                    h, qb = u // 2, u % 2
                    if q.due("dil_pT", 8 * l + u + 1):
                        pe.wait_ge(S["dil_pT"], 8 * l + u + 1)
                    if q.due("v_tile", 8 * (l + 1)):
                        pe.wait_ge(S["v_tile"], 8 * (l + 1))
                    if q.due("hid_lo", hid_base + 2):
                        pe.wait_ge(S["hid_lo"], hid_base + 2)
                    n = GROUPS * (qb + 1)
                    c = T * (h // 2) + qb * P
                    o = psum[HEAD * (h % 2):HEAD * (h % 2) + HEAD, BANK_O, c:c + P]
                    for i in range(n):
                        g, kb = i // (qb + 1), i % (qb + 1)
                        mm = mul(o, v_head(kb, g * HEADS + h), pT_of(u)[:, i * P:i * P + P], i == 0, i == n - 1)
                    mm.then_inc(S["dil_out"], 1)

                for s in plan.stages[(l, "in")]:
                    tick = s.index - TICK0
                    if tick >= 2:
                        sb_c(tick - 2) if tick < 6 else dil_c(tick - 6)
                    if tick >= 1:
                        sb_b(tick - 1) if tick < 5 else dil_b(tick - 5)
                    if tick >= 0:
                        sb_a(tick) if tick < 4 else dil_a(tick - 4)

                    def between(i):
                        if i == 0:
                            stat()
                        if i == 3:
                            token_factor(2 * l + 1)
                        if 0 <= i - 7 < 12:
                            turn_q(i - 7)

                    slab_two(s, xg, xg_base, between)
                dil_c(6)
                dil_b(7)
                dil_c(7)
                xg_base += KD
                sa, sbr = plan.stages[(l, "proj")]
                for m in range(KD):
                    main_tile(sa, sa.tiles[m], m, (hid_hi[:, 10 * T:], hid_lo[:, 10 * T:], "hid_lo"), hid_base + 2)
                    main_tile(sbr, sbr.tiles[m], m, (hid_hi[:, 8 * T:], hid_lo[:, 8 * T:], "hid_lo"), hid_base)
                hid_base += 4
                for s in plan.stages[(l, "out")]:
                    slab_two(s, hid, hid_base, lambda i: None)
                hid_base += KD
                for half, (f0, n) in enumerate(PARTS1):
                    for s in plan.stages[(l, "up", half)]:
                        slab_two(s, xg, xg_base, lambda i: stat() if i == half == 0 else None)
                    down((l, "down", half), hid_base, n)
                    hid_base += n
                xg_base += KD

            def wide(buf, i):
                return buf[:, i:i + 1].to_broadcast([buf.shape[0], P])

            def each_head(bank, lhsT, rhs):
                for h in range(GH):
                    mm = mul(psum[:, bank, h * P:h * P + P], lhsT(h), rhs(h))
                return mm

            def turn_heads(bank, src):
                for h in range(GH):
                    mm = nc.tensor.transpose(psum[:, bank, h * P:h * P + P], src(h), C("ident"))
                return mm

            def decay_rows():
                if q.due("e_decay", 1):
                    pe.wait_ge(S["e_decay"], 1)
                for b in range(NB):
                    mm = mul(psum[:, BANK_O, 4 * b:4 * b + 4], C("le"), decay[:, 4 * b:4 * b + 4])
                mm.then_inc(S["d_cum"], 1)
                if q.due("e_beta", 1):
                    pe.wait_ge(S["e_beta"], 1)
                for b in range(NB):
                    each_head(BANK_SC + b, lambda h: wide(decay, 4 * b + h), lambda h: C("le"))
                for b in range(NB):
                    mm = each_head(BANK_T + b, lambda h: wide(beta, 4 * b + h), lambda h: C("ident"))
                mm.then_inc(S["d_rows"], 1)

            def norm_sums(first, read):
                name, value = read
                if q.due(name, value):
                    pe.wait_ge(S[name], value)
                for c in range(4):
                    if q.due("e_square", first + c + 1):
                        pe.wait_ge(S["e_square"], first + c + 1)
                    mul(psum[0:8, BANK_O, 0:T], C("pick", 7 - c, 15 - c), tl(sq, c), c == 0, c == 3)\
                        .then_inc(S["d_sum"], 1)

            def spread(bank, rows):
                for n, c in enumerate(rows):
                    mm = mul(psum[:, bank, n * T:n * T + T], wide(C("ident")[0:8, :], c), N_RS)
                return mm

            def spread_k():
                if q.due("e_rs", 1):
                    pe.wait_ge(S["e_rs"], 1)
                if q.due("e_diff", 2):
                    pe.wait_ge(S["e_diff"], 2)
                if q.due("e_last", 1):
                    pe.wait_ge(S["e_last"], 1)
                spread(BANK_SC, (0, 1))
                spread(BANK_SC + 1, (2, 3)).then_inc(S["d_spread"], 1)

            def products_k():
                if q.due("e_qk", 2):
                    pe.wait_ge(S["e_qk"], 2)
                if q.due("e_masks", 2):
                    pe.wait_ge(S["e_masks"], 2)
                for b in range(NB):
                    k_of = lambda h: tl(qkv, 4 + h)[:, b * P:b * P + P]
                    each_head(pair(b)[0], k_of, k_of).then_inc(S["d_kk"], 1)
                turn_heads(BANK_O, lambda h: tl(qkv, 4 + h)[:, 0:P]).then_inc(S["d_turned"], 1)

            def first_x():
                for b in range(NB):
                    if q.due("e_xt0", b + 1):
                        pe.wait_ge(S["e_xt0"], b + 1)
                    turn_heads(pair(b)[0], lambda h: mat(XT, b, h)).then_inc(S["d_x0"], 1)

            def level_ax(lv):
                for b in range(NB):
                    if q.due("e_x", 2 * (lv - 1) + b + 1):
                        pe.wait_ge(S["e_x"], 2 * (lv - 1) + b + 1)
                    for h in range(GH):
                        mm = mul(blocks(psum[:, pair(b)[0], h * HALF:(h + 1) * HALF], lv), mat(AT, b, h),
                                 even(mat(XX, b, h), lv))
                    mm.then_inc(S["d_ax"], 1)

            def level_x(lv):
                for b in range(NB):
                    if q.due("e_mm", 2 * (lv - 1) + b + 1):
                        pe.wait_ge(S["e_mm"], 2 * (lv - 1) + b + 1)
                    if lv > 1 and q.due("e_xt", 2 * (lv - 2) + b + 1):
                        pe.wait_ge(S["e_xt"], 2 * (lv - 2) + b + 1)
                    for h in range(GH):
                        mm = mul(psum[:, pair(b)[1], h * HALF:(h + 1) * HALF], mat(XT, b, h), kept(b, h))
                    mm.then_inc(S["d_x"], 1)

            def turn_x(lv):
                for b in range(NB):
                    if q.due("e_x", 2 * lv + b + 1):
                        pe.wait_ge(S["e_x"], 2 * lv + b + 1)
                    turn_heads(pair(b)[1], lambda h: mat(XX, b, h)).then_inc(S["d_xt"], 1)

            def spread_q(n):
                if q.due("e_rs", 2):
                    pe.wait_ge(S["e_rs"], 2)
                if n and q.due("e_qk", 3):
                    pe.wait_ge(S["e_qk"], 3)
                spread(BANK_O, (2 * n, 2 * n + 1)).then_inc(S["d_spread"], 1)

            def products_q(b):
                if q.due("e_qk", 4):
                    pe.wait_ge(S["e_qk"], 4)
                if b and q.due("e_at", NB + b):
                    pe.wait_ge(S["e_at"], NB + b)
                each_head(BANK_O, lambda h: tl(qkv, 4 + h)[:, b * P:b * P + P],
                          lambda h: tl(qkv, h)[:, b * P:b * P + P]).then_inc(S["d_kk"], 1)

            def turn_v(b):
                if q.due("c_silu", 12):
                    pe.wait_ge(S["c_silu"], 12)
                if q.due("e_at", 2 * NB):
                    pe.wait_ge(S["e_at"], 2 * NB)
                if b and q.due("e_vtok", 1):
                    pe.wait_ge(S["e_vtok"], 1)
                turn_heads(BANK_O, lambda h: tl(qkv, 8 + h)[:, b * P:b * P + P]).then_inc(S["d_turned"], 1)

            def gate_logits(i):
                if q.due("load_lru", 16):
                    pe.wait_ge(S["load_lru"], 16)
                if q.due("c_conv", 16):
                    pe.wait_ge(S["c_conv"], 16)
                if q.due("e_vtok", 2):
                    pe.wait_ge(S["e_vtok"], 2)
                if i and q.due("l_gates", 2 * i):
                    pe.wait_ge(S["l_gates"], 2 * i)
                for n in range(2):
                    mm = mul(psum[:, BANK_O, n * T:n * T + T], tl(l_w, 2 * i + n, P), tl(lru_x, 2 * (i % 2) + n))
                mm.then_inc(S["l_logits"], 1)

            for s in plan.stages[(2, "in")]:
                def between(i):
                    if i == 0:
                        stat(True)
                    if i == 3:
                        token_factor(5)
                    if i == 6:
                        decay_rows()
                    if i == 7:
                        norm_sums(0, ("e_cum", 1))
                    if i == 9:
                        spread_k()
                    if i == 10:
                        products_k()
                    if i == 11:
                        norm_sums(4, ("e_kdec", 1))
                    if i == 12:
                        first_x()
                    if i == 20:
                        gate_logits(1)
                    if i >= 15 and i % 2 == 1:
                        turn_x((i - 13) // 2)
                    if 13 <= i < 25:
                        level_x((i - 12) // 2) if i % 2 == 0 else level_ax((i - 11) // 2)
                    if i in (13, 14):
                        spread_q(i - 13)
                    if i in (15, 16):
                        products_q(i - 15)
                    if i in (17, 18):
                        turn_v(i - 17)
                    if i in (19, 20, 21):
                        gate_logits((0, 2, 3)[i - 19])

                slab_two(s, xg, xg_base, between)
            xg_base += KD
            last = 2 * (LEVELS - 1)

            def new_first():
                if q.due("e_xt", last - 1):
                    pe.wait_ge(S["e_xt"], last - 1)
                if q.due("e_r", 1):
                    pe.wait_ge(S["e_r"], 1)
                each_head(BANK_SC, lambda h: mat(XT, 0, h), lambda h: tl(r_tok, h, P)).then_inc(S["d_new"], 1)

            def state_behind():
                if q.due("e_new", 1):
                    pe.wait_ge(S["e_new"], 1)
                if q.due("e_kdec", 1):
                    pe.wait_ge(S["e_kdec"], 1)
                each_head(BANK_SC + 1, lambda h: tl(k_dec, h, P), lambda h: tl(vn0, h, P)).then_inc(S["d_state"], 1)

            def predicted():
                if q.due("e_state", 1):
                    pe.wait_ge(S["e_state"], 1)
                if q.due("e_xt", last):
                    pe.wait_ge(S["e_xt"], last)
                each_head(BANK_T, lambda h: tl(qkv, 4 + h)[:, P:T], lambda h: tl(state, h, P)).then_inc(S["d_pred"], 1)

            def new_second():
                if q.due("e_r", 2):
                    pe.wait_ge(S["e_r"], 2)
                each_head(BANK_SC, lambda h: mat(XT, 1, h), lambda h: tl(r_tok, h, P)).then_inc(S["d_new"], 1)

            def rule_out():
                if q.due("e_new", 2):
                    pe.wait_ge(S["e_new"], 2)
                if q.due("e_qdec", 1):
                    pe.wait_ge(S["e_qdec"], 1)
                for h in range(GH):
                    o = psum[:, BANK_T + h // 2, (h % 2) * T:(h % 2) * T + T]
                    mul(o[:, 0:P], tl(vn0, h, P), mat(attn, 0, h))
                    mul(o[:, P:T], tl(vn1, h, P), mat(attn, 1, h), True, False)
                    mm = mul(o[:, P:T], tl(state, h, P), tl(q_dec, h, P), False, True)
                mm.then_inc(S["d_out"], 1)

            def spread_out():
                if q.due("e_rs", 3):
                    pe.wait_ge(S["e_rs"], 3)
                spread(BANK_SC, (0, 1))
                spread(BANK_SC + 1, (2, 3)).then_inc(S["d_spread"], 1)

            new_first()
            for s in plan.stages[(2, "out", "lru")]:
                def between(i):
                    if i == 0:
                        state_behind()
                    if i == 1:
                        predicted()
                    if i == 3:
                        new_second()
                    if i == 4:
                        rule_out()
                    if i == 5:
                        norm_sums(8, ("l_gates", 8))
                    if i == 7:
                        spread_out()

                slab_two(s, (hid_hi[:, GH * T:], hid_lo[:, GH * T:], "hid_lo"), hid_base, between)
            hid_base += LT
            for s in plan.stages[(2, "out", "gdn")]:
                slab_two(s, hid, hid_base, lambda i: None)
            hid_base += GH
            for half, (f0, n) in enumerate(PARTS2):
                for s in plan.stages[(2, "up", half)]:
                    slab_two(s, xg, xg_base, lambda i: stat() if i == half == 0 else None)
                down((2, "down", half), hid_base, n)
                hid_base += n
            for n, (b, half) in enumerate(Y_ORDER):
                if q.due("x_tile", X_TOTAL - 4 * (1 - half)):
                    pe.wait_ge(S["x_tile"], X_TOTAL - 4 * (1 - half))
                if n == 2:
                    stat()
                for i in range(4):
                    mm = nc.tensor.transpose(psum[:, Y_BANKS[n], i * P:i * P + P],
                                             tl(xt, 4 * half + i)[:, b * P:b * P + P], C("ident"))
                mm.then_inc(S["y_turned"], 1)
            token_factor(7)

        @block.scalar
        def _(act):
            q = Count()
            LOGEXP = "natural_log_exp_and_others"

            def f(out_, in_, func, **kw):
                return nc.scalar.activation(out_, in_, func, **kw)

            def split(n):
                if n >= len(plan.slabs):
                    return
                s = plan.slabs[n]
                if q.due(f"slab_in{n % SLOTS}", 16 * (n // SLOTS + 1)):
                    act.wait_ge(S[f"slab_in{n % SLOTS}"], 16 * (n // SLOTS + 1))
                if n >= SLOTS:
                    name, value = plan.slabs[n - SLOTS].freed
                    if q.due(name, value):
                        act.wait_ge(S[name], value)
                f(part(w_hi, s), part(raw, s), ACT.Copy).then_inc(S["split_hi"], 1)

            def split_behind(s, slabs):
                if s.index == slabs - 1:
                    split(s.n - 1 + SLOTS)
                if s.index != slabs - 2:
                    split(s.n + SLOTS)

            def square_room(m, kinds=1, n=0):
                adds, sums = kinds * (KD - 2), 2 * kinds
                if m == 0:
                    if q.due("sq_added", q.taken.get("sq_added", 0)):
                        act.wait_ge(S["sq_added"], q.taken["sq_added"])
                    if q.due("stat_sum", q.taken.get("stat_sum", 0)):
                        act.wait_ge(S["stat_sum"], q.taken["stat_sum"])
                    if n == kinds - 1:
                        q.next("sq_added", adds)
                        q.next("stat_sum", sums)
                if m >= 2:
                    if q.due("sq_added", q.taken["sq_added"] - adds + kinds * (max(m - 2, 1) - 1) + n + 1):
                        act.wait_ge(S["sq_added"], q.taken["sq_added"] - adds + kinds * (max(m - 2, 1) - 1) + n + 1)

            def prep(m, gain, square_gain=None):
                act.wait_ge(S["x_tile"], q.next("x_tile"))
                for n in range(2 if square_gain else 1):
                    square_room(m, 2 if square_gain else 1, n)
                    kw = {} if n == 0 else {"scale": square_gain(m)}
                    f(tl(sq, 2 * n + m % 2), tl(xt, m), ACT.Square, **kw).then_inc(S["square"], 1)
                f(tl(xg_hi, m), tl(xt, m), ACT.Copy, scale=gain(m)).then_inc(S["xg_hi"], 1)

            def guess():
                act.preload_act_table_set(LOGEXP)
                act.wait_ge(S["var"], q.next("var"))
                f(GUESS, VAR, ACT.Ln).then_inc(S["act_step"], q.one("act_step"))
                act.wait_ge(S["act_step"], q.sent["act_step"])
                f(GUESS, GUESS, ACT.Exp, scale=-0.5).then_inc(S["rs_guess"], 1)

            def hid_high(i, src):
                f(tl(hid_hi, i), src, ACT.Copy).then_inc(S["hid_hi"], 1)

            act.preload_act_table_set(LOGEXP)
            if q.due("load_params", 16):
                act.wait_ge(S["load_params"], 16)
            for m in range(KD):
                if m == 4:
                    split(0)
                prep(m, lambda m: col("norm_mix0", m))
            split(1)
            split(2)

            for l in range(DEPTH):
                guess()
                slabs = plan.stages[(l, "in")]
                for s in slabs:
                    tick = s.index - TICK0

                    def sb_tick(h):
                        if h:
                            sb_weights(h - 1)
                        if q.due("sb_z", 4 * l + h + 1):
                            act.wait_ge(S["sb_z"], 4 * l + h + 1)
                        if q.due("sb_loss", 4 * l + h):
                            act.wait_ge(S["sb_loss"], 4 * l + h)
                        z = psum[:, BANK_SC + h % 2, 0:384]
                        f(sb_log, z, ACT.Abs).then_inc(S["act_step"], q.one("act_step"))
                        act.wait_ge(S["act_step"], q.sent["act_step"])
                        f(sb_log, sb_log, ACT.Exp, scale=-1.0).then_inc(S["act_step"], q.one("act_step"))
                        act.wait_ge(S["act_step"], q.sent["act_step"])
                        f(sb_log, sb_log, ACT.Ln, bias=1.0).then_inc(S["sb_log"], 1)

                    def sb_weights(h):
                        if q.due("sb_min", 4 * l + h + 1):
                            act.wait_ge(S["sb_min"], 4 * l + h + 1)
                        f(attn_of(h), attn_of(h), ACT.Exp).then_inc(S["sb_attn"], 1)

                    def dil_turned(u):
                        if q.due("dil_turned", 8 * l + u + 1):
                            act.wait_ge(S["dil_turned"], 8 * l + u + 1)
                        n = GROUPS * (u % 2 + 1) * P
                        f(pT_of(u)[:, 0:n], flat(BANK_T, 0, n), ACT.Copy).then_inc(S["dil_pT"], 1)

                    def dil_exp(u):
                        if q.due("dil_masked", 8 * l + u + 1):
                            act.wait_ge(S["dil_masked"], 8 * l + u + 1)
                        n = GROUPS * (u % 2 + 1) * P
                        f(prob_of(u)[:, 0:n], prob_of(u)[:, 0:n], ACT.Exp, scale=-1.0,
                                 bias=dil_bias[:, u:u + 1], accum_out=dil_den[:, u:u + 1]).then_inc(S["dil_exp"], 1)

                    def take(s):
                        if s.kind == "v":
                            for j, t in enumerate(s.tiles):
                                if q.due("main_tile", t + 1):
                                    act.wait_ge(S["main_tile"], t + 1)
                                if q.due("rtok", l + 1):
                                    act.wait_ge(S["rtok"], l + 1)
                                v0 = (3 if s.index == 2 else s.index - 9) * T
                                f(tl(v_tok, j, 1024)[:, v0:v0 + T], psum[:, t % RING, 0:T], ACT.Copy,
                                  scale=rtok[:, j:j + 1]).then_inc(S["v_tile"], 1)
                        if s.kind == "rope":
                            for j, t in enumerate(s.tiles):
                                r = 2 * (s.index - 3) + j
                                if q.due("main_tile", t + 1):
                                    act.wait_ge(S["main_tile"], t + 1)
                                if q.due("q_turned", 12 * l + r - 1):
                                    act.wait_ge(S["q_turned"], 12 * l + r - 1)
                                f(tl(rope_raw, r % 2), psum[:, t % RING, 0:T], ACT.Copy).then_inc(S["q_raw"], 1)

                    if tick == 0:
                        act.preload_act_table_set(LOGEXP)
                    if 0 <= tick < 4:
                        sb_tick(tick)
                    elif tick == 4:
                        sb_weights(3)
                    elif tick > 4:
                        dil_turned(tick - 5)
                    if tick >= 4:
                        dil_exp(tick - 4)
                    if tick == 5:
                        if q.due("sb_out", 4 * (l + 1)):
                            act.wait_ge(S["sb_out"], 4 * (l + 1))
                        for i in range(2):
                            hid_high(8 + i, tl(psum[:, BANK_O, :], i))
                    if tick <= 0:
                        take(s)
                        split(s.n + SLOTS)
                        if l == 0 and s.index == 1:
                            if q.due("angle", 1):
                                act.wait_ge(S["angle"], 1)
                            f(SIN, SINR, ACT.Sin).then_inc(S["sine"], 1)
                            f(COS, SINR, ACT.Sin, scale=0.5).then_inc(S["sine"], 1)
                    elif tick >= 2:
                        take(slabs[s.index - 1])
                        split(slabs[s.index - 1].n + SLOTS)
                dil_turned(7)
                if q.due("dil_out", 8 * (l + 1)):
                    act.wait_ge(S["dil_out"], 8 * (l + 1))
                for i in range(2):
                    hid_high(10 + i, tl(psum[:, BANK_O, :], i))
                split(slabs[-1].n + SLOTS)
                for m in range(KD):
                    for i in (m, KD + m):
                        if q.due("gate_raw", 16 * (l + 1)):
                            act.wait_ge(S["gate_raw"], 16 * (l + 1))
                        f(tl(gates, i), tl(gates, i), ACT.Sigmoid, bias=col(f"b_gate{l}", i)).then_inc(S["gate"], 1)
                    if m:
                        act.wait_ge(S["mixed"], q.next("mixed"))
                        hid_high(m - 1, tl(mix32, (m - 1) % 2))
                act.wait_ge(S["mixed"], q.next("mixed"))
                hid_high(KD - 1, tl(mix32, (KD - 1) % 2))
                sa, sbr = plan.stages[(l, "proj")]
                split(sa.n + SLOTS)
                split(sbr.n + SLOTS)
                for s in plan.stages[(l, "out")]:
                    for j in range(2):
                        prep(2 * s.index + j, lambda m: col(f"norm_ffn{l}", m))
                    split_behind(s, 4)
                guess()
                for half, (f0, n) in enumerate(PARTS1):
                    for s in plan.stages[(l, "up", half)]:
                        for j in range(2):
                            i = f0 + s.index // 2 * 2 + j
                            r = i % 4
                            if s.kind == "fa":
                                act.wait_ge(S["a_tile"], q.next("a_tile"))
                                if q.due("a_silu", q.sent.get("a_silu", 0)):
                                    act.wait_ge(S["a_silu"], q.sent.get("a_silu", 0))
                                f(tl(y_conv, r), tl(AB, r, T + 2)[:, 2:], ACT.Identity,
                                         scale=col(f"conv_w{l}", 2 * FF_TILES + i), bias=col(f"conv_b{l}", i))\
                                             .then_inc(S["a_tap"], 1)
                            else:
                                act.wait_ge(S["h_tile"], q.next("h_tile"))
                                hid_high(i - f0, tl(h32, r))
                        if s.kind == "fa":
                            split(s.n + SLOTS)
                            for j in range(2):
                                r = (f0 + s.index // 2 * 2 + j) % 4
                                act.wait_ge(S["a_conv"], q.next("a_conv"))
                                if q.due("a_scaled", q.sent.get("a_silu", 0) - 3):
                                    act.wait_ge(S["a_scaled"], q.sent.get("a_silu", 0) - 3)
                                f(tl(s_silu, r), tl(y_conv, r), ACT.Silu).then_inc(S["a_silu"], q.one("a_silu"))
                        else:
                            split(s.n + SLOTS)
                    for s in plan.stages[(l, "down", half)]:
                        if s.index % 2 == 1:
                            for j in range(2):
                                m = s.index // 2 * 2 + j
                                if half < len(PARTS1) - 1:
                                    act.wait_ge(S["x_tile"], q.next("x_tile"))
                                elif l < DEPTH - 1:
                                    prep(m, lambda m: col(f"norm_mix{l + 1}", m))
                                else:
                                    prep(m, lambda m: gfg2[:, m:m + 1], lambda m: col("norm_final", m))
                        if half < len(PARTS1) - 1:
                            split(s.n + SLOTS)
                        else:
                            split_behind(s, 8)

            guess()
            guess()
            ba_v = ba.rearrange("p (b c) -> p b c", b=NB)

            def soft_log(dst, src):
                f(dst, src, ACT.Abs).then_inc(S["act_step"], q.one("act_step"))
                act.wait_ge(S["act_step"], q.sent["act_step"])
                f(dst, dst, ACT.Exp, scale=-1.0).then_inc(S["act_step"], q.one("act_step"))
                act.wait_ge(S["act_step"], q.sent["act_step"])
                return f(dst, dst, ACT.Ln, bias=1.0)

            def norm_squares(first, src):
                for c in range(4):
                    if first and q.due("d_sum", first - 4 + c + 1):
                        act.wait_ge(S["d_sum"], first - 4 + c + 1)
                    f(tl(sq, c), src(c), ACT.Square).then_inc(S["e_square"], 1)

            def row_guess():
                act.preload_act_table_set(LOGEXP)
                act.wait_ge(S["e_var"], q.next("e_var"))
                f(N_GUESS, N_VAR, ACT.Ln).then_inc(S["act_step"], q.one("act_step"))
                act.wait_ge(S["act_step"], q.sent["act_step"])
                f(N_GUESS, N_GUESS, ACT.Exp, scale=-0.5).then_inc(S["e_guess"], 1)

            def gates_of(i):
                if q.due("l_logits", i + 1):
                    act.wait_ge(S["l_logits"], i + 1)
                for n in range(2):
                    t = 2 * (i % 2) + n
                    f(tl(l_i if i // 2 else l_r, t), psum[:, BANK_O, n * T:n * T + T], ACT.Sigmoid,
                      bias=col("gate_x_b" if i // 2 else "gate_a_b", t)).then_inc(S["l_gates"], q.one("l_gates"))

            def v_token(b):
                if q.due("d_turned", b + 2):
                    act.wait_ge(S["d_turned"], b + 2)
                f(tl(v_tk, b, 512), psum[:, BANK_O, :], ACT.Copy).then_inc(S["e_vtok"], 1)

            def turned_x(lv):
                for b in range(NB):
                    if q.due("d_xt", 2 * (lv - 1) + b + 1):
                        act.wait_ge(S["d_xt"], 2 * (lv - 1) + b + 1)
                    f(tl(XT, b, 512), psum[:, pair(b)[1], :], ACT.Copy).then_inc(S["e_xt"], 1)

            for s in plan.stages[(2, "in")]:
                if s.index == 6:
                    for b in range(NB):
                        if q.due("d_x0", b + 1):
                            act.wait_ge(S["d_x0"], b + 1)
                        f(tl(XX, b, 512), psum[:, pair(b)[0], :], ACT.Copy).then_inc(S["e_x"], 1)
                if s.kind == "conv":
                    lru = s.conv >= 12
                    for j in range(2):
                        c = s.conv + j
                        act.wait_ge(S["c_tile"], q.next("c_tile"))
                        f(tl(lru_x, c - 12) if lru else tl(qkv, c), tl(cbuf, c % 4, T + 3)[:, 3:],
                          ACT.Identity, scale=col("lru_conv", 3 * LT + c - 12) if lru else col("gdn_conv", 36 + c),
                          bias=col("lru_conv_b", c - 12) if lru else zero_col).then_inc(S["c_tap"], 1)
                if s.index == 2:
                    if q.due("c_silu", 4):
                        act.wait_ge(S["c_silu"], 4)
                    norm_squares(0, lambda c: tl(qkv, 4 + c))
                    if q.due("ba_tile", 2):
                        act.wait_ge(S["ba_tile"], 2)
                    f(beta.rearrange("p (b c) -> p b c", b=NB), ba_v[:, :, 0:4], ACT.Sigmoid).then_inc(S["e_beta"], 1)
                    act.preload_act_table_set(LOGEXP)
                    if q.due("e_shift", 1):
                        act.wait_ge(S["e_shift"], 1)
                    soft_log(logs, shift).then_inc(S["e_log"], 1)
                    f(rate, par[:, PARAM_COLS["A_log"]:PARAM_COLS["A_log"] + GH], ACT.Exp).then_inc(S["e_rate"], 1)
                    soft_log(l_log, par[:, PARAM_COLS["a_param"]:PARAM_COLS["a_param"] + LT]).then_inc(S["l_log"], 1)
                if s.index == 3:
                    if q.due("d_rows", 1):
                        act.wait_ge(S["d_rows"], 1)
                    f(state, psum[:, BANK_SC + 1, :], ACT.Exp).then_inc(S["e_erow"], 1)
                    if q.due("e_cum", 1):
                        act.wait_ge(S["e_cum"], 1)
                    f(ecum, cum[:, 4:8], ACT.Exp).then_inc(S["e_ecum"], 1)
                    if q.due("e_last", 1):
                        act.wait_ge(S["e_last"], 1)
                    f(edec, edec, ACT.Exp).then_inc(S["e_edec"], 1)
                    for b in range(NB):
                        if q.due("e_diff", b + 1):
                            act.wait_ge(S["e_diff"], b + 1)
                        f(tl(MM, b, 512), tl(MM, b, 512), ACT.Exp).then_inc(S["e_exp"], 1)
                    row_guess()
                if s.index == 5:
                    row_guess()
                if s.kind == "conv":
                    if not lru:
                        for j in range(2):
                            act.wait_ge(S["c_conv"], q.next("c_conv"))
                            f(tl(qkv, s.conv + j), tl(qkv, s.conv + j), ACT.Silu).then_inc(S["c_silu"], 1)
                if s.index == 4:
                    if q.due("c_silu", 8):
                        act.wait_ge(S["c_silu"], 8)
                    norm_squares(4, lambda c: tl(qkv, c))
                if s.index == 10:
                    gates_of(1)
                    gates_of(2)
                if s.index == 11:
                    if q.due("l_gated", 1):
                        act.wait_ge(S["l_gated"], 1)
                    if q.due("lg_tile", 4):
                        act.wait_ge(S["lg_tile"], 4)
                    f(l_scan, lru_g, ACT.Square).then_inc(S["l_gsquare"], 1)
                if 7 <= s.index < 12:
                    turned_x(s.index - 6)
                if s.index == 8:
                    v_token(0)
                if s.index == 9:
                    v_token(1)
                    gates_of(0)
                if s.index == 10:
                    gates_of(3)
                    split(s.n + SLOTS)
                    if q.due("l_rate", 1):
                        act.wait_ge(S["l_rate"], 1)
                    if q.due("e_qdec", 1):
                        act.wait_ge(S["e_qdec"], 1)
                    act.wait_ge(S["l_gates"], q.sent["l_gates"])
                    for t in range(LT):
                        f(l_a[t], tl(l_r, t), ACT.Exp, scale=l_rate[:, t:t + 1]).then_inc(S["l_decay"], q.one("l_decay"))
                    for t in range(LT):
                        f(tl(l_t, t), tl(l_r, t), ACT.Tanh, scale=l_rate[:, t:t + 1]).then_inc(S["l_tanh"], q.one("l_tanh"))
                    act.wait_ge(S["l_decay"], q.sent["l_decay"])
                    act.wait_ge(S["l_tanh"], q.sent["l_tanh"])
                    for t in range(LT):
                        f(tl(l_r, t), l_a[t], ACT.Square).then_inc(S["l_square"], 1)
                if s.index == 11:
                    split(s.n + SLOTS)
                if s.index == 12:
                    if q.due("l_cubic", 1):
                        act.wait_ge(S["l_cubic"], 1)
                    f(l_scan, l_scan, ACT.Tanh, scale=GELU_C).then_inc(S["l_gelu"], 1)
                    if q.due("l_minus", 1):
                        act.wait_ge(S["l_minus"], 1)
                    f(l_t, l_t, ACT.Sqrt, scale=-1.0).then_inc(S["l_root"], 1)
                if s.index not in (10, 11):
                    split(s.n + SLOTS)
            turned_x(LEVELS - 1)
            for t in range(LT):
                if q.due("l_h", t + 1):
                    act.wait_ge(S["l_h"], t + 1)
                hid_high(GH + t, tl(l_scan, t))
            if q.due("d_new", 1):
                act.wait_ge(S["d_new"], 1)
            f(vn0, psum[:, BANK_SC, :], ACT.Copy).then_inc(S["e_new"], 1)
            for i in range(4):
                act.wait_ge(S["z_tile"], q.next("z_tile"))
                f(tl(z_t, i), tl(z_t, i), ACT.Silu).then_inc(S["z_silu"], 1)
            for s in plan.stages[(2, "out", "lru")]:
                if s.index == 0:
                    if q.due("d_state", 1):
                        act.wait_ge(S["d_state"], 1)
                    f(state, psum[:, BANK_SC + 1, :], ACT.Copy).then_inc(S["e_state"], 1)
                if s.index == 2:
                    if q.due("d_new", 2):
                        act.wait_ge(S["d_new"], 2)
                    f(vn1, psum[:, BANK_SC, :], ACT.Copy).then_inc(S["e_new"], 1)
                if s.index == 3:
                    if q.due("d_out", 1):
                        act.wait_ge(S["d_out"], 1)
                    norm_squares(8, lambda h: psum[:, BANK_T + h // 2, (h % 2) * T:(h % 2) * T + T])
                    split(s.n - 1 + SLOTS)
                    row_guess()
                if s.index != 2:
                    split(s.n + SLOTS)
            q.next("x_tile", KD)
            for h in range(GH):
                if q.due("e_h", h + 1):
                    act.wait_ge(S["e_h"], h + 1)
                hid_high(h, tl(z_t, h))
            for s in plan.stages[(2, "out", "gdn")]:
                for j in range(2):
                    prep(2 * s.index + j, lambda m: col("norm_mlp", m))
                split_behind(s, 4)
            guess()
            for half, (f0, n) in enumerate(PARTS2):
                for s in plan.stages[(2, "up", half)]:
                    for j in range(2):
                        act.wait_ge(S["r_square"], q.next("r_square"))
                        hid_high(2 * s.index + j, tl(h32, (f0 + 2 * s.index + j) % 4))
                    split(s.n + SLOTS)
                for s in plan.stages[(2, "down", half)]:
                    if s.index % 2 == 1:
                        for j in range(2):
                            m = s.index // 2 * 2 + j
                            act.wait_ge(S["x_tile"], q.next("x_tile"))
                            if half == len(PARTS2) - 1:
                                square_room(m)
                                f(tl(sq, m % 2), tl(xt, m), ACT.Square).then_inc(S["square"], 1)
                    split(s.n + SLOTS)
            guess()

        @block.vector
        def _(dve):
            q = Count()
            v = nc.vector

            def stt(out_, a, scalar, b, op0, op1):
                return v.scalar_tensor_tensor(out=out_, in0=a, scalar=scalar, in1=b, op0=op0, op1=op1)

            def split(n):
                if n >= len(plan.slabs) or plan.slabs[n].low[0] != "split_lo":
                    return
                s = plan.slabs[n]
                if q.due("split_hi", n + 1):
                    dve.wait_ge(S["split_hi"], n + 1)
                v.tensor_tensor(part(w_lo, s), part(raw, s), part(w_hi, s).bitcast(F32), ALU.subtract)\
                    .then_inc(S["split_lo"], 1)

            def x_low(m, gain):
                dve.wait_ge(S["xg_hi"], q.next("xg_hi"))
                stt(tl(xg_lo, m), tl(xt, m), gain(m), tl(xg_hi, m).bitcast(F32), ALU.mult, ALU.subtract)\
                    .then_inc(S["xg_lo"], 1)

            def x_add(m, t):
                if q.due("main_tile", t + 1):
                    dve.wait_ge(S["main_tile"], t + 1)
                v.tensor_tensor(tl(xt, m), tl(xt, m), psum[:, t % RING, 0:T], ALU.add).then_inc(S["x_tile"], 1)

            def x_stage(slabs, gain):
                for s in slabs:
                    for j, t in enumerate(s.tiles):
                        m = t - first_tile(slabs)
                        x_add(m, t)
                        if gain and m:
                            x_low(m - 1, gain)
                    if not gain:
                        split(s.n + SLOTS)
                    elif s is slabs[-1]:
                        x_low(KD - 1, gain)
                        split(s.n - 1 + SLOTS)
                        split(s.n + SLOTS)
                    elif s is not slabs[-2]:
                        split(s.n + SLOTS)

            def first_tile(slabs):
                return next(s.tiles[0] for s in slabs if s.tiles)

            def newton(var, guess_, tmp, dst, signal):
                v.tensor_tensor(tmp, guess_, guess_, ALU.mult).then_inc(S["dve_step"], q.one("dve_step"))
                dve.wait_ge(S["dve_step"], q.sent["dve_step"])
                stt(tmp, tmp, -0.5, var, ALU.mult, ALU.mult).then_inc(S["dve_step"], q.one("dve_step"))
                dve.wait_ge(S["dve_step"], q.sent["dve_step"])
                stt(dst, tmp, 1.5, guess_, ALU.add, ALU.mult).then_inc(S[signal], q.one(signal))

            def variance(n, eps):
                if q.due("stat_sum", n):
                    dve.wait_ge(S["stat_sum"], n)
                v.tensor_scalar(VAR, psum[:, BANK_T, 0:T], 1.0 / D, eps, ALU.mult, ALU.add)\
                    .then_inc(S["var"], q.one("var"))

            def norm(n, eps):
                variance(n, eps)
                dve.wait_ge(S["rs_guess"], q.next("rs_guess"))
                newton(VAR, GUESS, TMP, RSTD, "rstd")
                dve.wait_ge(S["rstd"], q.sent["rstd"])

            def take_rtok(n):
                if q.due("rtok_sum", n):
                    dve.wait_ge(S["rtok_sum"], n)
                v.tensor_copy(rtok, psum[:, BANK_T + 1, 384:384 + NB]).then_inc(S["rtok"], q.one("rtok"))
                dve.wait_ge(S["rtok"], q.sent["rtok"])

            def hid_low(i, src):
                dve.wait_ge(S["hid_hi"], q.next("hid_hi"))
                v.tensor_tensor(tl(hid_lo, i), src, tl(hid_hi, i).bitcast(F32), ALU.subtract).then_inc(S["hid_lo"], 1)

            def angles():
                if q.due("load_pos", 16):
                    dve.wait_ge(S["load_pos"], 16)
                if q.due("load_rest", 16):
                    dve.wait_ge(S["load_rest"], 16)
                v.tensor_copy(COSR, COS.bitcast(I32)).then_inc(S["dve_step"], q.one("dve_step"))
                dve.wait_ge(S["dve_step"], q.sent["dve_step"])
                v.tensor_scalar(COSR, COSR, C("inv_freq"), None, ALU.mult).then_inc(S["dve_step"], q.one("dve_step"))
                dve.wait_ge(S["dve_step"], q.sent["dve_step"])
                v.tensor_scalar(SIN, COSR, 1.0 / (2 * np.pi), ROUND, ALU.mult, ALU.add)\
                    .then_inc(S["dve_step"], q.one("dve_step"))
                dve.wait_ge(S["dve_step"], q.sent["dve_step"])
                v.tensor_scalar(SIN, SIN, ROUND, None, ALU.subtract).then_inc(S["dve_step"], q.one("dve_step"))
                dve.wait_ge(S["dve_step"], q.sent["dve_step"])
                for c in TWO_PI:
                    stt(COSR, SIN, -c, COSR, ALU.mult, ALU.add).then_inc(S["dve_step"], q.one("dve_step"))
                    dve.wait_ge(S["dve_step"], q.sent["dve_step"])
                v.tensor_scalar(SINR, COSR, PI_BELOW, -PI_BELOW, ALU.min, ALU.max).then_inc(S["angle"], 1)

            def cosine():
                if q.due("sine", 2):
                    dve.wait_ge(S["sine"], 2)
                v.tensor_tensor(COS, COS, COS, ALU.mult).then_inc(S["dve_step"], q.one("dve_step"))
                dve.wait_ge(S["dve_step"], q.sent["dve_step"])
                v.tensor_scalar(COS, COS, -2.0, 1.0, ALU.mult, ALU.add).then_inc(S["dve_step"], q.one("dve_step"))
                dve.wait_ge(S["dve_step"], q.sent["dve_step"])

            if q.due("load_params", 16):
                dve.wait_ge(S["load_params"], 16)
            for m in range(KD):
                if q.due("x_turned", m + 1):
                    dve.wait_ge(S["x_turned"], m + 1)
                v.tensor_copy(tl(xt, m), psum[:, BANK_SC + m % 4, 0:T]).then_inc(S["x_tile"], 1)
                if m:
                    x_low(m - 1, lambda m: col("norm_mix0", m))
                if m == 4:
                    split(0)
            x_low(KD - 1, lambda m: col("norm_mix0", m))
            split(1)
            v.memset(zero_col, 0.0).then_inc(S["dve_step"], q.one("dve_step"))
            v.tensor_tensor(gfg2, par[:, PARAM_COLS["norm_final"]:PARAM_COLS["norm_final"] + KD],
                            par[:, PARAM_COLS["norm_mix2"]:PARAM_COLS["norm_mix2"] + KD], ALU.mult)\
                .then_inc(S["dve_step"], q.one("dve_step"))
            stats = 2

            for l in range(DEPTH):
                def q_sin(r):
                    if q.due("q_turned", 12 * l + r + 1):
                        dve.wait_ge(S["q_turned"], 12 * l + r + 1)
                    if q.due("q_tile", 12 * l + r - 1):
                        dve.wait_ge(S["q_tile"], 12 * l + r - 1)
                    v.tensor_tensor(tl(rope_tmp, r % 2), psum[:, BANK_T + r % 2, 0:T], SINR, ALU.mult)\
                        .then_inc(S["q_sin"], 1)

                def sb_loss(h):
                    if q.due("sb_log", 4 * l + h + 1):
                        dve.wait_ge(S["sb_log"], 4 * l + h + 1)
                    loss = loss_of(h)
                    stt(loss, psum[:, BANK_SC + h % 2, 0:384], 0.0, sb_log, ALU.max, ALU.add)\
                        .then_inc(S["dve_step"], q.one("dve_step"))
                    dve.wait_ge(S["dve_step"], q.sent["dve_step"])
                    ends = loss.rearrange("p (n c) -> p n c", c=P)[:, 0:3:2, :]
                    v.tensor_tensor(ends, ends, C("lt").unsqueeze(1).to_broadcast([P, 2, P]), ALU.mult)\
                        .then_inc(S["sb_loss"], 1)

                def sb_min(h):
                    if q.due("sb_exponent", 4 * l + h + 1):
                        dve.wait_ge(S["sb_exponent"], 4 * l + h + 1)
                    stt(attn_of(h), psum[:, BANK_SC + h % 2, 0:384], 0.0, C("sb_mask"), ALU.min, ALU.add)\
                        .then_inc(S["sb_min"], 1)

                def dil_mask(u):
                    if q.due("dil_scores", 8 * l + u + 1):
                        dve.wait_ge(S["dil_scores"], 8 * l + u + 1)
                    n = GROUPS * (u % 2 + 1) * P
                    v.tensor_tensor_reduce(prob_of(u)[:, 0:n], flat(BANK_SC, 0, n), C(f"dil_mask{u % 2}"),
                                                  -HEAD ** -0.5, 3e38, ALU.add, ALU.min, dil_bias[:, u:u + 1])\
                                                      .then_inc(S["dil_masked"], 1)

                def dil_scale(u):
                    if q.due("dil_exp", 8 * l + u + 1):
                        dve.wait_ge(S["dil_exp"], 8 * l + u + 1)
                    n = GROUPS * (u % 2 + 1) * P
                    v.reciprocal(dil_rden[:, u:u + 1], dil_den[:, u:u + 1]).then_inc(S["dve_step"], q.one("dve_step"))
                    dve.wait_ge(S["dve_step"], q.sent["dve_step"])
                    v.tensor_scalar(prob_of(u)[:, 0:n], prob_of(u)[:, 0:n], dil_rden[:, u:u + 1], None, ALU.mult)\
                        .then_inc(S["dil_probs"], 1)

                norm(stats, EPS1)
                slabs = plan.stages[(l, "in")]
                for s in slabs:
                    tick = s.index - TICK0

                    def take(s):
                        for j, t in enumerate(s.tiles):
                            i = 2 * s.index + j
                            ps = psum[:, t % RING, 0:T]
                            if s.kind == "s":
                                if q.due("main_tile", t + 1):
                                    dve.wait_ge(S["main_tile"], t + 1)
                                stt(tl(s_t, i), ps, HEAD ** -0.5 if i < 2 else 1.0, RSTD, ALU.mult, ALU.mult)\
                                    .then_inc(S["s_tile"], 1)
                            if s.kind == "rope":
                                if q.due("q_raw", 12 * l + i - 5):
                                    dve.wait_ge(S["q_raw"], 12 * l + i - 5)
                                v.tensor_tensor(tl(qk, i - 6), ps, COSR, ALU.mult).then_inc(S["q_cos"], 1)
                            if s.kind == "gate":
                                if q.due("main_tile", t + 1):
                                    dve.wait_ge(S["main_tile"], t + 1)
                                v.tensor_tensor(tl(gates, i - 24), ps, RSTD, ALU.mult).then_inc(S["gate_raw"], 1)
                            if i == 4:
                                take_rtok(l + 1)
                            if 0 <= i - 8 < 10:
                                q_sin(i - 8)

                    if 1 <= tick < 5:
                        sb_min(tick - 1)
                    if tick == 1:
                        q_sin(10)
                    if tick >= 4:
                        dil_mask(tick - 4)
                    if tick == 5:
                        if q.due("hid_hi", q.taken.get("hid_hi", 0) + 2):
                            dve.wait_ge(S["hid_hi"], q.taken.get("hid_hi", 0) + 2)
                        for i in range(2):
                            hid_low(8 + i, tl(psum[:, BANK_O, :], i))
                    if tick >= 2:
                        take(slabs[s.index - 1])
                    if 0 <= tick < 4:
                        sb_loss(tick)
                    if tick >= 4:
                        dil_scale(tick - 4)
                    if tick >= 2:
                        split(slabs[s.index - 1].n + SLOTS)
                    if tick == 1:
                        q_sin(11)
                    if tick <= 0:
                        take(s)
                        if l == 0 and s.index == 1:
                            angles()
                        split(s.n + SLOTS)
                    if s.index == 2:
                        if l == 0:
                            cosine()
                        v.tensor_tensor(COSR, COS, RSTD, ALU.mult).then_inc(S["dve_step"], q.one("dve_step"))
                        v.tensor_tensor(SINR, SIN, RSTD, ALU.mult).then_inc(S["dve_step"], q.one("dve_step"))
                        dve.wait_ge(S["dve_step"], q.sent["dve_step"])
                take(slabs[-1])
                if q.due("hid_hi", q.taken["hid_hi"] + 2):
                    dve.wait_ge(S["hid_hi"], q.taken["hid_hi"] + 2)
                for i in range(2):
                    hid_low(10 + i, tl(psum[:, BANK_O, :], i))
                split(slabs[-1].n + SLOTS)
                sa, sbr = plan.stages[(l, "proj")]
                for m in range(KD):
                    if q.due("mixed", KD * l + m - 1):
                        dve.wait_ge(S["mixed"], KD * l + m - 1)
                    for s, buf, i, name in ((sa, mixA, m, "ya_gated"), (sbr, mixB, KD + m, "yb_gated")):
                        t = s.tiles[m]
                        if q.due("main_tile", t + 1):
                            dve.wait_ge(S["main_tile"], t + 1)
                        if q.due("gate", 16 * l + 2 * m + (1 if s is sa else 2)):
                            dve.wait_ge(S["gate"], 16 * l + 2 * m + (1 if s is sa else 2))
                        v.tensor_tensor(tl(buf, m % 2), psum[:, t % RING, 0:T], tl(gates, i), ALU.mult)\
                            .then_inc(S[name], q.one(name))
                    if m:
                        hid_low(m - 1, tl(mix32, (m - 1) % 2))
                hid_low(KD - 1, tl(mix32, (KD - 1) % 2))
                split(sa.n + SLOTS)
                split(sbr.n + SLOTS)
                x_stage(plan.stages[(l, "out")], lambda m: col(f"norm_ffn{l}", m))
                stats += 2
                norm(stats, EPS1)
                for r in range(4):
                    v.memset(tl(AB, r, T + 2)[:, 0:2], 0.0).then_inc(S["dve_step"], q.one("dve_step"))
                for half, (f0, n) in enumerate(PARTS1):
                    for s in plan.stages[(l, "up", half)]:
                        for j, t in enumerate(s.tiles):
                            r = (f0 + s.index // 2 * 2 + j) % 4
                            if q.due("main_tile", t + 1):
                                dve.wait_ge(S["main_tile"], t + 1)
                            ps = psum[:, t % RING, 0:T]
                            if s.kind == "fa":
                                v.tensor_tensor(tl(AB, r, T + 2)[:, 2:], ps, RSTD, ALU.mult).then_inc(S["a_tile"], 1)
                            else:
                                dve.wait_ge(S["a_scaled"], q.next("a_scaled"))
                                v.tensor_tensor(tl(h32, r), ps, tl(s_scaled, r), ALU.mult).then_inc(S["h_tile"], 1)
                        for j in range(2):
                            i = f0 + s.index // 2 * 2 + j
                            r = i % 4
                            if s.kind == "fa":
                                dve.wait_ge(S["a_tap"], q.next("a_tap"))
                                dve.wait_ge(S["dve_step"], q.sent["dve_step"])
                                for tap in (1, 0):
                                    ins = stt(tl(y_conv, r), tl(AB, r, T + 2)[:, tap:tap + T],
                                              col(f"conv_w{l}", tap * FF_TILES + i), tl(y_conv, r), ALU.mult, ALU.add)
                                    if tap:
                                        ins.then_inc(S["dve_step"], q.one("dve_step"))
                                        dve.wait_ge(S["dve_step"], q.sent["dve_step"])
                                    else:
                                        ins.then_inc(S["a_conv"], 1)
                            else:
                                hid_low(i - f0, tl(h32, r))
                        split(s.n + SLOTS)
                    last = half == len(PARTS1) - 1
                    gain = None
                    if last:
                        gain = (lambda m: col(f"norm_mix{l + 1}", m)) if l < DEPTH - 1 else (lambda m: gfg2[:, m:m + 1])
                    x_stage(plan.stages[(l, "down", half)], gain)
                stats += 4 if l == DEPTH - 1 else 2

            variance(stats, EPS1)
            dve.wait_ge(S["rs_guess"], q.next("rs_guess"))
            newton(VAR, GUESS, TMP, RSTD, "dve_step")
            dve.wait_ge(S["dve_step"], q.sent["dve_step"])
            v.tensor_tensor(TMP, RSTD, RSTD, ALU.mult).then_inc(S["dve_step"], q.one("dve_step"))
            dve.wait_ge(S["dve_step"], q.sent["dve_step"])
            stt(TMP, psum[:, BANK_T + 1, 0:T], 1.0 / D, TMP, ALU.mult, ALU.mult)\
                .then_inc(S["dve_step"], q.one("dve_step"))
            dve.wait_ge(S["dve_step"], q.sent["dve_step"])
            v.tensor_scalar(VAR, TMP, EPS2, None, ALU.add).then_inc(S["var"], q.one("var"))
            v.tensor_copy(RSTD2, RSTD).then_inc(S["dve_step"], q.one("dve_step"))
            dve.wait_ge(S["var"], q.sent["var"])
            dve.wait_ge(S["rs_guess"], q.next("rs_guess"))
            newton(VAR, GUESS, TMP, TMP2, "dve_step")
            dve.wait_ge(S["dve_step"], q.sent["dve_step"])
            v.tensor_tensor(RSTD, RSTD2, TMP2, ALU.mult).then_inc(S["rstd"], q.one("rstd"))
            dve.wait_ge(S["rstd"], q.sent["rstd"])
            for r in range(4):
                v.memset(tl(cbuf, r, T + 3)[:, 0:3], 0.0).then_inc(S["dve_step"], q.one("dve_step"))
            ba_v = ba.rearrange("p (b c) -> p b c", b=NB)

            def take(s, j):
                t = s.tiles[j]
                if q.due("main_tile", t + 1):
                    dve.wait_ge(S["main_tile"], t + 1)
                ps = psum[:, t % RING, 0:T]
                if s.kind == "conv":
                    v.tensor_tensor(tl(cbuf, (s.conv + j) % 4, T + 3)[:, 3:], ps, RSTD, ALU.mult).then_inc(S["c_tile"], 1)
                if s.kind == "ba":
                    v.tensor_scalar(tl(ba, j, 8), ps[:, 0:8], rtok[:, j:j + 1], None, ALU.mult)\
                        .then_inc(S["ba_tile"], q.one("ba_tile"))
                if s.kind == "z":
                    v.tensor_tensor(tl(z_t, 2 * (s.index - 11) + j), ps, RSTD, ALU.mult).then_inc(S["z_tile"], 1)
                if s.kind == "lg":
                    v.tensor_tensor(tl(lru_g, 2 * (s.index - 9) + j), ps, RSTD, ALU.mult)\
                        .then_inc(S["lg_tile"], q.one("lg_tile"))

            def convolve(s):
                for j in range(2):
                    c = s.conv + j
                    lru = c >= 12
                    dst = tl(lru_x, c - 12) if lru else tl(qkv, c)
                    dve.wait_ge(S["c_tap"], q.next("c_tap"))
                    dve.wait_ge(S["dve_step"], q.sent["dve_step"])
                    for tap in (2, 1, 0):
                        g = col("lru_conv", tap * LT + c - 12) if lru else col("gdn_conv", tap * 12 + c)
                        ins = stt(dst, tl(cbuf, c % 4, T + 3)[:, tap:tap + T], g, dst, ALU.mult, ALU.add)
                        if tap:
                            ins.then_inc(S["dve_step"], q.one("dve_step"))
                            dve.wait_ge(S["dve_step"], q.sent["dve_step"])
                        else:
                            ins.then_inc(S["c_conv"], q.one("c_conv"))

            def row_var(mean, count):
                if q.due("d_sum", count):
                    dve.wait_ge(S["d_sum"], count)
                v.tensor_scalar(N_VAR, psum[0:8, BANK_O, 0:T], mean, EPS2, ALU.mult, ALU.add).then_inc(S["e_var"], 1)

            def row_rs(scale):
                dve.wait_ge(S["e_guess"], q.next("e_guess"))
                newton(N_VAR, N_GUESS, N_TMP, N_RS, "dve_step")
                dve.wait_ge(S["dve_step"], q.sent["dve_step"])
                v.tensor_scalar(N_RS, N_RS, scale, None, ALU.mult).then_inc(S["e_rs"], 1)

            def log_decay():
                if q.due("e_log", 1):
                    dve.wait_ge(S["e_log"], 1)
                stt(decay, shift, 0.0, logs, ALU.max, ALU.add).then_inc(S["dve_step"], q.one("dve_step"))
                dve.wait_ge(S["dve_step"], q.sent["dve_step"])
                if q.due("e_rate", 1):
                    dve.wait_ge(S["e_rate"], 1)
                stt(decay.rearrange("p (b c) -> p b c", b=NB), decay.rearrange("p (b c) -> p b c", b=NB), -1.0,
                    rate.unsqueeze(1).to_broadcast([P, NB, GH]), ALU.mult, ALU.mult).then_inc(S["e_decay"], 1)

            def unit_rate():
                if q.due("l_log", 1):
                    dve.wait_ge(S["l_log"], 1)
                ap = par[:, PARAM_COLS["a_param"]:PARAM_COLS["a_param"] + LT]
                v.tensor_scalar(l_rate, ap, -1.0, 0.0, ALU.mult, ALU.max).then_inc(S["dve_step"], q.one("dve_step"))
                dve.wait_ge(S["dve_step"], q.sent["dve_step"])
                v.tensor_tensor(l_rate, l_rate, l_log, ALU.add).then_inc(S["dve_step"], q.one("dve_step"))
                dve.wait_ge(S["dve_step"], q.sent["dve_step"])
                v.tensor_scalar(l_rate, l_rate, -LRU_C, None, ALU.mult).then_inc(S["l_rate"], 1)

            def differences():
                if q.due("d_cum", 1):
                    dve.wait_ge(S["d_cum"], 1)
                v.tensor_copy(cum, psum[:, BANK_O, 0:8]).then_inc(S["e_cum"], q.one("e_cum"))
                dve.wait_ge(S["e_cum"], q.sent["e_cum"])
                if q.due("d_rows", 1):
                    dve.wait_ge(S["d_rows"], 1)
                v.tensor_tensor(edec.unsqueeze(2), heads(psum[:, BANK_SC, :])[:, :, P - 1:P], cum[:, 0:4].unsqueeze(2),
                                ALU.subtract).then_inc(S["e_last"], 1)
                if q.due("e_erow", 1):
                    dve.wait_ge(S["e_erow"], 1)
                for b in range(NB):
                    for h in range(GH):
                        ins = v.tensor_scalar(mat(MM, b, h), psum[:, BANK_SC + b, h * P:h * P + P],
                                              cum[:, 4 * b + h:4 * b + h + 1], 0.0, ALU.subtract, ALU.min)
                    ins.then_inc(S["e_diff"], 1)

            def times_beta():
                for b in range(NB):
                    if q.due("e_masked", b + 1):
                        dve.wait_ge(S["e_masked"], b + 1)
                    v.tensor_tensor(tl(AT, b, 512), tl(AT, b, 512), psum[:, BANK_T + b, :], ALU.mult)\
                        .then_inc(S["e_masks"], q.one("e_masks"))

            def scale_qk(i, bank, count):
                if q.due("d_spread", count):
                    dve.wait_ge(S["d_spread"], count)
                v.tensor_tensor(tl(qkv, i, 512), tl(qkv, i, 512), psum[:, bank, :], ALU.mult)\
                    .then_inc(S["e_qk"], q.one("e_qk"))

            def matrix_a():
                for b in range(NB):
                    if q.due("d_kk", b + 1):
                        dve.wait_ge(S["d_kk"], b + 1)
                    dve.wait_ge(S["e_masks"], q.sent["e_masks"])
                    v.tensor_tensor(tl(AT, b, 512), tl(AT, b, 512), psum[:, pair(b)[0], :], ALU.mult)\
                        .then_inc(S["e_at"], q.one("e_at"))
                    dve.wait_ge(S["e_at"], q.sent["e_at"])
                    v.tensor_tensor(heads(tl(XT, b, 512)), heads(tl(AT, b, 512)), over_heads(C("neg_level0")), ALU.mult)\
                        .then_inc(S["dve_step"], q.one("dve_step"))
                    dve.wait_ge(S["dve_step"], q.sent["dve_step"])
                    v.tensor_tensor(heads(tl(XT, b, 512)), heads(tl(XT, b, 512)), over_heads(C("ident")), ALU.add)\
                        .then_inc(S["e_xt0"], 1)

            def decayed_k():
                if q.due("d_turned", 1):
                    dve.wait_ge(S["d_turned"], 1)
                if q.due("e_edec", 1):
                    dve.wait_ge(S["e_edec"], 1)
                for h in range(GH):
                    ins = v.tensor_scalar(tl(k_dec, h, P), psum[:, BANK_O, h * P:h * P + P], edec[:, h:h + 1], None,
                                          ALU.mult)
                ins.then_inc(S["e_kdec"], 1)

            def level_mask(lv):
                for b in range(NB):
                    dve.wait_ge(S["d_ax"], q.next("d_ax"))
                    v.tensor_tensor(heads(kept(b), HALF), heads(psum[:, pair(b)[0], 0:T], HALF),
                                    C(f"neg_level{lv}").unsqueeze(1).to_broadcast([P, GH, HALF]), ALU.mult)\
                        .then_inc(S["e_mm"], 1)

            def level_add(lv):
                for b in range(NB):
                    dve.wait_ge(S["d_x"], q.next("d_x"))
                    x = even(tl(XX, b, 512), lv)
                    v.tensor_tensor(x, x, blocks(psum[:, pair(b)[1], 0:T], lv), ALU.add).then_inc(S["e_x"], 1)

            def attend(b):
                if q.due("d_kk", NB + b + 1):
                    dve.wait_ge(S["d_kk"], NB + b + 1)
                v.tensor_tensor(tl(attn, b, 512), tl(attn, b, 512), psum[:, BANK_O, :], ALU.mult)\
                    .then_inc(S["e_at"], q.one("e_at"))

            def values_in():
                if q.due("e_vtok", 2):
                    dve.wait_ge(S["e_vtok"], 2)
                for h in range(GH):
                    ins = v.tensor_scalar(tl(r_tok, h, P), tl(v_tk, h, P), beta[:, h:h + 1], None, ALU.mult)
                ins.then_inc(S["e_r"], 1)
                dve.wait_ge(S["e_qk"], q.sent["e_qk"])
                v.tensor_tensor(heads(q_dec), heads(qkv[:, 0:4 * T], T)[:, :, P:T], heads(state), ALU.mult)\
                    .then_inc(S["e_qdec"], 1)

            def gelu_cubic():
                if q.due("l_gsquare", 1):
                    dve.wait_ge(S["l_gsquare"], 1)
                v.tensor_scalar(l_scan, l_scan, 0.044715, 1.0, ALU.mult, ALU.add)\
                    .then_inc(S["dve_step"], q.one("dve_step"))
                dve.wait_ge(S["dve_step"], q.sent["dve_step"])
                v.tensor_tensor(l_scan, l_scan, lru_g, ALU.mult).then_inc(S["l_cubic"], 1)

            def one_minus():
                if q.due("l_square", LT):
                    dve.wait_ge(S["l_square"], LT)
                stt(l_t, l_r, 1.0, l_t, ALU.add, ALU.mult).then_inc(S["l_minus"], 1)

            def unit_out():
                if q.due("l_gelu", 1):
                    dve.wait_ge(S["l_gelu"], 1)
                stt(l_scan, l_scan, 1.0, lru_g, ALU.add, ALU.mult).then_inc(S["dve_step"], q.one("dve_step"))
                if q.due("l_gated", 1):
                    dve.wait_ge(S["l_gated"], 1)
                if q.due("l_root", 1):
                    dve.wait_ge(S["l_root"], 1)
                v.tensor_tensor(l_i, l_i, l_t, ALU.mult).then_inc(S["dve_step"], q.one("dve_step"))
                dve.wait_ge(S["dve_step"], q.sent["dve_step"])
                for t in range(LT):
                    v.tensor_tensor_scan(tl(l_r, t), l_a[t], tl(l_i, t), 0.0, ALU.mult, ALU.add)\
                        .then_inc(S["dve_step"], q.one("dve_step"))
                dve.wait_ge(S["dve_step"], q.sent["dve_step"])
                for t in range(LT):
                    stt(tl(l_scan, t), tl(l_scan, t), 0.5, tl(l_r, t), ALU.mult, ALU.mult).then_inc(S["l_h"], q.one("l_h"))

            for s in plan.stages[(2, "in")]:
                n = s.index
                take(s, 0)
                if 7 <= n < 13:
                    level_add(n - 6)
                if n == 7:
                    scale_qk(1, BANK_O, 3)
                if n == 8:
                    attend(1)
                if n == 11:
                    one_minus()
                    gelu_cubic()
                if n == 12:
                    unit_out()
                take(s, 1)
                if n == 12:
                    dve.wait_ge(S["l_h"], q.sent["l_h"])
                    for t in range(LT):
                        hid_low(GH + t, tl(l_scan, t))
                if n == 1:
                    take_rtok(DEPTH + 1)
                if n == 2:
                    dt = par[:, PARAM_COLS["dt_bias"]:PARAM_COLS["dt_bias"] + GH]
                    dve.wait_ge(S["ba_tile"], q.sent["ba_tile"])
                    v.tensor_tensor(shift.rearrange("p (b c) -> p b c", b=NB), ba_v[:, :, 4:8],
                                    dt.unsqueeze(1).to_broadcast([P, NB, GH]), ALU.add).then_inc(S["e_shift"], q.one("e_shift"))
                    dve.wait_ge(S["e_shift"], q.sent["e_shift"])
                    log_decay()
                if n == 3:
                    differences()
                    row_var(1.0, 4)
                if n == 4:
                    times_beta()
                if n == 5:
                    decayed_k()
                    matrix_a()
                    row_var(1.0, 8)
                if n == 6:
                    level_mask(1)
                    scale_qk(0, BANK_O, 2)
                if 7 <= n < 12:
                    level_mask(n - 5)
                if n == 7:
                    attend(0)
                if n == 9:
                    values_in()
                    unit_rate()
                if s.kind == "conv":
                    convolve(s)
                if n == 3:
                    row_rs(1.0)
                if n == 5:
                    row_rs(P ** -0.5)
                if 7 <= n < 11:
                    for m in (2 * n - 14, 2 * n - 13):
                        stt(tl(xt, m), tl(xt, m), col("norm_final", m), RSTD2, ALU.mult, ALU.mult)\
                            .then_inc(S["dve_step"], q.one("dve_step"))
                if n == 4:
                    scale_qk(2, BANK_SC, 1)
                    scale_qk(3, BANK_SC + 1, 1)
                split(s.n + SLOTS)
            slabs = plan.stages[(2, "out", "lru")]
            for s in slabs:
                n = s.index
                if n < 3:
                    x_add(2 * n, s.tiles[0])
                else:
                    if q.due("z_silu", 4):
                        dve.wait_ge(S["z_silu"], 4)
                    if q.due("e_square", 8 + GH):
                        dve.wait_ge(S["e_square"], 8 + GH)
                    row_var(1.0 / P, 8 + GH)
                    for h in range(GH):
                        if h == 2:
                            row_rs(1.0)
                            x_add(2 * n, s.tiles[0])
                        stt(tl(z_t, h), psum[:, BANK_T + h // 2, (h % 2) * T:(h % 2) * T + T], col("gdn_norm"), tl(z_t, h),
                            ALU.mult, ALU.mult).then_inc(S["e_og"], q.one("e_og"))
                x_add(2 * n + 1, s.tiles[1])
                if n == 0:
                    if q.due("e_ecum", 1):
                        dve.wait_ge(S["e_ecum"], 1)
                    v.tensor_scalar(ecum, ecum, -1.0, None, ALU.mult).then_inc(S["dve_step"], q.one("dve_step"))
                    dve.wait_ge(S["dve_step"], q.sent["dve_step"])
                    if q.due("d_pred", 1):
                        dve.wait_ge(S["d_pred"], 1)
                    for h in range(GH):
                        ins = stt(tl(r_tok, h, P), psum[:, BANK_T, h * P:h * P + P], ecum[:, h:h + 1],
                                  tl(v_tk, GH + h, P), ALU.mult, ALU.add)
                    ins.then_inc(S["dve_step"], q.one("dve_step"))
                    dve.wait_ge(S["dve_step"], q.sent["dve_step"])
                    for h in range(GH):
                        ins = v.tensor_scalar(tl(r_tok, h, P), tl(r_tok, h, P), beta[:, 4 + h:5 + h], None, ALU.mult)
                    ins.then_inc(S["e_r"], 1)
                split(s.n + SLOTS)
            if q.due("d_spread", 4):
                dve.wait_ge(S["d_spread"], 4)
            dve.wait_ge(S["e_og"], q.sent["e_og"])
            for h in range(GH):
                v.tensor_tensor(tl(z_t, h), tl(z_t, h), psum[:, BANK_SC + h // 2, (h % 2) * T:(h % 2) * T + T],
                                ALU.mult).then_inc(S["e_h"], q.one("e_h"))
            dve.wait_ge(S["e_h"], q.sent["e_h"])
            for h in range(GH):
                hid_low(h, tl(z_t, h))
            x_stage(plan.stages[(2, "out", "gdn")], lambda m: col("norm_mlp", m))
            stats += 2
            norm(stats, EPS2)
            for half, (f0, n) in enumerate(PARTS2):
                for s in plan.stages[(2, "up", half)]:
                    for j, t in enumerate(s.tiles):
                        i = f0 + 2 * s.index + j
                        if q.due("main_tile", t + 1):
                            dve.wait_ge(S["main_tile"], t + 1)
                        if q.due("r_square", i - 3):
                            dve.wait_ge(S["r_square"], i - 3)
                        stt(tl(y_conv, i % 4), psum[:, t % RING, 0:T], 0.0, RSTD, ALU.max, ALU.mult)\
                            .then_inc(S["r_tile"], 1)
                    for j in range(2):
                        i = 2 * s.index + j
                        hid_low(i, tl(h32, (f0 + i) % 4))
                    split(s.n + SLOTS)
                x_stage(plan.stages[(2, "down", half)], None)
            stats += 2
            norm(stats, EPS2)
            take_rtok(DEPTH + 2)
            if q.due("load_rows", 16):
                dve.wait_ge(S["load_rows"], 16)
            for n, (b, half) in enumerate(Y_ORDER):
                if q.due("y_turned", n + 1):
                    dve.wait_ge(S["y_turned"], n + 1)
                stt(tl(y_out, n, 512), psum[:, Y_BANKS[n], :], rtok[:, b:b + 1], tl(gain_rows, half, 512),
                           ALU.mult, ALU.mult).then_inc(S["y_tile"], 1)

        @block.gpsimd
        def _(pool):
            q = Count()
            g = nc.gpsimd

            def split(stage, first=0, end=None):
                for s in plan.stages[stage][first:end]:
                    if s.low[0] == "pool_lo":
                        if q.due("split_hi", s.n + 1):
                            pool.wait_ge(S["split_hi"], s.n + 1)
                        g.tensor_tensor(part(w_lo, s), part(raw, s), part(w_hi, s).bitcast(F32), ALU.subtract)\
                            .then_inc(S["pool_lo"], 1)

            def add_squares(kinds=1):
                before, sums = q.taken.get("square", 0), q.taken.get("stat_sum", 0)
                q.next("square", KD * kinds)
                q.next("stat_sum", 2 * kinds)
                if q.due("stat_sum", sums):
                    pool.wait_ge(S["stat_sum"], sums)
                for m in range(1, KD - 1):
                    for n in range(kinds):
                        pool.wait_ge(S["square"], before + kinds * m + n + 1)
                        if m > 1:
                            pool.wait_ge(S["sq_added"], q.sent["sq_added"] - kinds + 1)
                        g.tensor_tensor(SUMS[n], tl(sq, 2 * n) if m == 1 else SUMS[n], tl(sq, 2 * n + m % 2), ALU.add)\
                            .then_inc(S["sq_added"], q.one("sq_added"))

            add_squares()
            for l in range(DEPTH):
                split((l, "in"), 0, 3)
                for r in range(12):
                    pool.wait_ge(S["q_sin"], q.next("q_sin"))
                    if q.due("q_cos", 12 * l + r + 1):
                        pool.wait_ge(S["q_cos"], 12 * l + r + 1)
                    g.tensor_tensor(tl(qk, r), tl(qk, r), tl(rope_tmp, r % 2), ALU.add).then_inc(S["q_tile"], 1)
                split((l, "in"), 3)
                split((l, "proj"))
                for m in range(KD):
                    pool.wait_ge(S["yb_gated"], q.next("yb_gated"))
                    if q.due("hid_lo", MIX_BASE[l] + m - 1):
                        pool.wait_ge(S["hid_lo"], MIX_BASE[l] + m - 1)
                    g.tensor_tensor(tl(mix32, m % 2), tl(mixA, m % 2), tl(mixB, m % 2), ALU.add)\
                        .then_inc(S["mixed"], 1)
                split((l, "out"))
                add_squares()
                split((l, "up", 0))
                for i in range(FF_TILES):
                    pool.wait_ge(S["a_silu"], q.next("a_silu"))
                    if q.due("h_tile", FF_TILES * l + i - 3):
                        pool.wait_ge(S["h_tile"], FF_TILES * l + i - 3)
                    if q.due("rstd", 2 * l + 2):
                        pool.wait_ge(S["rstd"], 2 * l + 2)
                    g.tensor_tensor(tl(s_scaled, i % 4), tl(s_silu, i % 4), RSTD, ALU.mult).then_inc(S["a_scaled"], 1)
                add_squares(2 if l == DEPTH - 1 else 1)
            split((2, "in"), 0, 6)
            for b in range(NB):
                if q.due("e_exp", b + 1):
                    pool.wait_ge(S["e_exp"], b + 1)
                g.tensor_tensor(heads(tl(attn, b, 512)), heads(tl(MM, b, 512)), over_heads(C("le")), ALU.mult)\
                    .then_inc(S["pool_step"], q.one("pool_step"))
                pool.wait_ge(S["pool_step"], q.sent["pool_step"])
                g.tensor_tensor(heads(tl(AT, b, 512)), heads(tl(attn, b, 512)), over_heads(C("lt")), ALU.mult)\
                    .then_inc(S["e_masked"], 1)
            split((2, "in"), 6)
            if q.due("l_gates", 2 * LT):
                pool.wait_ge(S["l_gates"], 2 * LT)
            if q.due("c_conv", 16):
                pool.wait_ge(S["c_conv"], 16)
            g.tensor_tensor(l_i, l_i, lru_x, ALU.mult).then_inc(S["l_gated"], 1)
            add_squares()
            split((2, "up", 0))
            for i in range(FF2_TILES):
                pool.wait_ge(S["r_tile"], q.next("r_tile"))
                if q.due("hid_lo", LO_BEFORE_MLP + i - 3):
                    pool.wait_ge(S["hid_lo"], LO_BEFORE_MLP + i - 3)
                g.tensor_tensor(tl(h32, i % 4), tl(y_conv, i % 4), tl(y_conv, i % 4), ALU.mult)\
                    .then_inc(S["r_square"], 1)
            add_squares()


VECTORS = ("norm_mix", "b_gate", "norm_ffn", "conv_w", "conv_b", "norm_final", "norm_mix_w_2", "gdn_conv_w_2",
           "gdn_A_log_2", "gdn_dt_bias_2", "gdn_norm_w_2", "lru_conv_w_2", "lru_conv_b_2", "lru_gate_a_b_2",
           "lru_gate_x_b_2", "lru_a_param_2", "norm_mlp_w_2")
DIRECT = ("x", "positions", "w_in", "w_proj_a", "w_proj_b", "w_out", "w_up", "w_down", "w_in_2", "w_out_2", "w_ff1_2",
          "w_ff2_2", "final_norm_w_2")


def kernel(**inputs):
    import concourse.bacc as bacc
    from concourse.bass_utils import run_bass_kernel_spmd

    nc = bacc.Bacc("TRN2", target_bir_lowering=False, num_devices=1)
    a = {n: np.ascontiguousarray(v) for n, v in inputs.items()}
    packed = {"consts": CONSTS, "params": params(a), "lru_blocks": lru_blocks(a)}
    arrays, aps = {}, {}
    for name in (*DIRECT, *packed):
        v = np.ascontiguousarray(packed[name] if name in packed else a[name])
        arrays[f"in_{name}"] = v
        aps[name] = nc.dram_tensor(f"in_{name}", v.shape, mybir.dt.from_np(v.dtype), kind="ExternalInput").ap()
    out = nc.dram_tensor("out", (1, T, D), F32, kind="ExternalOutput").ap()
    build(nc, aps, aps["consts"], aps["params"], aps["lru_blocks"], out)
    r = run_bass_kernel_spmd(nc, [arrays], core_ids=[0])
    return r.results[0]["out"]
```
